# Optimizing a Trainium2 kernel written in Bass

```python
import math
import jax
import jax.numpy as jnp
from jax import lax
import numpy as np

D_MODEL = 1024
BATCH = 1
SEQ = 512
DEPTH = 1
DEC_BATCH = 8
DEC_SEQ = 16
PAST_LEN = 256

CHUNK = 64
Q_BLOCK = 128
N_HEADS = 8
QK_HEAD_DIM = 64
V_HEAD_DIM = 2 * QK_HEAD_DIM
ATTN_WIDTH = N_HEADS * V_HEAD_DIM
D_RNN = 1024
N_RNN_BLOCKS = 8
RNN_BLOCK = D_RNN // N_RNN_BLOCKS
CONV_WIDTH = 4
RG_C = 8.0
N_GROUPS = 4
EXPERTS_PER_GROUP = 4
N_EXPERTS = N_GROUPS * EXPERTS_PER_GROUP
TOP_K_IN_GROUP = 2
D_EXPERT = 512
N_BRANCHES = 2
EPS = 1e-6

Q_COLS = N_HEADS * 2 * QK_HEAD_DIM
K_COLS = N_HEADS * 2 * QK_HEAD_DIM
V_COLS = ATTN_WIDTH
IN_WIDTH = Q_COLS + K_COLS + V_COLS + 2 * D_RNN + N_BRANCHES * D_MODEL

kernel_name = 'hybrid_diffattn_rglru_hmoe_stream_step'

def _lambda_init(layer):
    return 0.8 - 0.6 * math.exp(-0.3 * layer)

def _rmsnorm(x, g):
    xf = x.astype(jnp.float32)
    y = xf * lax.rsqrt(jnp.mean(xf * xf, axis=-1, keepdims=True) + EPS)
    return (y * g.astype(jnp.float32)).astype(x.dtype)

def _diff_scores(qb, k, v, lam, mask):
    scale = QK_HEAD_DIM ** -0.5
    s = jnp.einsum('bqhmd,bkhmd->bmhqk', qb, k).astype(jnp.float32) * scale
    if mask is not None:
        s = jnp.where(mask, s, jnp.finfo(jnp.float32).min)
    p = jax.nn.softmax(s, axis=-1)
    w = p[:, 0] - lam * p[:, 1]
    return jnp.einsum('bhqk,bkhd->bqhd', w, v.astype(jnp.float32))

def _diff_attn_prompt(q, k, v, lam):
    b, s = q.shape[0], q.shape[1]
    n_blocks = s // Q_BLOCK
    k_chunk = jnp.arange(s) // CHUNK

    def one_block(i):
        start = i * Q_BLOCK
        qb = lax.dynamic_slice_in_dim(q, start, Q_BLOCK, axis=1)
        q_chunk = (start + jnp.arange(Q_BLOCK)) // CHUNK
        mask = k_chunk[None, :] <= q_chunk[:, None]
        return _diff_scores(qb, k, v, lam, mask)

    o = lax.map(one_block, jnp.arange(n_blocks))
    return jnp.moveaxis(o, 0, 1).reshape(b, s, N_HEADS, V_HEAD_DIM)

def _lin_combine(left, right):
    a_l, b_l = left
    a_r, b_r = right
    return a_l * a_r, a_r * b_l + b_r

def _rglru_branch(xr, gate_in, conv_state, h0, conv_w, conv_b, w_ra, b_ra, w_ri, b_ri, rg_lambda):
    t = xr.shape[1]
    xpad = jnp.concatenate([conv_state.astype(xr.dtype), xr], axis=1)
    xc = conv_b
    for j in range(CONV_WIDTH):
        xc = xc + xpad[:, j:j + t] * conv_w[j]
    new_conv = xpad[:, -(CONV_WIDTH - 1):]
    f32 = jnp.float32
    xf = xc.astype(f32)
    xb = xf.reshape(xf.shape[:2] + (N_RNN_BLOCKS, RNN_BLOCK))
    r = jax.nn.sigmoid(jnp.einsum('btni,nij->btnj', xb, w_ra.astype(f32)).reshape(xf.shape) + b_ra.astype(f32))
    i = jax.nn.sigmoid(jnp.einsum('btni,nij->btnj', xb, w_ri.astype(f32)).reshape(xf.shape) + b_ri.astype(f32))
    log_a = -RG_C * r * jax.nn.softplus(-rg_lambda.astype(f32))
    a = jnp.exp(log_a)
    mult = jnp.sqrt(-jnp.expm1(2.0 * log_a))
    bvec = mult * (i * xf)
    bvec = bvec.at[:, 0].add(a[:, 0] * h0.astype(f32))
    _, h = lax.associative_scan(_lin_combine, (a, bvec), axis=1)
    y = h * jax.nn.gelu(gate_in.astype(f32))
    return y.astype(xr.dtype), new_conv, h[:, -1].astype(xr.dtype)

def _token_mixer(xn, lp, layer, past):
    b, t, _ = xn.shape
    f32 = jnp.float32
    proj = xn @ lp['w_in']
    o1 = Q_COLS
    o2 = o1 + K_COLS
    o3 = o2 + V_COLS
    o4 = o3 + D_RNN
    o5 = o4 + D_RNN
    q = proj[..., :o1].reshape(b, t, N_HEADS, 2, QK_HEAD_DIM)
    k = proj[..., o1:o2].reshape(b, t, N_HEADS, 2, QK_HEAD_DIM)
    v = proj[..., o2:o3].reshape(b, t, N_HEADS, V_HEAD_DIM)
    xr = proj[..., o3:o4]
    gr = proj[..., o4:o5]
    gates = proj[..., o5:]
    lam_init = _lambda_init(layer)
    lam = (jnp.exp(jnp.sum(lp['lambda_q1'].astype(f32) * lp['lambda_k1'].astype(f32)))
           - jnp.exp(jnp.sum(lp['lambda_q2'].astype(f32) * lp['lambda_k2'].astype(f32))) + lam_init)
    if past is None:
        attn = _diff_attn_prompt(q, k, v, lam)
        conv_state = jnp.zeros((b, CONV_WIDTH - 1, D_RNN), xn.dtype)
        h0 = jnp.zeros((b, D_RNN), xn.dtype)
    else:
        cache_k, cache_v, conv_state, h0 = past
        k_all = jnp.concatenate([cache_k.astype(k.dtype), k], axis=1)
        v_all = jnp.concatenate([cache_v.astype(v.dtype), v], axis=1)
        attn = _diff_scores(q, k_all, v_all, lam, None)
    attn = _rmsnorm(attn, lp['subln_g']) * (1.0 - lam_init)
    attn = attn.astype(xn.dtype).reshape(b, t, ATTN_WIDTH)
    y_rnn, new_conv, h_last = _rglru_branch(xr, gr, conv_state, h0, lp['conv_w'], lp['conv_b'],
                                            lp['w_rg_a'], lp['b_rg_a'], lp['w_rg_i'], lp['b_rg_i'],
                                            lp['rg_lambda'])
    g = jax.nn.sigmoid(gates.astype(f32) + lp['b_gate'].astype(f32))
    g_a = g[..., :D_MODEL]
    g_r = g[..., D_MODEL:]
    merged = g_a * (attn @ lp['w_attn_proj']).astype(f32) + g_r * (y_rnn @ lp['w_rnn_proj']).astype(f32)
    out = merged.astype(xn.dtype) @ lp['w_out']
    return out, (k, v, new_conv, h_last)

def _hier_moe(xn, lp):
    f32 = jnp.float32
    shp = xn.shape
    xt = xn.reshape(-1, D_MODEL)
    n = xt.shape[0]
    g_logits = (xt @ lp['w_group'] + lp['b_group']).astype(f32)
    g_prob = jax.nn.softmax(g_logits, axis=-1)
    g_sel = jnp.argmax(g_logits, axis=-1)
    g_w = jnp.take_along_axis(g_prob, g_sel[:, None], axis=-1)
    e_logits = (xt @ lp['w_router'] + lp['b_router']).astype(f32).reshape(n, N_GROUPS, EXPERTS_PER_GROUP)
    e_in = jnp.take_along_axis(e_logits, g_sel[:, None, None], axis=1)[:, 0]
    top_v, top_i = lax.top_k(e_in, TOP_K_IN_GROUP)
    w_sel = jax.nn.softmax(top_v, axis=-1) * g_w
    e_ids = g_sel[:, None] * EXPERTS_PER_GROUP + top_i
    combine = jnp.sum(jax.nn.one_hot(e_ids, N_EXPERTS, dtype=f32) * w_sel[..., None], axis=1)
    y = jnp.zeros((n, D_MODEL), f32)
    for e in range(N_EXPERTS):
        h = jax.nn.silu(xt @ lp['w1'][e]) * (xt @ lp['w3'][e])
        y = y + combine[:, e:e + 1] * (h @ lp['w2'][e]).astype(f32)
    return y.astype(xn.dtype).reshape(shp)

def _layer(x, lp, layer, past):
    mix, new_state = _token_mixer(_rmsnorm(x, lp['norm1_g']), lp, layer, past)
    x = x + mix
    x = x + _hier_moe(_rmsnorm(x, lp['norm2_g']), lp)
    return x, new_state

def setup_inputs(seed: int = 0) -> dict:
    key = jax.random.key(seed)
    ks = jax.random.split(key, 40)
    f32 = jnp.float32
    nrm = lambda k, shape, s: jax.random.normal(k, shape, f32) * s
    u = jax.random.uniform(ks[20], (DEPTH, D_RNN), f32, minval=0.9, maxval=0.999)
    p = u ** (1.0 / RG_C)
    rg_lambda = jnp.log(p) - jnp.log1p(-p)
    return {
        'x_prompt': nrm(ks[0], (BATCH, SEQ, D_MODEL), 1.0),
        'x_sample': nrm(ks[1], (DEC_BATCH, DEC_SEQ, D_MODEL), 1.0),
        'cache_k': nrm(ks[2], (DEPTH, DEC_BATCH, PAST_LEN, N_HEADS, 2, QK_HEAD_DIM), 1.0),
        'cache_v': nrm(ks[3], (DEPTH, DEC_BATCH, PAST_LEN, N_HEADS, V_HEAD_DIM), 1.0),
        'state_conv': nrm(ks[4], (DEPTH, DEC_BATCH, CONV_WIDTH - 1, D_RNN), 1.0),
        'state_rnn': nrm(ks[5], (DEPTH, DEC_BATCH, D_RNN), 0.5),
        'norm1_g': 1.0 + nrm(ks[6], (DEPTH, D_MODEL), 0.02),
        'w_in': nrm(ks[7], (DEPTH, D_MODEL, IN_WIDTH), D_MODEL ** -0.5),
        'lambda_q1': nrm(ks[8], (DEPTH, QK_HEAD_DIM), 0.1),
        'lambda_k1': nrm(ks[9], (DEPTH, QK_HEAD_DIM), 0.1),
        'lambda_q2': nrm(ks[10], (DEPTH, QK_HEAD_DIM), 0.1),
        'lambda_k2': nrm(ks[11], (DEPTH, QK_HEAD_DIM), 0.1),
        'subln_g': 1.0 + nrm(ks[12], (DEPTH, V_HEAD_DIM), 0.02),
        'w_attn_proj': nrm(ks[13], (DEPTH, ATTN_WIDTH, D_MODEL), ATTN_WIDTH ** -0.5),
        'conv_w': nrm(ks[14], (DEPTH, CONV_WIDTH, D_RNN), CONV_WIDTH ** -0.5),
        'conv_b': nrm(ks[15], (DEPTH, D_RNN), 0.01),
        'w_rg_a': nrm(ks[16], (DEPTH, N_RNN_BLOCKS, RNN_BLOCK, RNN_BLOCK), RNN_BLOCK ** -0.5),
        'b_rg_a': nrm(ks[17], (DEPTH, D_RNN), 0.01),
        'w_rg_i': nrm(ks[18], (DEPTH, N_RNN_BLOCKS, RNN_BLOCK, RNN_BLOCK), RNN_BLOCK ** -0.5),
        'b_rg_i': nrm(ks[19], (DEPTH, D_RNN), 0.01),
        'rg_lambda': rg_lambda,
        'w_rnn_proj': nrm(ks[21], (DEPTH, D_RNN, D_MODEL), D_RNN ** -0.5),
        'b_gate': nrm(ks[22], (DEPTH, N_BRANCHES * D_MODEL), 0.01),
        'w_out': nrm(ks[23], (DEPTH, D_MODEL, D_MODEL), D_MODEL ** -0.5),
        'norm2_g': 1.0 + nrm(ks[24], (DEPTH, D_MODEL), 0.02),
        'w_group': nrm(ks[25], (DEPTH, D_MODEL, N_GROUPS), D_MODEL ** -0.5),
        'b_group': nrm(ks[26], (DEPTH, N_GROUPS), 0.01),
        'w_router': nrm(ks[27], (DEPTH, D_MODEL, N_EXPERTS), D_MODEL ** -0.5),
        'b_router': nrm(ks[28], (DEPTH, N_EXPERTS), 0.01),
        'w1': nrm(ks[29], (DEPTH, N_EXPERTS, D_MODEL, D_EXPERT), D_MODEL ** -0.5),
        'w3': nrm(ks[30], (DEPTH, N_EXPERTS, D_MODEL, D_EXPERT), D_MODEL ** -0.5),
        'w2': nrm(ks[31], (DEPTH, N_EXPERTS, D_EXPERT, D_MODEL), D_EXPERT ** -0.5),
        'final_norm_g': 1.0 + nrm(ks[32], (D_MODEL,), 0.02),
    }

def reference(x_prompt, x_sample, cache_k, cache_v, state_conv, state_rnn, norm1_g, w_in,
              lambda_q1, lambda_k1, lambda_q2, lambda_k2, subln_g, w_attn_proj, conv_w, conv_b,
              w_rg_a, b_rg_a, w_rg_i, b_rg_i, rg_lambda, w_rnn_proj, b_gate, w_out, norm2_g,
              w_group, b_group, w_router, b_router, w1, w3, w2, final_norm_g):
    xp = x_prompt
    xs = x_sample
    kp_l, vp_l, cp_l, hp_l = [], [], [], []
    ks_l, vs_l, cs_l, hs_l = [], [], [], []
    for l in range(DEPTH):
        lp = {
            'norm1_g': norm1_g[l], 'w_in': w_in[l],
            'lambda_q1': lambda_q1[l], 'lambda_k1': lambda_k1[l],
            'lambda_q2': lambda_q2[l], 'lambda_k2': lambda_k2[l],
            'subln_g': subln_g[l], 'w_attn_proj': w_attn_proj[l],
            'conv_w': conv_w[l], 'conv_b': conv_b[l],
            'w_rg_a': w_rg_a[l], 'b_rg_a': b_rg_a[l], 'w_rg_i': w_rg_i[l], 'b_rg_i': b_rg_i[l],
            'rg_lambda': rg_lambda[l], 'w_rnn_proj': w_rnn_proj[l], 'b_gate': b_gate[l],
            'w_out': w_out[l], 'norm2_g': norm2_g[l],
            'w_group': w_group[l], 'b_group': b_group[l],
            'w_router': w_router[l], 'b_router': b_router[l],
            'w1': w1[l], 'w3': w3[l], 'w2': w2[l],
        }
        xp, (kp, vp, cp, hp) = _layer(xp, lp, l, None)
        xs, (kk, vv, cc, hh) = _layer(xs, lp, l, (cache_k[l], cache_v[l], state_conv[l], state_rnn[l]))
        kp_l.append(kp)
        vp_l.append(vp)
        cp_l.append(cp)
        hp_l.append(hp)
        ks_l.append(kk)
        vs_l.append(vv)
        cs_l.append(cc)
        hs_l.append(hh)
    y_prompt = _rmsnorm(xp, final_norm_g)
    y_sample = _rmsnorm(xs, final_norm_g)
    return (y_prompt, y_sample,
            jnp.stack(kp_l), jnp.stack(vp_l), jnp.stack(cp_l), jnp.stack(hp_l),
            jnp.stack(ks_l), jnp.stack(vs_l), jnp.stack(cs_l), jnp.stack(hs_l))


_drawn_inputs = setup_inputs


def setup_inputs(seed=0):
    import zlib

    import numpy as np

    out = dict(_drawn_inputs(seed))
    spreads = {}
    factors = {'lambda_k1': 8.0,
     'lambda_q2': 8.0,
     'b_rg_a': 23.059,
     'b_rg_i': 8.0,
     'b_gate': 8.0,
     'b_group': 25.416,
     'b_router': 24.902,
     'final_norm_g': 20.629,
     'subln_g': 9.043,
     'norm2_g': 3.556}
    for name, (base, spread) in spreads.items():
        noise = np.random.default_rng([zlib.crc32(name.encode()), seed]).standard_normal(out[name].shape)
        drawn = base * np.exp(spread * noise) if base else spread * noise
        out[name] = jnp.asarray(drawn.astype(out[name].dtype))
    for name, factor in factors.items():
        out[name] = (out[name] * factor).astype(out[name].dtype)
    return out
```

```python
from contextlib import ExitStack

import numpy as np

import concourse.bass as bass
from concourse import mybir

F32 = mybir.dt.float32
I32 = mybir.dt.int32
ACT = mybir.ActivationFunctionType
ALU = mybir.AluOpType
AX = mybir.AxisListType

P = 128
D = 1024
KT = D // P
SEQ, NS, DS, PAST = 512, 8, 16, 256
NQ = SEQ // P
TOK = SEQ + NS * DS
TT = TOK // P
HALF = TOK // 2
H, DH, DV = 8, 64, 128
CW = 4
NG, EG = 4, 4
NE = NG * EG
FE = 512
EPS = 1e-6
LAM0 = 0.8 - 0.6
SCALE = DH ** -0.5
BIG = float(2 ** 100)
KNEW = PAST
SKEYS = PAST + P
NSEL = 2 * TOK
OVMAX = (NSEL - NE) // P
NBLK = NE + OVMAX
CREDIT = 1
GELU_C = float(np.sqrt(2.0 / np.pi))

R_CW, R_CB, R_BA, R_BI, R_LAM, R_GA, R_GR, R_N1 = 0, 4, 5, 6, 7, 8, 9, 10
NROW = 11
C_SP2 = 11
NCOL = 12

K_ID, K_ONE, K_TRI, K_SEL, K_M0, K_M1, K_MASKQ, K_MASKV, K_IND, K_MST, K_EID, K_BLK, K_TOK = (
    0, 128, 256, 384, 448, 449, 450, 578, 642, 898, 1026, 1042, 1051)
NK = K_TOK + TT


def shape_constants():
    c = np.zeros((P, NK), np.float32)
    p = np.arange(P)
    c[:, K_ID:K_ID + P] = np.eye(P)
    c[:, K_ONE:K_ONE + P] = 1.0
    c[:, K_TRI:K_TRI + P] = p[:, None] < p[None, :]
    b4, m, q = p // 32, (p // 16) % 2, p % 16
    c[p, K_SEL + b4 * 16 + q] = 1.0
    c[:, K_M0] = m == 0
    c[:, K_M1] = m == 1
    c[0, K_MASKQ:K_MASKQ + 64] = 1.0
    c[0, K_MASKV:K_MASKV + 64] = -BIG
    for g in range(2):
        for r in range(P):
            c[4 * g + b4[r], K_IND + g * P + r] = 1.0
    for b in range(NS):
        c[b, K_MST:K_MST + P] = np.where(p // DS == b, 0.0, -BIG)
    c[:, K_EID:K_EID + NE] = np.arange(NE)
    c[:, K_BLK:K_BLK + OVMAX] = np.arange(OVMAX)
    c[:, K_TOK:K_TOK + TT] = p[:, None] + P * np.arange(TT)
    return c


class Chain:

    def __init__(self, eng, sem, start=0):
        self.eng, self.sem, self.base, self.n = eng, sem, start, 0

    def at(self, base):
        self.base, self.n = base, 0

    def __call__(self, ins):
        self.n += 1
        ins.then_inc(self.sem, 1)
        self.eng.wait_ge(self.sem, self.base + self.n)


def build(nc, A, O):
    top = ExitStack()
    with top:
        def sb(name, shape, dt=F32, ctx=top):
            return ctx.enter_context(nc.sbuf_tensor(name, shape, dt))

        def sem(name):
            return top.enter_context(nc.semaphore(name))

        bank = [top.enter_context(nc.psum_tensor(f"bank{i}", [P, 512], F32)) for i in range(8)]
        cst = sb("cst", [P, NK])
        ident = cst[:, K_ID:K_ID + P]
        ones = cst[:, K_ONE:K_ONE + P]
        pcol = sb("pcol", [P, KT, NCOL])
        scol = sb("scol", [P, KT, 32])
        subln = sb("subln", [P, 1])
        lam = sb("lam", [P, 8])
        neglam, msign = lam[:, 0:1], lam[:, 1:2]
        eps_t = sb("eps_t", [P, 1])

        xn2_d = nc.dram_tensor("xn2_scratch", (TOK, D), F32, kind="Internal").ap()
        idx_d = nc.dram_tensor("block_tokens", (NBLK * P, 1), I32, kind="Internal").ap()
        y_d = nc.dram_tensor("block_outputs", (NBLK * P, D), F32, kind="Internal").ap()

        xp = A["x_prompt"].rearrange("b (t p) d -> p (b t) d", p=P)
        xs = A["x_sample"].rearrange("b s d -> (b s) d")

        mid = ExitStack()
        xnT = sb("xnT", [P, KT, TOK], ctx=mid)
        st1 = ExitStack()
        xt = sb("xt", [P, TT, D], ctx=st1)
        xn = sb("xn", [P, TT, D], ctx=st1)
        prow = sb("prow", [NROW, D], ctx=st1)
        srow = sb("srow", [32, D], ctx=st1)
        lvec = sb("lvec", [P, 4, DH], ctx=st1)
        ljunk = sb("ljunk", [P, 2, DH], ctx=st1)
        lsum = sb("lsum", [P, 4], ctx=st1)
        sq1 = sb("sq1", [P, D], ctx=st1)
        ss1 = sb("ss1", [P, 2, TT], ctx=st1)
        sp = sb("sp", [P, 6, KT], ctx=st1)
        zidx = sb("zidx", [NBLK, P], I32, ctx=st1)

        cst_in, x_in, rows_in, lam_in = sem("cst_in"), sem("x_in"), sem("rows_in"), sem("lam_in")
        zero = sb("zero", [P, D], ctx=st1)
        zero_set, y_zeroed = sem("zero_set"), sem("y_zeroed")
        idx_zeroed, zidx_set = sem("idx_zeroed"), sem("zidx_set")
        eps_set, squares, roots1 = sem("eps_set"), sem("squares"), sem("roots1")
        xn_ready, cols_turned, cols_out = sem("xn_ready"), sem("cols_turned"), sem("cols_out")
        xn_turned, xnT_out = sem("xn_turned"), sem("xnT_out")
        lam_dots, lam_exps, sp_in, sp_exp = sem("lam_dots"), sem("lam_exps"), sem("sp_in"), sem("sp_exp")
        dve1, act1 = sem("dve1"), sem("act1")

        with nc.Block() as block:
            @block.sync
            def _(sp_):
                sp_.dma_start(cst[:, :], A["shape_constants"]).then_inc(cst_in, 16)
                for t in range(TT):
                    src = xp[:, t, :] if t < NQ else xs
                    sp_.dma_start(xt[:, t, :], src).then_inc(x_in, 16)
                for r, n, src in ((R_CW, 4, A["conv_w"][0]), (R_CB, 1, A["conv_b"]), (R_BA, 1, A["b_rg_a"]),
                                  (R_BI, 1, A["b_rg_i"]), (R_LAM, 1, A["rg_lambda"]),
                                  (R_GA, 2, A["b_gate"].rearrange("l (g d) -> (l g) d", g=2)),
                                  (R_N1, 1, A["norm1_g"])):
                    sp_.dma_start(prow[r:r + n, :], src).then_inc(rows_in, 16)
                sp_.dma_start(srow[0:24, :], A["state_conv"].rearrange("l b w d -> (l b w) d")).then_inc(rows_in, 16)
                sp_.dma_start(srow[24:32, :], A["state_rnn"][0]).then_inc(rows_in, 16)
                for i, n in enumerate(("lambda_q1", "lambda_k1", "lambda_q2", "lambda_k2")):
                    sp_.dma_start(lvec[:, i, :], A[n].to_broadcast([P, DH])).then_inc(lam_in, 16)
                sp_.dma_start(subln[:, :], A["subln_g"].rearrange("l d -> d l")).then_inc(lam_in, 16)
                sp_.wait_ge(zidx_set, 1)
                sp_.dma_start(idx_d.rearrange("(b p) o -> b (p o)", p=P), zidx[:, :]).then_inc(idx_zeroed, 16)
                sp_.wait_ge(idx_zeroed, 16)

            @block.gpsimd
            def _(pool):
                nc.gpsimd.memset(zidx[:, :], 0).then_inc(zidx_set, 1)
                nc.gpsimd.memset(zero[:, :], 0.0).then_inc(zero_set, 1)
                pool.wait_ge(zero_set, 1)
                for b in range(NE, NBLK):
                    pool.dma_start(y_d[b * P:(b + 1) * P, :], zero[:, :]).then_inc(y_zeroed, 16)
                pool.wait_ge(y_zeroed, 16 * OVMAX)

            @block.scalar
            def _(act):
                for t in range(TT):
                    act.wait_ge(x_in, 16 * TT)
                    nc.scalar.activation(sq1[:, :], xt[:, t, :], ACT.Square, accum_out=ss1[:, 0, t:t + 1]) \
                        .then_inc(squares, 1)
                    act.wait_ge(squares, t + 1)
                act.wait_ge(eps_set, 1)
                nc.scalar.activation(ss1[:, 1, :], ss1[:, 0, :], ACT.Sqrt, scale=1.0 / D,
                                     bias=eps_t[:, 0:1]).then_inc(roots1, 1)
                act.wait_ge(lam_dots, 2)
                nc.scalar.activation(lsum[:, 2:4], lsum[:, 0:2], ACT.Exp).then_inc(lam_exps, 1)
                act.wait_ge(sp_in, 1)
                nc.scalar.activation(sp[:, 1, :], sp[:, 0, :], ACT.Exp).then_inc(sp_exp, 1)

            @block.vector
            def _(dve):
                chain = Chain(dve, dve1)
                nc.vector.memset(eps_t[:, :], EPS).then_inc(eps_set, 1)
                dve.wait_ge(roots1, 1)
                chain(nc.vector.reciprocal(ss1[:, 0, :], ss1[:, 1, :]))
                for t in range(TT):
                    nc.vector.tensor_scalar(xn[:, t, :], xt[:, t, :], ss1[:, 0, t:t + 1], None, ALU.mult) \
                        .then_inc(xn_ready, 1)
                dve.wait_ge(cols_turned, 1)
                nc.vector.tensor_copy(pcol[:, :, 0:NROW],
                                      bank[0][:, 0:KT * 16].rearrange("p (k r) -> p k r", r=16)[:, :, 0:NROW]) \
                    .then_inc(cols_out, 1)
                nc.vector.tensor_copy(scol[:, :, :], bank[1][:, 0:KT * 32].rearrange("p (k r) -> p k r", r=32)) \
                    .then_inc(cols_out, 1)
                dve.wait_ge(cols_out, 2)
                for t in range(TT):
                    for half in range(2):
                        u = 2 * t + half
                        dve.wait_ge(xn_turned, u + 1)
                        nc.vector.tensor_tensor(
                            xnT[:, 4 * half:4 * half + 4, t * P:(t + 1) * P],
                            bank[2 + u % 4][:, :].rearrange("p (k q) -> p k q", q=P),
                            pcol[:, 4 * half:4 * half + 4, R_N1:R_N1 + 1].to_broadcast([P, 4, P]),
                            ALU.mult).then_inc(xnT_out, 1)
                dve.wait_ge(lam_in, 16 * 5)
                for i in range(2):
                    nc.vector.tensor_tensor_reduce(ljunk[:, i, :], lvec[:, 2 * i, :], lvec[:, 2 * i + 1, :], 1.0, 0.0,
                                                   ALU.mult, ALU.add, lsum[:, i:i + 1]).then_inc(lam_dots, 1)
                chain(nc.vector.tensor_scalar(sp[:, 2, :], pcol[:, :, R_LAM], -1.0, None, ALU.mult))
                nc.vector.tensor_tensor(sp[:, 0, :], sp[:, 2, :], pcol[:, :, R_LAM], ALU.min).then_inc(sp_in, 1)
                chain(nc.vector.tensor_scalar(sp[:, 2, :], sp[:, 2, :], 0.0, 2.0, ALU.max, ALU.mult))
                dve.wait_ge(sp_exp, 1)
                chain(nc.vector.tensor_scalar(sp[:, 3, :], sp[:, 1, :], 2.0, None, ALU.add))
                chain(nc.vector.reciprocal(sp[:, 3, :], sp[:, 3, :]))
                chain(nc.vector.tensor_tensor(sp[:, 3, :], sp[:, 3, :], sp[:, 1, :], ALU.mult))
                chain(nc.vector.tensor_tensor(sp[:, 4, :], sp[:, 3, :], sp[:, 3, :], ALU.mult))
                chain(nc.vector.tensor_scalar(sp[:, 5, :], sp[:, 4, :], 1.0 / 19, 1.0 / 17, ALU.mult, ALU.add))
                for n in range(15, 0, -2):
                    chain(nc.vector.tensor_tensor(sp[:, 5, :], sp[:, 5, :], sp[:, 4, :], ALU.mult))
                    chain(nc.vector.tensor_scalar(sp[:, 5, :], sp[:, 5, :], 1.0 / n, None, ALU.add))
                chain(nc.vector.tensor_tensor(sp[:, 5, :], sp[:, 5, :], sp[:, 3, :], ALU.mult))
                nc.vector.scalar_tensor_tensor(pcol[:, :, C_SP2], sp[:, 5, :], 4.0, sp[:, 2, :], ALU.mult, ALU.add)
                nc.vector.tensor_scalar(pcol[:, :, R_BA:R_BI + 1], pcol[:, :, R_BA:R_BI + 1], 0.5, None, ALU.mult)
                nc.vector.tensor_scalar(pcol[:, :, R_GA:R_GR + 1], pcol[:, :, R_GA:R_GR + 1], 0.5, None, ALU.mult)
                nc.vector.tensor_scalar(subln[:, :], subln[:, :], 1.0 - LAM0, None, ALU.mult)
                dve.wait_ge(lam_exps, 1)
                chain(nc.vector.tensor_tensor(neglam, lsum[:, 3:4], lsum[:, 2:3], ALU.subtract))
                chain(nc.vector.tensor_scalar(neglam, neglam, -LAM0, None, ALU.add))
                dve.wait_ge(cst_in, 16)
                chain(nc.vector.scalar_tensor_tensor(msign, cst[:, K_M1:K_M1 + 1], neglam, cst[:, K_M0:K_M0 + 1],
                                                     ALU.mult, ALU.add))

            @block.tensor
            def _(pe):
                pe.wait_ge(cst_in, 16)
                pe.wait_ge(rows_in, 16 * 9)
                for k in range(KT):
                    nc.tensor.transpose(bank[0][:, 16 * k:16 * k + NROW], prow[:, k * P:(k + 1) * P],
                                        ident[0:NROW, 0:NROW])
                    last = nc.tensor.transpose(bank[1][:, 32 * k:32 * k + 32], srow[:, k * P:(k + 1) * P],
                                               ident[0:32, 0:32])
                last.then_inc(cols_turned, 1)
                for t in range(TT):
                    pe.wait_ge(xn_ready, t + 1)
                    for half in range(2):
                        u = 2 * t + half
                        if u >= 4:
                            pe.wait_ge(xnT_out, u - 3)
                        for k in range(4):
                            last = nc.tensor.transpose(bank[2 + u % 4][:, k * P:(k + 1) * P],
                                                       xn[:, t, (4 * half + k) * P:(4 * half + k + 1) * P], ident)
                        last.then_inc(xn_turned, 1)
        st1.close()

        yT = sb("yT", [P, KT, TOK], ctx=mid)
        on = sb("on", [P, H, NQ, DV], ctx=mid)
        oTs = sb("oTs", [P, H, P], ctx=mid)
        stc = sb("stc", [P, KT, P], ctx=mid)
        st2 = ExitStack()
        wb = [sb(f"wb{i}", [P, KT, 5, P], ctx=st2) for i in range(2)]
        wrg = [sb(f"wrg{i}", [P, 2, P], ctx=st2) for i in range(2)]
        kc = sb("kc", [P, NS * 2, P], ctx=st2)
        vc = sb("vc", [P, NS * 2, P], ctx=st2)
        hcol = [sb(f"hcol{i}", [P, NCOL + 32], ctx=st2) for i in range(2)]
        kvt = [sb(f"kvt{i}", [P, TT, 2, P], ctx=st2) for i in range(2)]
        qT = sb("qT", [P, TOK], ctx=st2)
        kT = sb("kT", [P, TOK], ctx=st2)
        kcT = sb("kcT", [P, NS, PAST], ctx=st2)
        qbd = sb("qbd", [P, NS, 2, DS], ctx=st2)
        ebuf = [sb(f"ebuf{i}", [P, 2, 512], ctx=st2) for i in range(2)]
        wc = [sb(f"wc{i}", [P, 512], ctx=st2) for i in range(2)]
        wT = [sb(f"wT{i}", [P, 512], ctx=st2) for i in range(2)]
        wTs = sb("wTs", [P, 3, P], ctx=st2)
        selc = sb("selc", [P, 2, 64], ctx=st2)
        stat = sb("stat", [P, 5, 10], ctx=st2)
        oraw = sb("oraw", [P, NQ, DV], ctx=st2)
        osq = sb("osq", [P, NQ, DV], ctx=st2)
        oms = sb("oms", [P, 4 * NQ], ctx=st2)
        xpad = sb("xpad", [P, 3 + SEQ], ctx=st2)
        spad = sb("spad", [P, NS, 3 + DS], ctx=st2)
        xc = sb("xc", [P, TOK], ctx=st2)
        thr = sb("thr", [P, TOK], ctx=st2)
        thi = sb("thi", [P, TOK], ctx=st2)
        gr = sb("gr", [P, TOK], ctx=st2)
        gw = sb("gw", [P, TOK], ctx=st2)
        ra = sb("ra", [P, TOK], ctx=st2)
        rw = sb("rw", [P, TOK], ctx=st2)
        rh = sb("rh", [P, TOK], ctx=st2)
        h0t = sb("h0t", [P, NS], ctx=st2)

        w_in = [sem(f"w_in{i}") for i in range(2)]
        kc_in, vc_in = sem("kc_in"), sem("vc_in")
        col_in = [sem(f"col_in{i}") for i in range(2)]
        kv_stored = [sem(f"kv_stored{i}") for i in range(2)]
        pr_done, pr_act, pr_dve = sem("pr_done"), sem("pr_act"), sem("pr_dve")
        pt_done, pt_out = sem("pt_done"), sem("pt_out")
        ss_done, sc_done, max_ready, exp_done = sem("ss_done"), sem("sc_done"), sem("max_ready"), sem("exp_done")
        selc_ready, comb_ready = sem("selc_ready"), sem("comb_ready")
        os_done, os_out, op_done, op_out = sem("os_done"), sem("os_out"), sem("op_done"), sem("op_out")
        conv_done, gcube, gtanh = sem("conv_done"), sem("gcube"), sem("gtanh")
        decay, ms_ready, roots2, rnn_done = sem("decay"), sem("ms_ready"), sem("roots2"), sem("rnn_done")
        init2, dve2, act2 = sem("init2"), sem("dve2"), sem("act2")
        DVE_STEPS = 33

        UNITS = ["kv0", "kv1", "kv2", "kv3", "kv4", "q0", "q1", "kT0", "kT1", "kT2", "xr0", "xr1",
                 "gr0", "gr1", "ra0", "ra1", "ri0", "ri1"]
        ON_DVE = [u for u in UNITS if u[:2] in ("kv", "xr")]
        ON_ACT = [u for u in UNITS if u not in ON_DVE]
        NU = len(UNITS)
        RING = 3
        NT = 9
        w_cols = A["w_in"][0].rearrange("(k p) n -> p k n", p=P)

        def unit_bank(name):
            return bank[UNITS.index(name) % RING]

        def wait_unit(eng, h, name):
            eng.wait_ge(pr_done, h * NU + (UNITS.index(name) + 1))

        with nc.Block() as block:
            @block.sync
            def _(sp_):
                def load_weights(h, par):
                    for j in range(5):
                        sp_.dma_start(wb[par][:, :, j, :], w_cols[:, :, bass.ds(h * P + j * D, P)]) \
                            .then_inc(w_in[par], 16)
                    sp_.dma_start(hcol[par][:, 0:NCOL], pcol[:, bass.ds(h, 1), :].rearrange("p o c -> p (o c)")) \
                        .then_inc(col_in[par], 16)
                    sp_.dma_start(hcol[par][:, NCOL:], scol[:, bass.ds(h, 1), :].rearrange("p o c -> p (o c)")) \
                        .then_inc(col_in[par], 16)
                    for j, n in enumerate(("w_rg_a", "w_rg_i")):
                        sp_.dma_start(wrg[par][:, j, :], A[n][0, bass.ds(h, 1)].rearrange("o i j -> i (o j)")) \
                            .then_inc(col_in[par], 16)

                def load_cache(h, dst, src, s):
                    sp_.dma_start(dst[:, :, :], src.rearrange("b (k p) c -> p (b k) c", p=P)[:, :, bass.ds(h * P, P)]) \
                        .then_inc(s, 16)

                def store_kv(h, par):
                    sp_.wait_ge(pr_dve, CREDIT + h * len(ON_DVE) + TT)
                    for j, n in enumerate(("k", "v")):
                        outp, outs = O[f"new_{n}_prompt"][0, 0], O[f"new_{n}_sample"][0]
                        if n == "k":
                            outp, outs = outp.rearrange("s h m d -> s h (m d)"), outs.rearrange("b s h m d -> b s h (m d)")
                        outp = outp.rearrange("(t p) h c -> p t (h c)", p=P)
                        outs = outs.rearrange("b s h c -> (b s) (h c)")
                        sp_.dma_start(outp[:, :, bass.ds(h * P, P)], kvt[par][:, 0:NQ, j, :]).then_inc(kv_stored[par], 16)
                        sp_.dma_start(outs[:, bass.ds(h * P, P)], kvt[par][:, NQ, j, :]).then_inc(kv_stored[par], 16)

                k_src = A["cache_k"][0].rearrange("b s h m d -> b s (h m d)")
                v_src = A["cache_v"][0].rearrange("b s h d -> b s (h d)")
                load_weights(0, 0)
                load_cache(0, kc, k_src, kc_in)
                load_cache(0, vc, v_src, vc_in)
                load_weights(1, 1)
                with sp_.Fori(0, H // 2 - 1) as i:
                    for par in range(2):
                        h = i * 2 + par
                        sp_.wait_ge(pt_done, h * NT + 4)
                        load_cache(h + 1, kc, k_src, kc_in)
                        store_kv(h, par)
                        sp_.wait_ge(os_done, h + 1)
                        load_cache(h + 1, vc, v_src, vc_in)
                        sp_.wait_ge(rnn_done, CREDIT + h + 1)
                        load_weights(h + 2, par)
                sp_.wait_ge(pt_done, (H - 2) * NT + 4)
                load_cache(H - 1, kc, k_src, kc_in)
                store_kv(H - 2, 0)
                sp_.wait_ge(os_done, H - 1)
                load_cache(H - 1, vc, v_src, vc_in)
                store_kv(H - 1, 1)
                for par in range(2):
                    sp_.wait_ge(kv_stored[par], CREDIT + 64 * (H // 2))

            @block.tensor
            def _(pe):
                def project(h, par, j, name, half):
                    ring_wait(h, par, name)
                    out = unit_bank(name)[:, 0:HALF]
                    for k in range(KT):
                        mm = nc.tensor.matmul(out, wb[par][:, k, j, :], xnT[:, k, half * HALF:(half + 1) * HALF],
                                              start=(k == 0), stop=(k == KT - 1))
                    mm.then_inc(pr_done, 1)

                def ring_wait(h, par, name):
                    n = UNITS.index(name) - RING
                    old = UNITS[n]
                    on_, s = (ON_DVE, pr_dve) if old in ON_DVE else (ON_ACT, pr_act)
                    back = len(on_) - (on_.index(old) + 1)
                    if n >= 0:
                        pe.wait_ge(s, CREDIT + h * len(on_) + (on_.index(old) + 1))
                    elif back == 0 or par == 1:
                        pe.wait_ge(s, CREDIT + h * len(on_) - back)
                    else:
                        pe.wait_ge(s, CREDIT + h * len(on_))

                def turn_wait(h, par, u):
                    if u >= 2:
                        pe.wait_ge(pt_out, CREDIT + h * NT + (u - 1))
                    else:
                        pe.wait_ge(pt_out, CREDIT + h * NT - (1 - u if par == 1 else 0))

                def tbank(par, u):
                    return bank[5 + (par * NT + u) % 2]

                def attend(h, par, qt):
                    L = qt + 1
                    u = 5 + qt
                    pe.wait_ge(comb_ready, h * NQ + (qt + 1))
                    turn_wait(h, par, u)
                    for k in range(L):
                        mm = nc.tensor.transpose(tbank(par, u)[:, k * P:(k + 1) * P],
                                                 wc[qt % 2][:, k * P:(k + 1) * P], ident)
                    mm.then_inc(pt_done, 1)
                    pe.wait_ge(pt_out, CREDIT + h * NT + (u + 1))
                    if qt == 0:
                        pe.wait_ge(os_out, h + 1)
                    for k in range(L):
                        mm = nc.tensor.matmul(bank[7][:, qt * P:(qt + 1) * P], wT[qt % 2][:, k * P:(k + 1) * P],
                                              kvt[par][:, k, 1, :], start=(k == 0), stop=(k == L - 1))
                    if qt == NQ - 1:
                        mm.then_inc(op_done, 1)

                def scores(h, qt):
                    n = (qt + 1) * P
                    pe.wait_ge(exp_done, CREDIT + h * 5 + (qt + 1))
                    for m in range(2):
                        rows = slice(m * DH, (m + 1) * DH)
                        nc.tensor.matmul(bank[3 + m][:, 0:n], qT[rows, qt * P:(qt + 1) * P], kT[rows, 0:n],
                                         start=True, stop=False)
                        mm = nc.tensor.matmul(bank[3 + m][:, n - 64:n], cst[0:1, K_MASKQ:K_MASKQ + P],
                                              cst[0:1, K_MASKV:K_MASKV + 64], start=False, stop=True)
                    mm.then_inc(sc_done, 1)

                pe.wait_ge(init2, 3)
                with pe.Fori(0, H // 2) as i:
                    for par in range(2):
                        h = i * 2 + par
                        pe.wait_ge(w_in[par], i * 80 + 80)
                        for t in range(TT):
                            ring_wait(h, par, f"kv{t}")
                            for k in range(KT):
                                mm = nc.tensor.matmul(unit_bank(f"kv{t}")[:, 0:2 * P], xnT[:, k, t * P:(t + 1) * P],
                                                      wb[par][:, k, 1:3, :], start=(k == 0), stop=(k == KT - 1))
                            mm.then_inc(pr_done, 1)
                        project(h, par, 0, "q0", 0)
                        project(h, par, 0, "q1", 1)
                        for n, ts in enumerate(((0, 1), (2, 3), (4,))):
                            ring_wait(h, par, f"kT{n}")
                            pe.wait_ge(pr_dve, CREDIT + h * len(ON_DVE) + (ts[-1] + 1))
                            for t in ts:
                                mm = nc.tensor.transpose(unit_bank(f"kT{n}")[:, (t % 2) * P:(t % 2 + 1) * P],
                                                         kvt[par][:, t, 0, :], ident)
                            mm.then_inc(pr_done, 1)
                        pe.wait_ge(kc_in, h * 16 + 16)
                        for u in range(4):
                            turn_wait(h, par, u)
                            for n in range(4):
                                mm = nc.tensor.transpose(tbank(par, u)[:, n * P:(n + 1) * P],
                                                         kc[:, 4 * u + n, :], ident)
                            mm.then_inc(pt_done, 1)
                        pe.wait_ge(pr_act, CREDIT + h * len(ON_ACT) + (ON_ACT.index("kT2") + 1))
                        pe.wait_ge(exp_done, CREDIT + h * 5)
                        for g in range(2):
                            nc.tensor.matmul(bank[3 + g][:, KNEW:SKEYS],
                                             qbd[:, 4 * g:4 * g + 4, :, :].rearrange("p b m q -> p (b m q)"),
                                             kT[:, SEQ:TOK], start=True, stop=False)
                            nc.tensor.matmul(bank[3 + g][:, KNEW:SKEYS], cst[0:NS, K_IND + g * P:K_IND + (g + 1) * P],
                                             cst[0:NS, K_MST:K_MST + P], start=False, stop=True)
                        pe.wait_ge(pt_out, CREDIT + h * NT + 4)
                        for b in range(NS):
                            r = 32 * (b % 4)
                            mm = nc.tensor.matmul(bank[3 + b // 4][r:r + 32, 0:PAST],
                                                  qbd[:, b, :, :].rearrange("p m q -> p (m q)"), kcT[:, b, :],
                                                  start=True, stop=True)
                        mm.then_inc(ss_done, 1)
                        project(h, par, 3, "xr0", 0)
                        project(h, par, 3, "xr1", 1)
                        pe.wait_ge(selc_ready, h + 1)
                        turn_wait(h, par, 4)
                        for k in range(3):
                            for g in range(2):
                                mm = nc.tensor.matmul(tbank(par, 4)[:, k * P + g * 64:k * P + g * 64 + 64],
                                                      ebuf[0][:, g, k * P:(k + 1) * P], selc[:, g, :],
                                                      start=True, stop=True)
                        mm.then_inc(pt_done, 1)
                        scores(h, 0)
                        project(h, par, 4, "gr0", 0)
                        pe.wait_ge(pt_out, CREDIT + h * NT + 5)
                        pe.wait_ge(vc_in, h * 16 + 16)
                        pe.wait_ge(op_out, CREDIT + h)
                        nc.tensor.matmul(bank[7][:, 0:P], kvt[par][:, NQ, 1, :], wTs[:, 2, :], start=True, stop=True)
                        for b in range(NS):
                            for k in range(2):
                                mm = nc.tensor.matmul(bank[7][:, b * DS:(b + 1) * DS], vc[:, 2 * b + k, :],
                                                      wTs[:, k, b * DS:(b + 1) * DS], start=False,
                                                      stop=True, skip_group_check=True)
                        mm.then_inc(os_done, 1)
                        attend(h, par, 0)
                        scores(h, 1)
                        project(h, par, 4, "gr1", 1)
                        attend(h, par, 1)
                        scores(h, 2)
                        pe.wait_ge(conv_done, h + 1)
                        pe.wait_ge(col_in[par], i * 64 + 64)
                        for j, name in enumerate(("ra0", "ra1", "ri0", "ri1")):
                            if name == "ri1":
                                attend(h, par, 2)
                                scores(h, 3)
                            ring_wait(h, par, name)
                            nc.tensor.matmul(unit_bank(name)[:, 0:HALF], wrg[par][:, j // 2, :],
                                             xc[:, (j % 2) * HALF:(j % 2 + 1) * HALF],
                                             start=True, stop=True).then_inc(pr_done, 1)
                        attend(h, par, 3)

            @block.scalar
            def _(act):
                def softmax_exp(h, u, n):
                    act.wait_ge(max_ready, h * 5 + (u + 1))
                    for m in range(2):
                        ins = nc.scalar.activation(ebuf[u % 2][:, m, 0:n], bank[3 + m][:, 0:n], ACT.Exp,
                                                   bias=stat[:, u, 2 + m:3 + m], scale=SCALE,
                                                   accum_out=stat[:, u, 4 + m:5 + m])
                    ins.then_inc(exp_done, 1)

                def turned(h, par, u, out, n):
                    act.wait_ge(pt_done, h * NT + (u + 1))
                    nc.scalar.activation(out, bank[5 + (par * NT + u) % 2][:, 0:n], ACT.Copy).then_inc(pt_out, 1)

                act.wait_ge(init2, 3)
                with act.Fori(0, H // 2) as i:
                    for par in range(2):
                        h = i * 2 + par
                        wait_unit(act, h, "q0")
                        nc.scalar.activation(qT[:, 0:HALF], unit_bank("q0")[:, 0:HALF], ACT.Copy).then_inc(pr_act, 1)
                        wait_unit(act, h, "q1")
                        qs = unit_bank("q1")[:, SEQ - HALF:HALF].rearrange("p (b q) -> p b q", q=DS)
                        for m in range(2):
                            rows = slice(m * DH, (m + 1) * DH)
                            nc.scalar.activation(qbd[rows, :, m, :], qs[rows], ACT.Copy)
                        nc.scalar.activation(qT[:, HALF:TOK], unit_bank("q1")[:, 0:HALF], ACT.Copy).then_inc(pr_act, 1)
                        for n, (c0, c1) in enumerate(((0, 256), (256, 512), (512, 640))):
                            wait_unit(act, h, f"kT{n}")
                            nc.scalar.activation(kT[:, c0:c1], unit_bank(f"kT{n}")[:, 0:c1 - c0], ACT.Copy) \
                                .then_inc(pr_act, 1)
                        for u in range(4):
                            turned(h, par, u, kcT[:, 2 * u:2 * u + 2, :].rearrange("p b k -> p (b k)"), 512)
                        act.wait_ge(ss_done, h + 1)
                        softmax_exp(h, 0, SKEYS)
                        turned(h, par, 4, wTs[:, :, :].rearrange("p k q -> p (k q)"), 3 * P)
                        softmax_exp(h, 1, P)
                        act.wait_ge(rnn_done, CREDIT + h)
                        wait_unit(act, h, "gr0")
                        nc.scalar.activation(gr[:, 0:HALF], unit_bank("gr0")[:, 0:HALF], ACT.Copy).then_inc(pr_act, 1)
                        turned(h, par, 5, wT[0][:, 0:P], P)
                        softmax_exp(h, 2, 2 * P)
                        wait_unit(act, h, "gr1")
                        nc.scalar.activation(gr[:, HALF:TOK], unit_bank("gr1")[:, 0:HALF], ACT.Copy).then_inc(pr_act, 1)
                        turned(h, par, 6, wT[1][:, 0:2 * P], 2 * P)
                        softmax_exp(h, 3, 3 * P)
                        act.wait_ge(col_in[par], i * 64 + 64)
                        for name, out, c in (("ra0", thr, R_BA), ("ra1", thr, R_BA), ("ri0", thi, R_BI)):
                            wait_unit(act, h, name)
                            s = slice(HALF * int(name[2]), HALF * int(name[2]) + HALF)
                            nc.scalar.activation(out[:, s], unit_bank(name)[:, 0:HALF], ACT.Tanh,
                                                 bias=hcol[par][:, c:c + 1], scale=0.5).then_inc(pr_act, 1)
                        turned(h, par, 7, wT[0][:, 0:3 * P], 3 * P)
                        softmax_exp(h, 4, 4 * P)
                        wait_unit(act, h, "ri1")
                        nc.scalar.activation(thi[:, HALF:TOK], unit_bank("ri1")[:, 0:HALF], ACT.Tanh,
                                             bias=hcol[par][:, R_BI:R_BI + 1], scale=0.5).then_inc(pr_act, 1)
                        turned(h, par, 8, wT[1][:, 0:4 * P], 4 * P)
                        act.wait_ge(pr_act, CREDIT + h * len(ON_ACT) + len(ON_ACT))
                        nc.scalar.activation(ra[:, :], thr[:, :], ACT.Tanh, bias=hcol[par][:, C_SP2:C_SP2 + 1],
                                             scale=hcol[par][:, C_SP2:C_SP2 + 1]).then_inc(decay, 1)
                        act.wait_ge(gcube, h + 1)
                        nc.scalar.activation(gw[:, :], gw[:, :], ACT.Tanh, scale=GELU_C).then_inc(gtanh, 1)
                        act.wait_ge(decay, h + 1)
                        nc.scalar.activation(rw[:, :], ra[:, :], ACT.Sqrt).then_inc(roots2, 1)
                        act.wait_ge(ms_ready, h + 1)
                        nc.scalar.activation(oms[:, NQ:2 * NQ], oms[:, 0:NQ], ACT.Sqrt, scale=1.0 / DV,
                                             bias=eps_t[:, 0:1]).then_inc(roots2, 1)

            @block.vector
            def _(dve):
                chain = Chain(dve, dve2)

                def row_max(h, u, n):
                    for m in range(2):
                        ins = nc.vector.tensor_reduce(stat[:, u, m:m + 1], bank[3 + m][:, 0:n], AX.X, ALU.max)
                    chain(ins)
                    nc.vector.tensor_scalar(stat[:, u, 2:4], stat[:, u, 0:2], -SCALE, None, ALU.mult) \
                        .then_inc(max_ready, 1)

                def combine(h, qt):
                    u = qt + 1
                    n = (qt + 1) * P
                    dve.wait_ge(exp_done, CREDIT + h * 5 + (u + 1))
                    chain(nc.vector.reciprocal(stat[:, u, 6:8], stat[:, u, 4:6]))
                    chain(nc.vector.scalar_tensor_tensor(stat[:, u, 8:9], stat[:, u, 4:5], stat[:, u, 7:8], neglam,
                                                         ALU.mult, ALU.mult))
                    nc.vector.scalar_tensor_tensor(wc[qt % 2][:, 0:n], ebuf[u % 2][:, 1, 0:n], stat[:, u, 8:9],
                                                   ebuf[u % 2][:, 0, 0:n], ALU.mult, ALU.add).then_inc(comb_ready, 1)

                dve.wait_ge(init2, 3)
                with dve.Fori(0, H // 2) as i:
                    for par in range(2):
                        h = i * 2 + par
                        chain.at(h * DVE_STEPS)
                        dve.wait_ge(kv_stored[par], CREDIT + i * 64)
                        for t in range(TT):
                            wait_unit(dve, h, f"kv{t}")
                            nc.vector.tensor_copy(kvt[par][:, t, :, :].rearrange("p j c -> p (j c)"),
                                                  unit_bank(f"kv{t}")[:, 0:2 * P]).then_inc(pr_dve, 1)
                        dve.wait_ge(ss_done, h + 1)
                        row_max(h, 0, SKEYS)
                        wait_unit(dve, h, "xr0")
                        nc.vector.tensor_copy(xpad[:, 3:3 + HALF], unit_bank("xr0")[:, 0:HALF]).then_inc(pr_dve, 1)
                        wait_unit(dve, h, "xr1")
                        nc.vector.tensor_copy(xpad[:, 3 + HALF:3 + SEQ], unit_bank("xr1")[:, 0:SEQ - HALF])
                        nc.vector.tensor_copy(spad[:, :, 3:], unit_bank("xr1")[:, SEQ - HALF:HALF]
                                              .rearrange("p (b q) -> p b q", q=DS)).then_inc(pr_dve, 1)
                        dve.wait_ge(col_in[par], i * 64 + 64)
                        chain(nc.vector.tensor_copy(spad[:, :, 0:3],
                                                    hcol[par][:, NCOL:NCOL + 24].rearrange("p (b w) -> p b w", w=3)))
                        dve.wait_ge(exp_done, CREDIT + h * 5 + 1)
                        chain(nc.vector.reciprocal(stat[:, 0, 6:8], stat[:, 0, 4:6]))
                        chain(nc.vector.tensor_scalar(stat[:, 0, 8:10], stat[:, 0, 6:8], msign, None, ALU.mult))
                        for g in range(2):
                            ins = nc.vector.tensor_scalar(selc[:, g, :], cst[:, K_SEL:K_SEL + 64],
                                                          stat[:, 0, 8 + g:9 + g], None, ALU.mult)
                        ins.then_inc(selc_ready, 1)
                        dve.wait_ge(sc_done, h * NQ + 1)
                        row_max(h, 1, P)
                        xcs = xc[:, SEQ:TOK].rearrange("p (b q) -> p b q", q=DS)
                        cw = hcol[par]
                        nc.vector.tensor_scalar(xc[:, 0:SEQ], xpad[:, 0:SEQ], cw[:, R_CW:R_CW + 1],
                                                cw[:, R_CB:R_CB + 1], ALU.mult, ALU.add)
                        chain(nc.vector.tensor_scalar(xcs, spad[:, :, 0:DS], cw[:, R_CW:R_CW + 1],
                                                      cw[:, R_CB:R_CB + 1], ALU.mult, ALU.add))
                        for j in range(1, CW):
                            nc.vector.scalar_tensor_tensor(xc[:, 0:SEQ], xpad[:, j:j + SEQ], cw[:, j:j + 1],
                                                           xc[:, 0:SEQ], ALU.mult, ALU.add)
                            ins = nc.vector.scalar_tensor_tensor(xcs, spad[:, :, j:j + DS], cw[:, j:j + 1],
                                                                 xcs, ALU.mult, ALU.add)
                            if j < CW - 1:
                                chain(ins)
                        ins.then_inc(conv_done, 1)
                        nc.vector.tensor_scalar(stc[:, bass.ds(h, 1), 0:3], xpad[:, SEQ:SEQ + 3]
                                                .rearrange("p (o c) -> p o c", o=1), 1.0, None, ALU.mult)
                        nc.vector.tensor_scalar(stc[:, bass.ds(h, 1), 3:27].rearrange("p o (b w) -> p (o b) w", w=3),
                                                spad[:, :, DS:DS + 3], 1.0, None, ALU.mult)
                        dve.wait_ge(os_done, h + 1)
                        nc.vector.tensor_scalar(oTs[:, bass.ds(h, 1), :], bank[7][:, 0:P]
                                                .rearrange("p (o c) -> p o c", o=1), 1.0, None, ALU.mult) \
                            .then_inc(os_out, 1)
                        combine(h, 0)
                        dve.wait_ge(sc_done, h * NQ + 2)
                        row_max(h, 2, 2 * P)
                        dve.wait_ge(pr_act, CREDIT + h * len(ON_ACT) + (ON_ACT.index("gr0") + 1))
                        combine(h, 1)
                        dve.wait_ge(sc_done, h * NQ + 3)
                        row_max(h, 3, 3 * P)
                        dve.wait_ge(pr_act, CREDIT + h * len(ON_ACT) + (ON_ACT.index("gr1") + 1))
                        chain(nc.vector.tensor_tensor(gw[:, :], gr[:, :], gr[:, :], ALU.mult))
                        chain(nc.vector.tensor_scalar(gw[:, :], gw[:, :], 0.044715, 1.0, ALU.mult, ALU.add))
                        nc.vector.tensor_tensor(gw[:, :], gw[:, :], gr[:, :], ALU.mult).then_inc(gcube, 1)
                        combine(h, 2)
                        dve.wait_ge(sc_done, h * NQ + 4)
                        row_max(h, 4, 4 * P)
                        combine(h, 3)
                        dve.wait_ge(op_done, h + 1)
                        ins = nc.vector.tensor_tensor(oraw[:, :, :], bank[7][:, :].rearrange("p (t c) -> p t c", c=DV),
                                                      stat[:, 1:5, 6:7].to_broadcast([P, NQ, DV]), ALU.mult)
                        ins.then_inc(op_out, 1)
                        dve.wait_ge(op_out, CREDIT + h + 1)
                        chain(nc.vector.tensor_tensor(osq[:, :, :], oraw[:, :, :], oraw[:, :, :], ALU.mult))
                        nc.vector.tensor_reduce(oms[:, 0:NQ], osq[:, :, :], AX.X, ALU.add).then_inc(ms_ready, 1)
                        dve.wait_ge(decay, h + 1)
                        chain(nc.vector.tensor_scalar(thr[:, :], ra[:, :], 1.0, None, ALU.add))
                        chain(nc.vector.reciprocal(thr[:, :], thr[:, :]))
                        dve.wait_ge(roots2, h * 2 + 1)
                        chain(nc.vector.tensor_scalar(ra[:, :], thr[:, :], 2.0, -1.0, ALU.mult, ALU.add))
                        chain(nc.vector.scalar_tensor_tensor(thi[:, :], thi[:, :], 1.0, xc[:, :], ALU.add, ALU.mult))
                        chain(nc.vector.tensor_tensor(rw[:, :], rw[:, :], thr[:, :], ALU.mult))
                        chain(nc.vector.tensor_tensor(rw[:, :], rw[:, :], thi[:, :], ALU.mult))
                        a0 = ra[:, SEQ:TOK].rearrange("p (b q) -> p b q", q=DS)[:, :, 0]
                        b0 = rw[:, SEQ:TOK].rearrange("p (b q) -> p b q", q=DS)[:, :, 0]
                        chain(nc.vector.tensor_tensor(h0t[:, :], a0, hcol[par][:, NCOL + 24:NCOL + 32], ALU.mult))
                        nc.vector.tensor_tensor(b0, b0, h0t[:, :], ALU.add)
                        chain(nc.vector.memset(a0, 0.0))
                        chain(nc.vector.tensor_tensor_scan(rh[:, :], ra[:, :], rw[:, :], 0.0, ALU.mult, ALU.add))
                        nc.vector.tensor_scalar(stc[:, bass.ds(h, 1), 27:28], rh[:, SEQ - 1:SEQ]
                                                .rearrange("p (o c) -> p o c", o=1), 1.0, None, ALU.mult)
                        nc.vector.tensor_scalar(
                            stc[:, bass.ds(h, 1), 28:36],
                            rh[:, SEQ:TOK].rearrange("p (o b q) -> p o b q", o=1, q=DS)[:, :, :, DS - 1],
                            1.0, None, ALU.mult)
                        dve.wait_ge(gtanh, h + 1)
                        chain(nc.vector.scalar_tensor_tensor(gw[:, :], gw[:, :], 1.0, gr[:, :], ALU.add, ALU.mult))
                        nc.vector.scalar_tensor_tensor(
                            yT[:, bass.ds(h, 1), :], rh[:, :].rearrange("p (o c) -> p o c", o=1), 0.5,
                            gw[:, :].rearrange("p (o c) -> p o c", o=1), ALU.mult, ALU.mult).then_inc(rnn_done, 1)
                        dve.wait_ge(roots2, h * 2 + 2)
                        chain(nc.vector.reciprocal(oms[:, 2 * NQ:3 * NQ], oms[:, NQ:2 * NQ]))
                        nc.vector.tensor_tensor(
                            on[:, bass.ds(h, 1), :, :].rearrange("p o t c -> p (o t) c"), oraw[:, :, :],
                            oms[:, 2 * NQ:3 * NQ].rearrange("p (t o) -> p t o", o=1).to_broadcast([P, NQ, DV]),
                            ALU.mult)
                        assert chain.n == DVE_STEPS, chain.n

            @block.gpsimd
            def _(pool):
                for s in (pr_act, pr_dve, pt_out, exp_done, op_out, rnn_done, *kv_stored):
                    pool.sem_inc(s, CREDIT)
                nc.gpsimd.memset(qbd[:, :, :, :], 0.0).then_inc(init2, 1)
                nc.gpsimd.memset(xpad[:, 0:3], 0.0).then_inc(init2, 1)
                nc.gpsimd.memset(stc[:, :, :], 0.0).then_inc(init2, 1)
        st2.close()
        build_rest(nc, A, O, locals())
        mid.close()


def build_rest(nc, A, O, v):
    top, mid, bank, cst, ident, ones = (v[n] for n in ("top", "mid", "bank", "cst", "ident", "ones"))
    sb, sem, eps_t, pcol, subln = (v[n] for n in ("sb", "sem", "eps_t", "pcol", "subln"))
    xnT, yT, on, oTs, stc = (v[n] for n in ("xnT", "yT", "on", "oTs", "stc"))
    xn2_d, idx_d, y_d, xp, xs = (v[n] for n in ("xn2_d", "idx_d", "y_d", "xp", "xs"))

    def sbr(name, shape, ctx, dt=F32):
        return ctx.enter_context(nc.sbuf_tensor(name, shape, dt, side="right"))

    x2 = sbr("x2", [P, TT, D], top)
    late = ExitStack()
    mT = sbr("mT", [P, KT, TOK], late)
    wo = sbr("wo", [P, KT, D], late)
    st3 = ExitStack()
    attnT = sb("attnT", [P, KT, TOK], ctx=st3)
    wm = [sb(f"wm{i}", [P, KT, 4, P], ctx=st3) for i in range(2)]
    gcol = [sb(f"gcol{i}", [P, 2], ctx=st3) for i in range(2)]
    tg = sb("tg", [P, 2, TOK], ctx=st3)
    m1 = sb("m1", [P, TOK], ctx=st3)
    m2 = sb("m2", [P, TOK], ctx=st3)
    srow2 = sb("srow2", [P, D], ctx=st3)
    wm_in = [sem(f"wm_in{i}") for i in range(2)]
    x2_in, wo_in = sem("x2_in"), sem("wo_in")
    at_done, at_out, osq_ready, oms_done = sem("at_done"), sem("at_out"), sem("osq_ready"), sem("oms_done")
    oroot, os_norm, st_out, st_stored = sem("oroot"), sem("os_norm"), sem("st_out"), sem("st_stored")
    mg_done, mg_act, mg_dve, merged = sem("mg_done"), sem("mg_act"), sem("mg_dve"), sem("merged")
    dve3 = sem("dve3")
    KINDS = ("ga", "ap", "gr", "rp")
    NM = 2 * len(KINDS)
    w_cols = A["w_in"][0].rearrange("(k p) n -> p k n", p=P)
    gate0 = 5 * D

    with nc.Block() as block:
        @block.sync
        def _(sp_):
            def load(n, par):
                for j, src in enumerate((w_cols[:, :, bass.ds(gate0 + n * P, P)],
                                         A["w_attn_proj"][0].rearrange("(k p) n -> p k n", p=P)[:, :, bass.ds(n * P, P)],
                                         w_cols[:, :, bass.ds(gate0 + D + n * P, P)],
                                         A["w_rnn_proj"][0].rearrange("(k p) n -> p k n", p=P)[:, :, bass.ds(n * P, P)])):
                    sp_.dma_start(wm[par][:, :, j, :], src).then_inc(wm_in[par], 16)
                sp_.dma_start(gcol[par][:, :], pcol[:, bass.ds(n, 1), R_GA:R_GR + 1]
                              .rearrange("p o c -> p (o c)")).then_inc(wm_in[par], 16)

            load(0, 0)
            load(1, 1)
            for t in range(TT):
                sp_.dma_start(x2[:, t, :], xp[:, t, :] if t < NQ else xs).then_inc(x2_in, 16)
            sp_.dma_start(wo[:, :, :], A["w_out"][0].rearrange("(k p) n -> p k n", p=P)).then_inc(wo_in, 16)
            with sp_.Fori(0, KT // 2 - 1) as i:
                for par in range(2):
                    n = i * 2 + (2 + par)
                    sp_.wait_ge(merged, CREDIT + i * 2 + (1 + par))
                    load(n, par)
            sp_.wait_ge(st_out, 2)
            for dst, r0, r1 in ((O["new_conv_prompt"][0, 0], 0, 3),
                                (O["new_conv_sample"][0].rearrange("b w d -> (b w) d"), 3, 27),
                                (O["new_rnn_prompt"][0], 27, 28), (O["new_rnn_sample"][0], 28, 36)):
                sp_.dma_start(dst, srow2[r0:r1, :]).then_inc(st_stored, 16)
            sp_.wait_ge(st_stored, 64)

        @block.tensor
        def _(pe):
            for g in range(2):
                pe.wait_ge(osq_ready, g + 1)
                nc.tensor.matmul(bank[g][:, :], ones, attnT[:, 4 * g:4 * g + 4, 0:P], start=True, stop=True) \
                    .then_inc(oms_done, 1)
            for g in range(2):
                for k in range(4):
                    mm = nc.tensor.transpose(bank[2 + g][:, k * P:(k + 1) * P], stc[:, 4 * g + k, :], ident)
                mm.then_inc(oms_done, 1)
            for h in range(H):
                if h >= 4:
                    pe.wait_ge(at_out, h - 3)
                if h == 0:
                    pe.wait_ge(osq_ready, 2)
                for t in range(NQ):
                    mm = nc.tensor.transpose(bank[4 + h % 4][:, t * P:(t + 1) * P], on[:, h, t, :], ident)
                mm.then_inc(at_done, 1)
            pe.wait_ge(at_out, H)
            pe.wait_ge(os_norm, 2)
            pe.wait_ge(st_out, 2)
            with pe.Fori(0, KT // 2) as i:
                for par in range(2):
                    n = i * 2 + par
                    pe.wait_ge(wm_in[par], i * 80 + 80)
                    for j, kind in enumerate(KINDS):
                        src = {"ga": xnT, "ap": attnT, "gr": xnT, "rp": yT}[kind]
                        if kind[0] == "g":
                            pe.wait_ge(mg_act, CREDIT + n * 4)
                        else:
                            pe.wait_ge(mg_dve, CREDIT + n * 4)
                        for half in range(2):
                            for k in range(KT):
                                mm = nc.tensor.matmul(bank[2 * j + half][:, 0:HALF], wm[par][:, k, j, :],
                                                      src[:, k, half * HALF:(half + 1) * HALF],
                                                      start=(k == 0), stop=(k == KT - 1))
                            mm.then_inc(mg_done, 1)

        @block.gpsimd
        def _(pool):
            for s in (mg_act, mg_dve, merged):
                pool.sem_inc(s, CREDIT)

        @block.scalar
        def _(act):
            for g in range(2):
                act.wait_ge(oms_done, g + 1)
                nc.scalar.activation(tg[:, g, 0:512], bank[g][:, :], ACT.Sqrt, scale=1.0 / DV,
                                     bias=eps_t[:, 0:1]).then_inc(oroot, 1)
            for h in range(H):
                act.wait_ge(at_done, h + 1)
                if h == 0:
                    act.wait_ge(oms_done, 2)
                nc.scalar.activation(attnT[:, h, 0:SEQ], bank[4 + h % 4][:, :], ACT.Copy,
                                     scale=subln[:, 0:1]).then_inc(at_out, 1)
            act.wait_ge(os_norm, 2)
            with act.Fori(0, KT // 2) as i:
                for par in range(2):
                    n = i * 2 + par
                    act.wait_ge(wm_in[par], i * 80 + 80)
                    act.wait_ge(merged, CREDIT + n)
                    for j, kind in enumerate(KINDS):
                        for half in range(2):
                            if kind[0] != "g":
                                continue
                            act.wait_ge(mg_done, n * NM + (2 * j + half + 1))
                            nc.scalar.activation(tg[:, j // 2, half * HALF:(half + 1) * HALF],
                                                 bank[2 * j + half][:, 0:HALF], ACT.Tanh,
                                                 bias=gcol[par][:, j // 2:j // 2 + 1], scale=0.5).then_inc(mg_act, 1)

        @block.vector
        def _(dve):
            chain = Chain(dve, dve3)
            for g in range(2):
                nc.vector.tensor_tensor(attnT[:, 4 * g:4 * g + 4, 0:P], oTs[:, 4 * g:4 * g + 4, :],
                                        oTs[:, 4 * g:4 * g + 4, :], ALU.mult).then_inc(osq_ready, 1)
            for g in range(2):
                dve.wait_ge(oms_done, 2 + g + 1)
                nc.vector.tensor_copy(srow2[:, g * 512:(g + 1) * 512], bank[2 + g][:, :]).then_inc(st_out, 1)
            for g in range(2):
                dve.wait_ge(oroot, g + 1)
                chain(nc.vector.reciprocal(tg[:, g, 0:512], tg[:, g, 0:512]))
                nc.vector.scalar_tensor_tensor(attnT[:, 4 * g:4 * g + 4, SEQ:TOK], oTs[:, 4 * g:4 * g + 4, :],
                                               subln[:, 0:1], tg[:, g, 0:512].rearrange("p (k q) -> p k q", q=P),
                                               ALU.mult, ALU.mult).then_inc(os_norm, 1)
            with dve.Fori(0, KT // 2) as i:
                for par in range(2):
                    n = i * 2 + par
                    for j, kind in enumerate(KINDS):
                        if kind[0] == "g":
                            continue
                        dst = m1 if kind[0] == "a" else m2
                        for half in range(2):
                            s = slice(half * HALF, (half + 1) * HALF)
                            dve.wait_ge(mg_done, n * NM + (2 * j + half + 1))
                            dve.wait_ge(mg_act, CREDIT + n * 4 + (2 * (j // 2) + half + 1))
                            nc.vector.scalar_tensor_tensor(dst[:, s], tg[:, j // 2, s], 1.0,
                                                           bank[2 * j + half][:, 0:HALF], ALU.add, ALU.mult) \
                                .then_inc(mg_dve, 1)
                    dve.wait_ge(mg_dve, CREDIT + n * 4 + 4)
                    nc.vector.tensor_tensor(mT[:, bass.ds(n, 1), :], m1[:, :].rearrange("p (o c) -> p o c", o=1),
                                            m2[:, :].rearrange("p (o c) -> p o c", o=1), ALU.add).then_inc(merged, 1)
    st3.close()
    mid.close()

    w13 = [sb(f"w13_{i}", [P, 2, KT, FE]) for i in range(2)]
    w2b = [sb(f"w2_{i}", [P, FE // P, D]) for i in range(2)]
    wgt = sb("wgt", [P, 2, TT])
    slot = sb("slot", [P, 2, TT], I32)
    ovc = sb("ovc", [1, NE], I32)
    ovp = sb("ovp", [1, NE + 1], I32)
    w13_in = [sem(f"w13_in{i}") for i in range(2)]
    w2_in = [sem(f"w2_in{i}") for i in range(2)]

    w1s = A["w1"][0].rearrange("e (k p) f -> e p k f", p=P)
    w3s = A["w3"][0].rearrange("e (k p) f -> e p k f", p=P)
    w2s = A["w2"][0].rearrange("e (k p) n -> e p k n", p=P)

    def load13(eng, e, par, s):
        for j, src in enumerate((w1s, w3s)):
            eng.dma_start(w13[par][:, j, :, :], src[bass.ds(e, 1)].rearrange("o p k f -> p (o k) f")).then_inc(s, 16)

    def load2(eng, e, par, s):
        eng.dma_start(w2b[par][:, :, :], w2s[bass.ds(e, 1)].rearrange("o p k n -> p (o k) n")).then_inc(s, 16)

    st4 = ExitStack()
    g2 = sb("g2", [P, D], ctx=st4)
    xn2 = [sb(f"xn2_{i}", [P, D], ctx=st4) for i in range(2)]
    xn2T = sb("xn2T", [P, KT, P], ctx=st4)
    sq4 = sb("sq4", [P, 512], ctx=st4)
    wr = sb("wr", [P, KT, NG + NE], ctx=st4)
    rb = sb("rb", [P, NG + NE], ctx=st4)
    lg = sb("lg", [P, TT, NG + NE], ctx=st4)
    ss4 = sb("ss4", [P, 4, TT], ctx=st4)
    sm = sb("sm", [P, TT, 64], ctx=st4)
    oh = sb("oh", [P, 3, TT, NE], ctx=st4)
    rk = sb("rk", [P, 3, TT, NE], ctx=st4)
    ex = sb("ex", [P, 8, NE], ctx=st4)
    toki = sb("toki", [P, TT], I32, ctx=st4)
    r_in, mo_done, x2_ready = sem("r_in"), sem("mo_done"), sem("x2_ready")
    ss_ready, root4, rec4, xn2_ready = sem("ss_ready"), sem("root4"), sem("rec4"), sem("xn2_ready")
    xn2_stored = [sem(f"xn2_stored{i}") for i in range(2)]
    x2t_done, x2t_out, rt_done, rt_out = sem("x2t_done"), sem("x2t_out"), sem("rt_done"), sem("rt_out")
    gl_ready, ge_ready, ranks_done, oh_ready = sem("gl_ready"), sem("ge_ready"), sem("ranks_done"), sem("oh_ready")
    slots_ready, scattered, dve4, act4 = sem("slots_ready"), sem("scattered"), sem("dve4"), sem("act4")

    with nc.Block() as block:
        @block.sync
        def _(sp_):
            sp_.dma_start(g2[:, :], A["norm2_g"].to_broadcast([P, D])).then_inc(r_in, 16)
            sp_.dma_start(wr[:, :, 0:NG], A["w_group"][0].rearrange("(k p) n -> p k n", p=P)).then_inc(r_in, 16)
            sp_.dma_start(wr[:, :, NG:], A["w_router"][0].rearrange("(k p) n -> p k n", p=P)).then_inc(r_in, 16)
            sp_.dma_start(rb[:, 0:NG], A["b_group"].to_broadcast([P, NG])).then_inc(r_in, 16)
            sp_.dma_start(rb[:, NG:], A["b_router"].to_broadcast([P, NE])).then_inc(r_in, 16)
            for e in range(2):
                load13(sp_, e, e, w13_in[e])
                load2(sp_, e, e, w2_in[e])
            for t in range(TT):
                sp_.wait_ge(xn2_ready, t + 1)
                sp_.dma_start(xn2_d[t * P:(t + 1) * P, :], xn2[t % 2][:, :]).then_inc(xn2_stored[t % 2], 16)
            sp_.wait_ge(xn2_stored[0], 48)
            sp_.wait_ge(xn2_stored[1], 32)

        @block.gpsimd
        def _(pool):
            pool.wait_ge(slots_ready, 1)
            for t in range(TT):
                for k in range(2):
                    pool.indirect_dma_start(idx_d, bass.IndirectOffsetOnAxis(ap=slot[:, k, t:t + 1], axis=0),
                                            toki[:, t:t + 1], None).then_inc(scattered, 16)
            pool.wait_ge(scattered, 16 * 2 * TT)

        @block.tensor
        def _(pe):
            pe.wait_ge(x2_in, 16 * TT)
            pe.wait_ge(wo_in, 16)

            def route(t):
                pe.wait_ge(xn2_ready, t + 1)
                if t >= 1:
                    pe.wait_ge(x2t_out, 2 * t)
                for half in range(2):
                    for k in range(4):
                        c = (4 * half + k) * P
                        mm = nc.tensor.transpose(bank[4 + half][:, k * P:(k + 1) * P], xn2[t % 2][:, c:c + P], ident)
                    mm.then_inc(x2t_done, 1)
                pe.wait_ge(x2t_out, 2 * t + 2)
                for k in range(KT):
                    mm = nc.tensor.matmul(bank[6][:, t * 32:t * 32 + NG + NE], xn2T[:, k, :], wr[:, k, :],
                                          start=(k == 0), stop=(k == KT - 1))
                mm.then_inc(rt_done, 1)

            pe.wait_ge(r_in, 80)
            for t in range(TT):
                for half in range(2):
                    u = 2 * t + half
                    if u >= 4:
                        pe.wait_ge(x2_ready, u - 3)
                    for k in range(KT):
                        mm = nc.tensor.matmul(bank[u % 4][:, :], mT[:, k, t * P:(t + 1) * P],
                                              wo[:, k, half * 512:(half + 1) * 512],
                                              start=(k == 0), stop=(k == KT - 1))
                    mm.then_inc(mo_done, 1)
                if t >= 1:
                    route(t - 1)
            route(TT - 1)
            pe.wait_ge(oh_ready, 1)
            for t in range(TT):
                for s in range(t + 1):
                    nc.tensor.matmul(bank[7][:, t * NE:(t + 1) * NE], ones if s < t else cst[:, K_TRI:K_TRI + P],
                                     oh[:, 2, s, :], start=(s == 0), stop=(s == t))
            for s in range(TT):
                mm = nc.tensor.matmul(bank[7][:, TT * NE:(TT + 1) * NE], ones, oh[:, 2, s, :],
                                      start=(s == 0), stop=(s == TT - 1))
            mm.then_inc(ranks_done, 1)

        @block.scalar
        def _(act):
            for t in range(TT):
                act.wait_ge(x2_ready, 2 * t + 2)
                if t >= 1:
                    act.wait_ge(act4, t)
                for half in range(2):
                    ins = nc.scalar.activation(sq4[:, :], x2[:, t, half * 512:(half + 1) * 512], ACT.Square,
                                               accum_out=ss4[:, half, t:t + 1])
                    ins.then_inc(act4, 1) if half else ins.then_inc(ss_ready, 1)
                    if half == 0:
                        act.wait_ge(ss_ready, 2 * t + 1)
                act.wait_ge(act4, t + 1)
                nc.scalar.activation(ss4[:, 2, t:t + 1], ss4[:, 0, t:t + 1], ACT.Identity,
                                     bias=ss4[:, 1, t:t + 1]).then_inc(ss_ready, 1)
                act.wait_ge(ss_ready, 2 * t + 2)
                nc.scalar.activation(ss4[:, 3, t:t + 1], ss4[:, 2, t:t + 1], ACT.Sqrt, scale=1.0 / D,
                                     bias=eps_t[:, 0:1]).then_inc(root4, 1)
                act.wait_ge(x2t_done, 2 * t + 1)
                if t >= 1:
                    act.wait_ge(rt_done, t)
                nc.scalar.activation(xn2T[:, 0:4, :].rearrange("p k q -> p (k q)"), bank[4][:, :], ACT.Copy) \
                    .then_inc(x2t_out, 1)
                act.wait_ge(x2t_done, 2 * t + 2)
                nc.scalar.activation(xn2T[:, 4:8, :].rearrange("p k q -> p (k q)"), bank[5][:, :], ACT.Copy) \
                    .then_inc(x2t_out, 1)
            act.wait_ge(gl_ready, 1)
            nc.scalar.activation(sm[:, :, 8:13], sm[:, :, 0:5], ACT.Exp).then_inc(ge_ready, 1)

        @block.vector
        def _(dve):
            chain = Chain(dve, dve4)
            dve.wait_ge(r_in, 80)
            for t in range(TT):
                for half in range(2):
                    u = 2 * t + half
                    s = slice(half * 512, (half + 1) * 512)
                    dve.wait_ge(mo_done, u + 1)
                    nc.vector.scalar_tensor_tensor(x2[:, t, s], bank[u % 4][:, :], 0.5, x2[:, t, s],
                                                   ALU.mult, ALU.add).then_inc(x2_ready, 1)
                dve.wait_ge(root4, t + 1)
                chain(nc.vector.reciprocal(ss4[:, 2, t:t + 1], ss4[:, 3, t:t + 1]))
                if t >= 2:
                    dve.wait_ge(xn2_stored[t % 2], 16 * (t // 2))
                nc.vector.scalar_tensor_tensor(xn2[t % 2][:, :], x2[:, t, :], ss4[:, 2, t:t + 1], g2[:, :],
                                               ALU.mult, ALU.mult).then_inc(xn2_ready, 1)
            dve.wait_ge(rt_done, TT)
            chain(nc.vector.tensor_tensor(
                lg[:, :, :], bank[6][:, 0:TT * 32].rearrange("p (t c) -> p t c", c=32)[:, :, 0:NG + NE],
                rb[:, :].rearrange("p (o c) -> p o c", o=1).to_broadcast([P, TT, NG + NE]), ALU.add))

            def col(i, n=1):
                return sm[:, :, i:i + n]

            def tt(out, a, b, op):
                chain(nc.vector.tensor_tensor(out, a, b, op))

            def ts(out, a, s1, s2, op0, op1=None):
                if op1 is None:
                    chain(nc.vector.tensor_scalar(out, a, s1, None, op0))
                else:
                    chain(nc.vector.tensor_scalar(out, a, s1, s2, op0, op1))

            def first_max(src, top_, hot, t0):
                chain(nc.vector.tensor_reduce(top_, src, AX.X, ALU.max))
                tt(hot, src, top_.to_broadcast([P, TT, 4]), ALU.is_equal)
                seen = col(t0)
                ts(seen, hot[:, :, 0:1], -1.0, 1.0, ALU.mult, ALU.add)
                for j in range(1, 4):
                    tt(hot[:, :, j:j + 1], hot[:, :, j:j + 1], seen, ALU.mult)
                    if j < 3:
                        tt(seen, seen, hot[:, :, j:j + 1], ALU.subtract)

            gmax, ghot, ein, e1, f1, em, e2, f2 = col(16), col(20, 4), col(24, 4), col(28), col(32, 4), col(36, 4), \
                col(40), col(44, 4)
            first_max(lg[:, :, 0:NG], gmax, ghot, 17)
            tt(col(0, 4), lg[:, :, 0:NG], gmax.to_broadcast([P, TT, 4]), ALU.subtract)
            tt(ein, lg[:, :, NG:NG + EG], ghot[:, :, 0:1].to_broadcast([P, TT, EG]), ALU.mult)
            for g in range(1, NG):
                tt(col(48, 4), lg[:, :, NG + g * EG:NG + (g + 1) * EG],
                   ghot[:, :, g:g + 1].to_broadcast([P, TT, EG]), ALU.mult)
                tt(ein, ein, col(48, 4), ALU.add)
            first_max(ein, e1, f1, 18)
            ts(col(48, 4), f1, -1.0, 1.0, ALU.mult, ALU.add)
            tt(em, ein, col(48, 4), ALU.mult)
            ts(col(52, 4), f1, -BIG, None, ALU.mult)
            tt(em, em, col(52, 4), ALU.add)
            first_max(em, e2, f2, 19)
            nc.vector.tensor_tensor(col(4), e2, e1, ALU.subtract).then_inc(gl_ready, 1)
            for g in range(NG):
                for k, f in enumerate((f1, f2)):
                    ins = nc.vector.tensor_tensor(oh[:, k, :, g * EG:(g + 1) * EG], f,
                                                  ghot[:, :, g:g + 1].to_broadcast([P, TT, EG]), ALU.mult)
            chain(ins)
            nc.vector.tensor_tensor(oh[:, 2, :, :], oh[:, 0, :, :], oh[:, 1, :, :], ALU.add).then_inc(oh_ready, 1)
            dve.wait_ge(ge_ready, 1)
            chain(nc.vector.tensor_reduce(col(56), col(8, 4), AX.X, ALU.add))
            ts(col(57), col(12), 1.0, None, ALU.add)
            tt(col(56), col(56), col(57), ALU.mult)
            chain(nc.vector.reciprocal(col(58), col(56)))
            ts(wgt[:, 0, :], sm[:, :, 58], 1.0, None, ALU.mult)
            tt(wgt[:, 1, :], sm[:, :, 58], sm[:, :, 12], ALU.mult)
            dve.wait_ge(ranks_done, 1)
            cnt, ov, pre, tmp = (ex[:, i, :] for i in range(4))
            chain(nc.vector.tensor_copy(cnt, bank[7][:, TT * NE:(TT + 1) * NE]))
            ts(ov, cnt, float(P), None, ALU.is_gt)
            for j in range(2, TT):
                ts(tmp, cnt, float(j * P), None, ALU.is_gt)
                tt(ov, ov, tmp, ALU.add)
            a, b = ex[:, 4, :], ex[:, 5, :]
            chain(nc.vector.tensor_copy(a, ov))
            for d in (1, 2, 4, 8):
                chain(nc.vector.tensor_copy(b[:, 0:d], a[:, 0:d]))
                tt(b[:, d:], a[:, d:], a[:, 0:NE - d], ALU.add)
                a, b = b, a
            tt(pre, a, ov, ALU.subtract)
            incl = a
            r, q, z = rk[:, 0, :, :], rk[:, 1, :, :], rk[:, 2, :, :]
            chain(nc.vector.tensor_copy(r, bank[7][:, 0:TT * NE].rearrange("p (t e) -> p t e", e=NE)))
            ts(q, r, float(P), None, ALU.is_ge)
            for j in range(2, TT):
                ts(z, r, float(j * P), None, ALU.is_ge)
                tt(q, q, z, ALU.add)
            chain(nc.vector.scalar_tensor_tensor(r, q, -float(P), r, ALU.mult, ALU.add))
            ts(z, q, 0.0, None, ALU.is_gt)
            ts(tmp, pre, float(NE - 1), None, ALU.add)
            tt(tmp, tmp, cst[:, K_EID:K_EID + NE], ALU.subtract)

            def per_expert(x):
                return x.rearrange("p (o e) -> p o e", o=1).to_broadcast([P, TT, NE])

            tt(q, q, per_expert(tmp), ALU.add)
            tt(q, q, z, ALU.mult)
            tt(q, q, per_expert(cst[:, K_EID:K_EID + NE]), ALU.add)
            chain(nc.vector.scalar_tensor_tensor(r, q, float(P), r, ALU.mult, ALU.add))
            for k in range(2):
                tt(z, r, oh[:, k, :, :], ALU.mult)
                chain(nc.vector.tensor_reduce(col(60 + k), z, AX.X, ALU.add))
                chain(nc.vector.tensor_copy(slot[:, k, :], sm[:, :, 60 + k]))
            chain(nc.vector.tensor_copy(ovc[:, :], ov[0:1]))
            chain(nc.vector.tensor_copy(ovp[:, 0:NE], pre[0:1]))
            chain(nc.vector.tensor_copy(ovp[:, NE:], incl[0:1, NE - 1:NE]))
            chain(nc.vector.tensor_copy(toki[:, :], cst[:, K_TOK:K_TOK + TT]))
            nc.vector.memset(ex[:, 7, :], 0.0).then_inc(slots_ready, 1)
    st4.close()
    late.close()

    gf = sb("gf", [P, D])
    st5 = ExitStack()
    gf_in = sem("gf_in")
    passed = sem("passed")
    held = [sem("held_ex"), sem("held_ov")]
    gate_set = sem("gate_set")
    gate = sb("gate", [P, 4], ctx=st5)

    class Blocks:
        def __init__(self, tag, pars):
            self.pars = pars
            self.idx = [sb(f"{tag}_idx{i}", [P, 1], I32, ctx=st5) for i in range(pars)]
            self.xg = [sbr(f"{tag}_xg{i}", [P, D], st5) for i in range(pars)]
            self.xeT = [sbr(f"{tag}_xeT{i}", [P, KT, P], st5) for i in range(pars)]
            self.th = sbr(f"{tag}_th", [P, FE], st5)
            self.gg = [sbr(f"{tag}_gg{i}", [P, FE], st5) for i in range(pars)]
            self.hT = sbr(f"{tag}_hT", [P, FE], st5)
            self.y = [sbr(f"{tag}_y{i}", [P, D], st5) for i in range(pars)]
            self.idx_in = [sem(f"{tag}_idx_in{i}") for i in range(pars)]
            self.xg_in = [sem(f"{tag}_xg_in{i}") for i in range(pars)]
            self.y_stored = [sem(f"{tag}_y_stored{i}") for i in range(pars)]
            self.xt_done = sem(f"{tag}_xt_done")
            self.xt_act = sem(f"{tag}_xt_act")
            self.xt_dve = sem(f"{tag}_xt_dve")
            self.h_done = sem(f"{tag}_h_done")
            self.th_ready = sem(f"{tag}_th_ready")
            self.s_ready = sem(f"{tag}_s_ready")
            self.gg_ready = sem(f"{tag}_gg_ready")
            self.ht_done = sem(f"{tag}_ht_done")
            self.ht_out = sem(f"{tag}_ht_out")
            self.y_done = sem(f"{tag}_y_done")
            self.y_act = sem(f"{tag}_y_act")
            self.y_dve = sem(f"{tag}_y_dve")

    M, V = Blocks("ex", 2), Blocks("ov", 1)


    def pe_turn(pe, S, e, i, par):
        pe.wait_ge(S.xg_in[par], i * 16 + 16)
        pe.wait_ge(S.xt_act, CREDIT + e)
        pe.wait_ge(S.xt_dve, CREDIT + e)
        for half in range(2):
            for k in range(4):
                c = (4 * half + k) * P
                mm = nc.tensor.transpose(bank[half][:, k * P:(k + 1) * P], S.xg[par][:, c:c + P], ident)
        mm.then_inc(S.xt_done, 1)

    def pe_up(pe, S, e, i, par, wp):
        pe.wait_ge(S.gg_ready, CREDIT + e)
        pe.wait_ge(S.xt_act, CREDIT + e + 1)
        pe.wait_ge(S.xt_dve, CREDIT + e + 1)
        for j in range(2):
            for k in range(KT):
                mm = nc.tensor.matmul(bank[2 + j][:, :], S.xeT[par][:, k, :], w13[wp][:, j, k, :],
                                      start=(k == 0), stop=(k == KT - 1))
        mm.then_inc(S.h_done, 1)

    def pe_turn_h(pe, S, e, par):
        pe.wait_ge(S.gg_ready, CREDIT + e + 1)
        for k in range(FE // P):
            mm = nc.tensor.transpose(bank[4][:, k * P:(k + 1) * P], S.gg[par][:, k * P:(k + 1) * P], ident)
        mm.then_inc(S.ht_done, 1)

    def pe_down(pe, S, e, wp):
        pe.wait_ge(S.y_act, CREDIT + e)
        pe.wait_ge(S.y_dve, CREDIT + e)
        pe.wait_ge(S.ht_out, e + 1)
        for half in range(2):
            for k in range(FE // P):
                mm = nc.tensor.matmul(bank[5 + half][:, :], S.hT[:, k * P:(k + 1) * P],
                                      w2b[wp][:, k, half * 512:(half + 1) * 512],
                                      start=(k == 0), stop=(k == FE // P - 1))
        mm.then_inc(S.y_done, 1)

    def act_up(act, S, e, par):
        act.wait_ge(S.xt_done, CREDIT + e + 1)
        nc.scalar.activation(S.xeT[par][:, 0:4, :].rearrange("p k q -> p (k q)"), bank[0][:, :], ACT.Copy) \
            .then_inc(S.xt_act, 1)
        act.wait_ge(S.h_done, e + 1)
        act.wait_ge(S.s_ready, CREDIT + e)
        nc.scalar.activation(S.th[:, :], bank[2][:, :], ACT.Tanh, scale=0.5).then_inc(S.th_ready, 1)

    def act_down(act, S, e, i, par, row0):
        act.wait_ge(S.ht_done, e + 1)
        nc.scalar.activation(S.hT[:, :], bank[4][:, :], ACT.Copy).then_inc(S.ht_out, 1)
        act.wait_ge(S.y_stored[par], CREDIT + i * 16)
        act.wait_ge(S.y_done, CREDIT + e + 1)
        nc.scalar.activation(S.y[par][:, 0:512], bank[5][:, :], ACT.Copy).then_inc(S.y_act, 1)
        act.wait_ge(S.y_act, CREDIT + e + 1)
        act.wait_ge(S.y_dve, CREDIT + e + 1)
        act.dma_start(y_d[bass.ds(row0, P), :], S.y[par][:, :]).then_inc(S.y_stored[par], 16)

    def dve_up(dve, S, e, par):
        dve.wait_ge(S.xt_done, CREDIT + e + 1)
        nc.vector.tensor_copy(S.xeT[par][:, 4:8, :].rearrange("p k q -> p (k q)"), bank[1][:, :]) \
            .then_inc(S.xt_dve, 1)
        dve.wait_ge(S.th_ready, e + 1)
        nc.vector.scalar_tensor_tensor(S.gg[par][:, :], S.th[:, :], 1.0, bank[2][:, :], ALU.add, ALU.mult) \
            .then_inc(S.s_ready, 1)
        dve.wait_ge(S.s_ready, CREDIT + e + 1)
        nc.vector.scalar_tensor_tensor(S.gg[par][:, :], S.gg[par][:, :], 0.5, bank[3][:, :], ALU.mult, ALU.mult) \
            .then_inc(S.gg_ready, 1)

    def dve_down(dve, S, e, i, par):
        dve.wait_ge(S.y_stored[par], CREDIT + i * 16)
        dve.wait_ge(S.y_done, CREDIT + e + 1)
        nc.vector.tensor_copy(S.y[par][:, 512:D], bank[6][:, :]).then_inc(S.y_dve, 1)

    def each_overflow(eng, e, step):
        n = eng.value_load(ovc[0:1, bass.ds(e, 1)], min_val=0, max_val=TT - 1)
        with eng.If(n > 0):
            first = eng.value_load(ovp[0:1, bass.ds(e, 1)], min_val=0, max_val=OVMAX - 1)
            end = eng.value_load(ovp[0:1, bass.ds(e + 1, 1)], min_val=0, max_val=OVMAX)
            with eng.Fori(first, end) as j:
                step(j)

    def all_overflow(eng):
        return eng.value_load(ovp[0:1, NE:NE + 1], min_val=0, max_val=OVMAX)

    with nc.Block() as block:
        @block.sync
        def _(sp_):
            def load_idx(row0, dst, s):
                sp_.dma_start(dst[:, :], idx_d[bass.ds(row0, P), :]).then_inc(s, 16)

            def load_overflow_idx(j):
                sp_.wait_ge(V.xt_done, CREDIT + j)
                load_idx(j * P + NE * P, V.idx[0], V.idx_in[0])

            for e in range(2):
                load_idx(e * P, M.idx[e], M.idx_in[e])
            sp_.dma_start(gf[:, :], A["final_norm_g"].rearrange("(o d) -> o d", o=1).to_broadcast([P, D])) \
                .then_inc(gf_in, 16)
            each_overflow(sp_, 0, load_overflow_idx)
            with sp_.Fori(0, NE // 2 - 1) as i:
                for par in range(2):
                    e = i * 2 + (2 + par)
                    sp_.wait_ge(M.xg_in[par], i * 16 + 16)
                    load_idx(e * P, M.idx[par], M.idx_in[par])
                    each_overflow(sp_, i * 2 + (1 + par), load_overflow_idx)
                    sp_.wait_ge(passed, i * 2 + (1 + par))
                    load13(sp_, e, par, w13_in[par])
                    sp_.wait_ge(M.y_done, CREDIT + i * 2 + (1 + par))
                    load2(sp_, e, par, w2_in[par])
            each_overflow(sp_, NE - 1, load_overflow_idx)

        @block.gpsimd
        def _(pool):
            for S in (M, V):
                for s in (S.xt_act, S.xt_dve, S.gg_ready, S.s_ready, S.y_act, S.y_dve, S.xt_done, S.y_done,
                          *S.y_stored):
                    pool.sem_inc(s, CREDIT)
            for s in held:
                pool.sem_inc(s, CREDIT)
            nc.gpsimd.memset(gate[:, 0:1], 0.0).then_inc(gate_set, 1)
            pool.wait_ge(gate_set, 1)

            def gather(S, par):
                pool.indirect_dma_start(S.xg[par][:, :], None, xn2_d,
                                        bass.IndirectOffsetOnAxis(ap=S.idx[par][:, 0:1], axis=0)) \
                    .then_inc(S.xg_in[par], 16)

            def hold_waits(s, n):
                pool.wait_ge(held[s], CREDIT + n)
                nc.gpsimd.tensor_tensor(gate[:, s + 1:s + 2], gate[:, 0:1], gate[:, 0:1], ALU.add) \
                    .then_inc(held[s], 1)

            def gather_overflow(j):
                pool.wait_ge(V.xt_done, CREDIT + j)
                pool.wait_ge(V.idx_in[0], j * 16 + 16)
                hold_waits(1, j)
                gather(V, 0)

            for e in range(2):
                pool.wait_ge(M.idx_in[e], 16)
                gather(M, e)
            with pool.Fori(0, NE // 2 - 1) as i:
                for par in range(2):
                    each_overflow(pool, i * 2 + par, gather_overflow)
                    pool.wait_ge(M.xt_done, CREDIT + i * 2 + (1 + par))
                    pool.wait_ge(M.idx_in[par], i * 16 + 32)
                    hold_waits(0, i * 2 + par)
                    gather(M, par)
            for e in (NE - 2, NE - 1):
                each_overflow(pool, e, gather_overflow)

        @block.tensor
        def _(pe):
            def up(e, i, par):
                pe_turn(pe, M, e, i, par)
                pe.wait_ge(w13_in[par], i * 32 + 32)
                pe_up(pe, M, e, i, par, par)

                def overflow(j):
                    pe.wait_ge(w2_in[par], i * 16 + 16)
                    pe.wait_ge(M.gg_ready, CREDIT + e + 1)
                    pe.wait_ge(M.y_act, e - 1 + CREDIT)
                    pe.wait_ge(M.y_dve, e - 1 + CREDIT)
                    pe_turn(pe, V, j, j, 0)
                    pe_up(pe, V, j, j, 0, par)
                    pe_turn_h(pe, V, j, 0)
                    pe_down(pe, V, j, par)
                    pe.wait_ge(V.y_act, CREDIT + j + 1)
                    pe.wait_ge(V.y_dve, CREDIT + j + 1)
                each_overflow(pe, e, overflow)
                nc.tensor.matmul(bank[7][:, 0:2], ident, cst[:, 0:2], start=True, stop=True).then_inc(passed, 1)

            def down(e, i, par):
                pe_turn_h(pe, M, e, par)
                pe.wait_ge(w2_in[par], i * 16 + 16)
                pe_down(pe, M, e, par)

            up(0, 0, 0)
            up(1, 0, 1)
            down(0, 0, 0)
            with pe.Fori(1, NE // 2) as i:
                up(i * 2, i, 0)
                down(i * 2 - 1, i - 1, 1)
                up(i * 2 + 1, i, 1)
                down(i * 2, i, 0)
            down(NE - 1, NE // 2 - 1, 1)

        @block.scalar
        def _(act):
            def up(e, par):
                act_up(act, M, e, par)

                def overflow(j):
                    act_up(act, V, j, 0)
                    act_down(act, V, j, j, 0, j * P + NE * P)
                each_overflow(act, e, overflow)

            up(0, 0)
            up(1, 1)
            act_down(act, M, 0, 0, 0, 0)
            with act.Fori(1, NE // 2) as i:
                up(i * 2, 0)
                act_down(act, M, i * 2 - 1, i - 1, 1, i * (2 * P) - P)
                up(i * 2 + 1, 1)
                act_down(act, M, i * 2, i, 0, i * (2 * P))
            act_down(act, M, NE - 1, NE // 2 - 1, 1, (NE - 1) * P)
            for s in M.y_stored:
                act.wait_ge(s, CREDIT + 16 * (NE // 2))
            n = all_overflow(act)
            with act.If(n > 0):
                act.wait_ge(V.y_stored[0], CREDIT + n * 16)
                nc.scalar.activation(gate[:, 3:4], eps_t[:, 0:1], ACT.Copy)

        @block.vector
        def _(dve):
            def up(e, par):
                dve_up(dve, M, e, par)

                def overflow(j):
                    dve_up(dve, V, j, 0)
                    dve_down(dve, V, j, j, 0)
                each_overflow(dve, e, overflow)

            up(0, 0)
            up(1, 1)
            dve_down(dve, M, 0, 0, 0)
            with dve.Fori(1, NE // 2) as i:
                up(i * 2, 0)
                dve_down(dve, M, i * 2 - 1, i - 1, 1)
                up(i * 2 + 1, 1)
                dve_down(dve, M, i * 2, i, 0)
            dve_down(dve, M, NE - 1, NE // 2 - 1, 1)
    st5.close()

    st6 = ExitStack()
    yg = [sb(f"yg{i}", [P, 2, D], ctx=st6) for i in range(2)]
    sq6 = sb("sq6", [P, D], ctx=st6)
    yo = [sb(f"yo{i}", [P, D], ctx=st6) for i in range(2)]
    ss6 = sb("ss6", [P, 3, TT], ctx=st6)
    yg_in = [sem(f"yg_in{i}") for i in range(2)]
    yo_stored = [sem(f"yo_stored{i}") for i in range(2)]
    x3_ready, sq6_ready, root6, yo_ready, dve6 = sem("x3_ready"), sem("sq6_ready"), sem("root6"), sem("yo_ready"), sem("dve6")
    yp = O["y_prompt"].rearrange("b (t p) d -> p (b t) d", p=P)
    ysm = O["y_sample"].rearrange("b s d -> (b s) d")

    with nc.Block() as block:
        @block.gpsimd
        def _(pool):
            for t in range(TT):
                if t >= 2:
                    pool.wait_ge(x3_ready, t - 1)
                for k in range(2):
                    pool.indirect_dma_start(yg[t % 2][:, k, :], None, y_d,
                                            bass.IndirectOffsetOnAxis(ap=slot[:, k, t:t + 1], axis=0)) \
                        .then_inc(yg_in[t % 2], 16)

        @block.vector
        def _(dve):
            chain = Chain(dve, dve6)

            def scale_out(t):
                dve.wait_ge(root6, t + 1)
                chain(nc.vector.reciprocal(ss6[:, 2, t:t + 1], ss6[:, 1, t:t + 1]))
                if t >= 2:
                    dve.wait_ge(yo_stored[t % 2], 16 * (t // 2))
                nc.vector.scalar_tensor_tensor(yo[t % 2][:, :], x2[:, t, :], ss6[:, 2, t:t + 1], gf[:, :],
                                               ALU.mult, ALU.mult).then_inc(yo_ready, 1)

            for t in range(TT):
                dve.wait_ge(yg_in[t % 2], 32 * (t // 2 + 1))
                chain(nc.vector.scalar_tensor_tensor(x2[:, t, :], yg[t % 2][:, 0, :], wgt[:, 0, t:t + 1],
                                                     x2[:, t, :], ALU.mult, ALU.add))
                nc.vector.scalar_tensor_tensor(x2[:, t, :], yg[t % 2][:, 1, :], wgt[:, 1, t:t + 1],
                                               x2[:, t, :], ALU.mult, ALU.add).then_inc(x3_ready, 1)
                if t >= 1:
                    scale_out(t - 1)
            scale_out(TT - 1)

        @block.scalar
        def _(act):
            for t in range(TT):
                act.wait_ge(x3_ready, t + 1)
                nc.scalar.activation(sq6[:, :], x2[:, t, :], ACT.Square, accum_out=ss6[:, 0, t:t + 1]) \
                    .then_inc(sq6_ready, 1)
                act.wait_ge(sq6_ready, t + 1)
                nc.scalar.activation(ss6[:, 1, t:t + 1], ss6[:, 0, t:t + 1], ACT.Sqrt, scale=1.0 / D,
                                     bias=eps_t[:, 0:1]).then_inc(root6, 1)

        @block.sync
        def _(sp_):
            sp_.wait_ge(gf_in, 16)
            for t in range(TT):
                sp_.wait_ge(yo_ready, t + 1)
                sp_.dma_start(yp[:, t, :] if t < NQ else ysm, yo[t % 2][:, :]).then_inc(yo_stored[t % 2], 16)
            sp_.wait_ge(yo_stored[0], 48)
            sp_.wait_ge(yo_stored[1], 32)
    st6.close()


_INS = ["x_prompt", "x_sample", "cache_k", "cache_v", "state_conv", "state_rnn", "norm1_g", "w_in",
        "lambda_q1", "lambda_k1", "lambda_q2", "lambda_k2", "subln_g", "w_attn_proj", "conv_w", "conv_b",
        "w_rg_a", "b_rg_a", "w_rg_i", "b_rg_i", "rg_lambda", "w_rnn_proj", "b_gate", "w_out", "norm2_g",
        "w_group", "b_group", "w_router", "b_router", "w1", "w3", "w2", "final_norm_g"]
_OUTS = [("y_prompt", (1, SEQ, D)), ("y_sample", (NS, DS, D)),
         ("new_k_prompt", (1, 1, SEQ, H, 2, DH)), ("new_v_prompt", (1, 1, SEQ, H, DV)),
         ("new_conv_prompt", (1, 1, CW - 1, D)), ("new_rnn_prompt", (1, 1, D)),
         ("new_k_sample", (1, NS, DS, H, 2, DH)), ("new_v_sample", (1, NS, DS, H, DV)),
         ("new_conv_sample", (1, NS, CW - 1, D)), ("new_rnn_sample", (1, NS, D))]


def kernel(**inputs):
    import concourse.bacc as bacc
    from concourse.bass_utils import run_bass_kernel_spmd

    nc = bacc.Bacc("TRN2", target_bir_lowering=False, num_devices=1)
    arrays = {name: np.ascontiguousarray(inputs[name]) for name in _INS}
    arrays["shape_constants"] = shape_constants()
    A = {n: nc.dram_tensor(f"in_{n}", a.shape, mybir.dt.from_np(a.dtype), kind="ExternalInput").ap()
         for n, a in arrays.items()}
    O = {n: nc.dram_tensor(f"out_{n}", s, F32, kind="ExternalOutput").ap() for n, s in _OUTS}
    build(nc, A, O)
    r = run_bass_kernel_spmd(nc, [{f"in_{n}": a for n, a in arrays.items()}], core_ids=[0])
    return tuple(r.results[0][f"out_{n}"] for n, _ in _OUTS)
```

```python
from contextlib import ExitStack

import numpy as np

import concourse.bass as bass
from concourse import mybir

F32 = mybir.dt.float32
I32 = mybir.dt.int32
F32R = mybir.dt.float32r
ACT = mybir.ActivationFunctionType
ALU = mybir.AluOpType
AX = mybir.AxisListType

P = 128
D = 1024
KT = D // P
SEQ, NS, DS, PAST = 512, 8, 16, 256
NQ = SEQ // P
TOK = SEQ + NS * DS
TT = TOK // P
HALF = TOK // 2
H, DH, DV = 8, 64, 128
CW = 4
NG, EG = 4, 4
NE = NG * EG
FE = 512
EPS = 1e-6
LAM0 = 0.8 - 0.6
SCALE = DH ** -0.5
BIG = float(2 ** 100)
KNEW = PAST
SKEYS = PAST + P
NSEL = 2 * TOK
OVMAX = (NSEL - NE) // P
NBLK = NE + OVMAX
CREDIT = 1
GELU_C = float(np.sqrt(2.0 / np.pi))

R_CW, R_CB, R_BA, R_BI, R_LAM, R_GA, R_GR, R_N1 = 0, 4, 5, 6, 7, 8, 9, 10
NROW = 11
C_SP2 = 11
NCOL = 12

K_ID, K_ONE, K_TRI, K_SEL, K_M0, K_M1, K_MASKQ, K_MASKV, K_IND, K_MST, K_EID, K_TOK = (
    0, 128, 256, 384, 448, 449, 450, 578, 642, 898, 1026, 1042)
NK = K_TOK + TT


def shape_constants():
    c = np.zeros((P, NK), np.float32)
    p = np.arange(P)
    c[:, K_ID:K_ID + P] = np.eye(P)
    c[:, K_ONE:K_ONE + P] = 1.0
    c[:, K_TRI:K_TRI + P] = p[:, None] < p[None, :]
    b4, m, q = p // 32, (p // 16) % 2, p % 16
    c[p, K_SEL + b4 * 16 + q] = 1.0
    c[:, K_M0] = m == 0
    c[:, K_M1] = m == 1
    c[0, K_MASKQ:K_MASKQ + 64] = 1.0
    c[0, K_MASKV:K_MASKV + 64] = -BIG
    for g in range(2):
        for r in range(P):
            c[4 * g + b4[r], K_IND + g * P + r] = 1.0
    for b in range(NS):
        c[b, K_MST:K_MST + P] = np.where(p // DS == b, 0.0, -BIG)
    c[:, K_EID:K_EID + NE] = np.arange(NE)
    c[:, K_TOK:K_TOK + TT] = p[:, None] + P * np.arange(TT)
    return c


class Chain:

    def __init__(self, eng, sem, start=0):
        self.eng, self.sem, self.base, self.n = eng, sem, start, 0

    def at(self, base):
        self.base, self.n = base, 0

    def __call__(self, ins):
        self.n += 1
        ins.then_inc(self.sem, 1)
        self.eng.wait_ge(self.sem, self.base + self.n)


def build(nc, A, O):
    top = ExitStack()
    with top:
        def sb(name, shape, dt=F32, ctx=top):
            return ctx.enter_context(nc.sbuf_tensor(name, shape, dt))

        def sem(name):
            return top.enter_context(nc.semaphore(name))

        bank = [top.enter_context(nc.psum_tensor(f"bank{i}", [P, 512], F32)) for i in range(8)]
        cst = sb("cst", [P, NK])
        ident = cst[:, K_ID:K_ID + P]
        ones = cst[:, K_ONE:K_ONE + P]
        pcol = sb("pcol", [P, KT, NCOL])
        scol = sb("scol", [P, KT, 32])
        subln = sb("subln", [P, 1])
        lam = sb("lam", [P, 8])
        neglam, msign = lam[:, 0:1], lam[:, 1:2]
        eps_t = sb("eps_t", [P, 1])

        xn2_d = nc.dram_tensor("xn2_scratch", (TOK, D), F32, kind="Internal").ap()
        idx_d = nc.dram_tensor("block_tokens", ((NBLK + 3) * P, 1), I32, kind="Internal").ap()
        y_d = nc.dram_tensor("block_outputs", ((NBLK + 1) * P, D), F32, kind="Internal").ap()

        xp = A["x_prompt"].rearrange("b (t p) d -> p (b t) d", p=P)
        xs = A["x_sample"].rearrange("b s d -> (b s) d")

        on = sb("on", [P, H, NQ, DV])
        mid = ExitStack()
        xh = sb("xh", [P, KT, TOK], F32R, ctx=mid)
        xl = sb("xl", [P, KT, TOK], F32R, ctx=mid)
        early = ExitStack()

        def sbe(name, shape, dt=F32):
            return early.enter_context(nc.sbuf_tensor(name, shape, dt, side="right"))

        raw = [sbe(f"raw{i}", [P, KT, P]) for i in range(2)]
        wh = sbe("wh", [P, KT, 5, P], F32R)
        wl = sbe("wl", [P, KT, 5, P], F32R)
        zcol = sbe("zcol", [P, 1])
        raw_in = [sem(f"raw_in{i}") for i in range(2)]
        highs, split, zcol_set = sem("highs"), sem("split"), sem("zcol_set")
        Q, K, V, XR, GR = range(5)
        ORDER = ((K, 0), (V, 0), (Q, 0), (XR, 0), (GR, 0), (K, 1), (V, 1), (Q, 1))
        EARLY = 3
        w_cols = A["w_in"][0].rearrange("(k p) n -> p k n", p=P)

        def need(eng, s, n):
            if not (isinstance(n, int) and n <= 0):
                eng.wait_ge(s, n)

        def load_tile(eng, n_static, n, j, h):
            refill(eng, raw_in[n_static % 2], split, n - 1)
            eng.dma_start(raw[n_static % 2][:, :, :], w_cols[:, :, j * D:][:, :, bass.ds(h * P, P)]) \
                .then_inc(raw_in[n_static % 2], 16)

        def refill(eng, arrived, s, n):
            if not isinstance(n, int):
                n = nc.snap(n)
                eng.wait_ge(arrived, 16)
            need(eng, s, n)

        def split_tile(pool, n_static, n, c, j):
            r = raw[n_static % 2]
            pool.wait_ge(raw_in[n_static % 2], c * 16)
            nc.gpsimd.tensor_tensor(wh[:, :, j, :], r[:, :, :], zcol[:, 0:1].rearrange("p (a b) -> p a b", a=1)
                                    .to_broadcast([P, KT, P]), ALU.add).then_inc(highs, 1)
            pool.wait_ge(highs, n + 1)
            nc.gpsimd.tensor_tensor(wl[:, :, j, :], r[:, :, :], wh[:, :, j, :].bitcast(F32), ALU.subtract) \
                .then_inc(split, 1)

        st1 = ExitStack()
        xt = sb("xt", [P, TT, D], ctx=st1)
        xn = sb("xn", [P, TT, D], ctx=st1)
        xnT = sb("xnT", [P, KT, TOK], ctx=st1)
        prow = sb("prow", [NROW, D], ctx=st1)
        srow = sb("srow", [32, D], ctx=st1)
        lvec = sb("lvec", [P, 4, DH], ctx=st1)
        ljunk = sb("ljunk", [P, 2, DH], ctx=st1)
        lsum = sb("lsum", [P, 4], ctx=st1)
        sq1 = sb("sq1", [P, D], ctx=st1)
        ss1 = sb("ss1", [P, 2, TT], ctx=st1)
        sp = sb("sp", [P, 6, KT], ctx=st1)
        zidx = sb("zidx", [NBLK + 3, P], I32, ctx=st1)

        cst_in, rows_in, lam_in = sem("cst_in"), sem("rows_in"), sem("lam_in")
        x_in = [sem(f"x_in{t}") for t in range(TT)]
        idx_zeroed, zidx_set = sem("idx_zeroed"), sem("zidx_set")
        eps_set, squares, roots1 = sem("eps_set"), sem("squares"), sem("roots1")
        xn_ready, cols_turned, cols_out = sem("xn_ready"), sem("cols_turned"), sem("cols_out")
        xn_turned, xnT_out, xh_ready = sem("xn_turned"), sem("xnT_out"), sem("xh_ready")
        lam_dots, lam_exps, sp_in, sp_exp = sem("lam_dots"), sem("lam_exps"), sem("sp_in"), sem("sp_exp")
        dve1, act1 = sem("dve1"), sem("act1")

        def part(x, u):
            return x[:, 4 * (u % 2):4 * (u % 2) + 4, u // 2 * P:(u // 2 + 1) * P]

        with nc.Block() as block:
            @block.sync
            def _(sp_):
                sp_.dma_start(cst[:, :], A["shape_constants"]).then_inc(cst_in, 16)
                for r, n, src in ((R_CW, 4, A["conv_w"][0]), (R_CB, 1, A["conv_b"]), (R_BA, 1, A["b_rg_a"]),
                                  (R_BI, 1, A["b_rg_i"]), (R_LAM, 1, A["rg_lambda"]),
                                  (R_GA, 2, A["b_gate"].rearrange("l (g d) -> (l g) d", g=2)),
                                  (R_N1, 1, A["norm1_g"])):
                    sp_.dma_start(prow[r:r + n, :], src).then_inc(rows_in, 16)
                sp_.dma_start(srow[0:24, :], A["state_conv"].rearrange("l b w d -> (l b w) d")).then_inc(rows_in, 16)
                sp_.dma_start(srow[24:32, :], A["state_rnn"][0]).then_inc(rows_in, 16)
                for i, n in enumerate(("lambda_q1", "lambda_k1", "lambda_q2", "lambda_k2")):
                    sp_.dma_start(lvec[:, i, :], A[n].to_broadcast([P, DH])).then_inc(lam_in, 16)
                sp_.dma_start(subln[:, :], A["subln_g"].rearrange("l d -> d l")).then_inc(lam_in, 16)
                for t in range(TT):
                    src = xp[:, t, :] if t < NQ else xs
                    sp_.dma_start(xt[:, t, :], src).then_inc(x_in[t], 16)
                for n, (j, h) in enumerate(ORDER[:EARLY + 1]):
                    load_tile(sp_, n, n, j, h)
                sp_.wait_ge(zidx_set, 1)
                sp_.dma_start(idx_d.rearrange("(b p) o -> b (p o)", p=P), zidx[:, :]).then_inc(idx_zeroed, 16)
                sp_.wait_ge(idx_zeroed, 16)

            @block.gpsimd
            def _(pool):
                nc.gpsimd.memset(zidx[:, :], 0).then_inc(zidx_set, 1)
                nc.gpsimd.memset(zcol[:, :], 0.0).then_inc(zcol_set, 1)
                pool.wait_ge(zcol_set, 1)
                for n, (j, _) in enumerate(ORDER[:EARLY]):
                    split_tile(pool, n, n, n // 2 + 1, j)

            @block.scalar
            def _(act):
                act.wait_ge(lam_dots, 2)
                nc.scalar.activation(lsum[:, 2:4], lsum[:, 0:2], ACT.Exp).then_inc(lam_exps, 1)
                act.wait_ge(sp_in, 1)
                nc.scalar.activation(sp[:, 1, :], sp[:, 0, :], ACT.Exp).then_inc(sp_exp, 1)
                for t in range(TT):
                    act.wait_ge(x_in[t], 16)
                    nc.scalar.activation(sq1[:, :], xt[:, t, :], ACT.Square, accum_out=ss1[:, 0, t:t + 1]) \
                        .then_inc(squares, 1)
                    act.wait_ge(squares, t + 1)
                act.wait_ge(eps_set, 1)
                nc.scalar.activation(ss1[:, 1, :], ss1[:, 0, :], ACT.Sqrt, scale=1.0 / D,
                                     bias=eps_t[:, 0:1]).then_inc(roots1, 1)
                for u in range(2 * TT):
                    act.wait_ge(xnT_out, u + 1)
                    nc.scalar.activation(part(xh, u), part(xnT, u), ACT.Copy).then_inc(xh_ready, 1)

            @block.vector
            def _(dve):
                chain = Chain(dve, dve1)
                nc.vector.memset(eps_t[:, :], EPS).then_inc(eps_set, 1)
                dve.wait_ge(cols_turned, 1)
                nc.vector.tensor_copy(pcol[:, :, 0:NROW],
                                      bank[0][:, 0:KT * 16].rearrange("p (k r) -> p k r", r=16)[:, :, 0:NROW]) \
                    .then_inc(cols_out, 1)
                nc.vector.tensor_copy(scol[:, :, :], bank[1][:, 0:KT * 32].rearrange("p (k r) -> p k r", r=32)) \
                    .then_inc(cols_out, 1)
                dve.wait_ge(cols_out, 2)
                dve.wait_ge(lam_in, 16 * 5)
                for i in range(2):
                    nc.vector.tensor_tensor_reduce(ljunk[:, i, :], lvec[:, 2 * i, :], lvec[:, 2 * i + 1, :], 1.0, 0.0,
                                                   ALU.mult, ALU.add, lsum[:, i:i + 1]).then_inc(lam_dots, 1)
                chain(nc.vector.tensor_scalar(sp[:, 2, :], pcol[:, :, R_LAM], -1.0, None, ALU.mult))
                nc.vector.tensor_tensor(sp[:, 0, :], sp[:, 2, :], pcol[:, :, R_LAM], ALU.min).then_inc(sp_in, 1)
                chain(nc.vector.tensor_scalar(sp[:, 2, :], sp[:, 2, :], 0.0, 2.0, ALU.max, ALU.mult))
                dve.wait_ge(sp_exp, 1)
                chain(nc.vector.tensor_scalar(sp[:, 3, :], sp[:, 1, :], 2.0, None, ALU.add))
                chain(nc.vector.reciprocal(sp[:, 3, :], sp[:, 3, :]))
                chain(nc.vector.tensor_tensor(sp[:, 3, :], sp[:, 3, :], sp[:, 1, :], ALU.mult))
                chain(nc.vector.tensor_tensor(sp[:, 4, :], sp[:, 3, :], sp[:, 3, :], ALU.mult))
                chain(nc.vector.tensor_scalar(sp[:, 5, :], sp[:, 4, :], 1.0 / 19, 1.0 / 17, ALU.mult, ALU.add))
                for n in range(15, 0, -2):
                    chain(nc.vector.tensor_tensor(sp[:, 5, :], sp[:, 5, :], sp[:, 4, :], ALU.mult))
                    chain(nc.vector.tensor_scalar(sp[:, 5, :], sp[:, 5, :], 1.0 / n, None, ALU.add))
                chain(nc.vector.tensor_tensor(sp[:, 5, :], sp[:, 5, :], sp[:, 3, :], ALU.mult))
                nc.vector.scalar_tensor_tensor(pcol[:, :, C_SP2], sp[:, 5, :], 4.0, sp[:, 2, :], ALU.mult, ALU.add)
                nc.vector.tensor_scalar(pcol[:, :, R_BA:R_BI + 1], pcol[:, :, R_BA:R_BI + 1], 0.5, None, ALU.mult)
                nc.vector.tensor_scalar(pcol[:, :, R_GA:R_GR + 1], pcol[:, :, R_GA:R_GR + 1], 0.5, None, ALU.mult)
                nc.vector.tensor_scalar(subln[:, :], subln[:, :], 1.0 - LAM0, None, ALU.mult)
                dve.wait_ge(lam_exps, 1)
                chain(nc.vector.tensor_tensor(neglam, lsum[:, 3:4], lsum[:, 2:3], ALU.subtract))
                chain(nc.vector.tensor_scalar(neglam, neglam, -LAM0, None, ALU.add))
                dve.wait_ge(cst_in, 16)
                chain(nc.vector.scalar_tensor_tensor(msign, cst[:, K_M1:K_M1 + 1], neglam, cst[:, K_M0:K_M0 + 1],
                                                     ALU.mult, ALU.add))
                dve.wait_ge(roots1, 1)
                chain(nc.vector.reciprocal(ss1[:, 0, :], ss1[:, 1, :]))
                for t in range(TT):
                    nc.vector.tensor_scalar(xn[:, t, :], xt[:, t, :], ss1[:, 0, t:t + 1], None, ALU.mult) \
                        .then_inc(xn_ready, 1)
                def low(u):
                    dve.wait_ge(xh_ready, u + 1)
                    nc.vector.tensor_tensor(part(xl, u), part(xnT, u), part(xh, u).bitcast(F32), ALU.subtract)

                for u in range(2 * TT):
                    half = u % 2
                    dve.wait_ge(xn_turned, u + 1)
                    nc.vector.tensor_tensor(
                        part(xnT, u), bank[2 + u % 4][:, :].rearrange("p (k q) -> p k q", q=P),
                        pcol[:, 4 * half:4 * half + 4, R_N1:R_N1 + 1].to_broadcast([P, 4, P]),
                        ALU.mult).then_inc(xnT_out, 1)
                    if u >= 1:
                        low(u - 1)
                low(2 * TT - 1)

            @block.tensor
            def _(pe):
                pe.wait_ge(cst_in, 16)
                pe.wait_ge(rows_in, 16 * 9)
                for k in range(KT):
                    nc.tensor.transpose(bank[0][:, 16 * k:16 * k + NROW], prow[:, k * P:(k + 1) * P],
                                        ident[0:NROW, 0:NROW])
                    last = nc.tensor.transpose(bank[1][:, 32 * k:32 * k + 32], srow[:, k * P:(k + 1) * P],
                                               ident[0:32, 0:32])
                last.then_inc(cols_turned, 1)
                for t in range(TT):
                    pe.wait_ge(xn_ready, t + 1)
                    for half in range(2):
                        u = 2 * t + half
                        if u >= 4:
                            pe.wait_ge(xnT_out, u - 3)
                        for k in range(4):
                            last = nc.tensor.transpose(bank[2 + u % 4][:, k * P:(k + 1) * P],
                                                       xn[:, t, (4 * half + k) * P:(4 * half + k + 1) * P], ident)
                        last.then_inc(xn_turned, 1)
        st1.close()

        yT = sb("yT", [P, KT, TOK], ctx=mid)
        oTs = sb("oTs", [P, H, P], ctx=mid)
        stc = sb("stc", [P, KT, 36], ctx=mid)
        st2 = ExitStack()
        wrg = [sb(f"wrg{i}", [P, 2, P], ctx=st2) for i in range(2)]
        kc = sb("kc", [P, NS * 2, P], ctx=st2)
        vc = sb("vc", [P, NS * 2, P], ctx=st2)
        hcol = [sb(f"hcol{i}", [P, NCOL + 32], ctx=st2) for i in range(2)]
        kvt = sb("kvt", [P, 3, TT, P], ctx=st2)
        qT = sb("qT", [P, TOK], ctx=st2)
        kT = sb("kT", [P, TOK], ctx=st2)
        qbd = sb("qbd", [P, NS, 2, DS], ctx=st2)
        ebuf = [sb(f"ebuf{i}", [P, 2, 512], ctx=st2) for i in range(2)]
        wT = [sb(f"wT{i}", [P, 512], ctx=st2) for i in range(2)]
        wTs = sb("wTs", [P, 3, P], ctx=st2)
        selc = sb("selc", [P, 2, 64], ctx=st2)
        stat = sb("stat", [P, 5, 10], ctx=st2)
        oraw = sb("oraw", [P, NQ, DV], ctx=st2)
        osq = ebuf[0][:, 1, :].rearrange("p (t c) -> p t c", c=DV)
        oms = sb("oms", [P, 4 * NQ], ctx=st2)
        xpad = sb("xpad", [P, 3 + SEQ], ctx=st2)
        spad = sb("spad", [P, NS, 3 + DS], ctx=st2)
        xc = sb("xc", [P, TOK], ctx=st2)
        thr = sb("thr", [P, TOK], ctx=st2)
        thi = sb("thi", [P, TOK], ctx=st2)
        gr = [sb(f"gr{i}", [P, TOK], ctx=st2) for i in range(2)]
        gw = sb("gw", [P, TOK], ctx=st2)
        ra = sb("ra", [P, TOK], ctx=st2)
        rw = sb("rw", [P, TOK], ctx=st2)
        rh = thr
        h0t = sb("h0t", [P, NS], ctx=st2)

        kc_in, vc_in = sem("kc_in"), sem("vc_in")
        col_in = [sem(f"col_in{i}") for i in range(2)]
        kv_stored = sem("kv_stored")
        pr_done, pr_act, pr_dve = sem("pr_done"), sem("pr_act"), sem("pr_dve")
        pt_done, pt_out = sem("pt_done"), sem("pt_out")
        ss_done, sc_done, max_ready, exp_done = sem("ss_done"), sem("sc_done"), sem("max_ready"), sem("exp_done")
        selc_ready, comb_ready = sem("selc_ready"), sem("comb_ready")
        os_done, os_out, op_done, op_out = sem("os_done"), sem("os_out"), sem("op_done"), sem("op_out")
        conv_done, gcube, gtanh = sem("conv_done"), sem("gcube"), sem("gtanh")
        decay, ms_ready, roots2, rnn_done = sem("decay"), sem("ms_ready"), sem("roots2"), sem("rnn_done")
        init2, dve2 = sem("init2"), sem("dve2")
        BODY_STEPS, TAIL_STEPS = 22, 10

        UNITS = ["xr0", "xr1", "kv0", "kv1", "kv2", "gr0", "gr1", "kv3", "ra0", "ra1", "ri0", "kv4", "ri1",
                 "q0", "q1", "kT0", "kT1", "kT2"]
        AHEAD = [u for u in UNITS if u[0] in "kq"]
        LAST = [u for u in UNITS if u[0] not in "kq"]
        RING = 3
        assert len(UNITS) % RING == 0
        NT = 9
        TILES = 5

        def by_act(units):
            return [u for u in units if u[:2] not in ("kv", "xr")]

        def by_dve(units):
            return [u for u in units if u[:2] in ("kv", "xr")]

        class Step:
            def __init__(self, i, h0, ahead=False):
                self.i, self.h0, self.par, self.h = i, h0, h0 % 2, i * 2 + h0
                self.first, self.last = isinstance(self.h, int) and self.h == 0, isinstance(self.h, int) and self.h == H - 1
                self.units = AHEAD if ahead else LAST if self.last else UNITS
                h = self.h
                self.u0 = 0 if ahead else h * len(UNITS) + len(AHEAD)
                self.a0 = 0 if ahead else h * len(by_act(UNITS)) + len(by_act(AHEAD))
                self.d0 = 0 if ahead else h * len(by_dve(UNITS)) + len(by_dve(AHEAD))
                self.before = [] if ahead else AHEAD if self.first else UNITS
                self.shift = 0 if ahead else len(AHEAD)

            def bank(self, name):
                return bank[(self.shift + self.units.index(name)) % RING]

            def done(self, eng, name):
                eng.wait_ge(pr_done, self.u0 + (self.units.index(name) + 1))

            def out(self, eng, name):
                for on_, s, n0 in ((by_act, pr_act, self.a0), (by_dve, pr_dve, self.d0)):
                    if name in on_(self.units):
                        eng.wait_ge(s, n0 + (on_(self.units).index(name) + 1))

            def free(self, eng, name):
                n = self.units.index(name) - RING
                if n >= 0:
                    self.out(eng, self.units[n])
                elif self.before:
                    old = self.before[n]
                    for on_, s, n0 in ((by_act, pr_act, self.a0), (by_dve, pr_dve, self.d0)):
                        if old in on_(self.before):
                            eng.wait_ge(s, n0 - (len(on_(self.before)) - on_(self.before).index(old) - 1))

        AHEAD_STEP, FIRST, FINAL = Step(0, 0, ahead=True), Step(0, 0), Step(0, H - 1)

        STEP_ORDER = ((XR, 1, "xr1"), (GR, 1, "gr1"), (K, 2, "kv4"), (V, 2, "kv4"), (Q, 2, "q1"))

        with nc.Block() as block:
            @block.sync
            def _(sp_):
                def load_columns(h, par):
                    sp_.dma_start(hcol[par][:, 0:NCOL], pcol[:, bass.ds(h, 1), :].rearrange("p o c -> p (o c)")) \
                        .then_inc(col_in[par], 16)
                    sp_.dma_start(hcol[par][:, NCOL:], scol[:, bass.ds(h, 1), :].rearrange("p o c -> p (o c)")) \
                        .then_inc(col_in[par], 16)
                    for j, n in enumerate(("w_rg_a", "w_rg_i")):
                        sp_.dma_start(wrg[par][:, j, :], A[n][0, bass.ds(h, 1)].rearrange("o i j -> i (o j)")) \
                            .then_inc(col_in[par], 16)

                def load_cache(h, dst, src, s):
                    sp_.dma_start(dst[:, :, :], src.rearrange("b (k p) c -> p (b k) c", p=P)[:, :, bass.ds(h * P, P)]) \
                        .then_inc(s, 16)

                def store_kv(h, par):
                    for j, n in ((0, "k"), (1 + par, "v")):
                        outp, outs = O[f"new_{n}_prompt"][0, 0], O[f"new_{n}_sample"][0]
                        if n == "k":
                            outp, outs = outp.rearrange("s h m d -> s h (m d)"), outs.rearrange("b s h m d -> b s h (m d)")
                        outp = outp.rearrange("(t p) h c -> p t (h c)", p=P)
                        outs = outs.rearrange("b s h c -> (b s) (h c)")
                        sp_.dma_start(outp[:, :, bass.ds(h * P, P)], kvt[:, j, 0:NQ, :]).then_inc(kv_stored, 16)
                        sp_.dma_start(outs[:, bass.ds(h * P, P)], kvt[:, j, NQ, :]).then_inc(kv_stored, 16)

                k_src = A["cache_k"][0].rearrange("b s h m d -> b s (h m d)")
                v_src = A["cache_v"][0].rearrange("b s h d -> b s (h d)")

                def body(S):
                    h, par = S.h, S.par
                    if not S.last:
                        n = 5 * h + 8
                        ns = 5 * S.h0
                        load_tile(sp_, ns + 0, n, XR, h + 1)
                        refill(sp_, kc_in, ss_done, h + 1)
                        load_cache(h + 1, kc, k_src, kc_in)
                        need(sp_, rnn_done, h)
                        load_columns(h + 1, 1 - par)
                        refill(sp_, vc_in, os_done, h + 1)
                        load_cache(h + 1, vc, v_src, vc_in)
                        load_tile(sp_, ns + 1, n + 1, GR, h + 1)
                        S.out(sp_, "kv4")

                        store_kv(h + 1, 1 - par)

                        def ahead():
                            for x, j in enumerate((K, V, Q)):
                                load_tile(sp_, ns + 2 + x, n + (2 + x), j, h + 2)
                        if S.h0 == 2:
                            with sp_.If(S.i < H // 2 - 2):
                                ahead()
                        else:
                            ahead()

                load_columns(0, 0)
                load_cache(0, kc, k_src, kc_in)
                for n, (j, h) in enumerate(ORDER):
                    if n > EARLY:
                        load_tile(sp_, n, n, j, h)
                load_cache(0, vc, v_src, vc_in)
                AHEAD_STEP.out(sp_, "kv4")
                store_kv(0, 0)
                body(FIRST)
                with sp_.Fori(0, H // 2 - 1) as i:
                    body(Step(i, 1))
                    body(Step(i, 2))
                sp_.wait_ge(kv_stored, 64 * H)

            @block.gpsimd
            def _(pool):
                def body(S):
                    if S.last:
                        return

                    def tiles(x0, x1):
                        for x in range(x0, x1):
                            j, _, unit = STEP_ORDER[x]
                            S.done(pool, unit)
                            split_tile(pool, 5 * S.h0 + x, S.h * 5 + (8 + x), 5 * S.i + ((8 + 5 * S.h0 + x) // 2 + 1), j)
                    tiles(0, 2)
                    if S.h0 == 2:
                        with pool.If(S.i < H // 2 - 2):
                            tiles(2, 5)
                    else:
                        tiles(2, 5)

                nc.gpsimd.memset(qbd[:, :, :, :], 0.0).then_inc(init2, 1)
                nc.gpsimd.memset(xpad[:, 0:3], 0.0).then_inc(init2, 1)
                pool.wait_ge(init2, 2)
                for n, (j, h) in enumerate(ORDER):
                    if n >= 5:
                        AHEAD_STEP.done(pool, "kv4" if j != Q else "q1")
                    if n >= EARLY:
                        split_tile(pool, n, n, n // 2 + 1, j)
                body(FIRST)
                with pool.Fori(0, H // 2 - 1) as i:
                    body(Step(i, 1))
                    body(Step(i, 2))

            @block.tensor
            def _(pe):
                def product(out, pairs):
                    for k, (ah, al, bh, bl) in enumerate(pairs):
                        nc.tensor.matmul(out, ah, bh, start=(k == 0), stop=False)
                        nc.tensor.matmul(out, ah, bl, start=False, stop=False)
                        mm = nc.tensor.matmul(out, al, bh, start=False, stop=(k == len(pairs) - 1))
                    mm.then_inc(pr_done, 1)

                def features(S, name, j):
                    half = int(name[-1])
                    s = slice(half * HALF, (half + 1) * HALF)
                    S.free(pe, name)
                    product(S.bank(name)[:, 0:HALF],
                            [(wh[:, k, j, :], wl[:, k, j, :], xh[:, k, s], xl[:, k, s]) for k in range(KT)])

                def keys_values(S, name):
                    s = slice(int(name[2]) * P, int(name[2]) * P + P)
                    S.free(pe, name)
                    product(S.bank(name)[:, 0:2 * P],
                            [(xh[:, k, s], xl[:, k, s], wh[:, k, K:V + 1, :], wl[:, k, K:V + 1, :])
                             for k in range(KT)])

                def turn_keys(S):
                    for n, ts in enumerate(((0, 1), (2, 3), (4,))):
                        S.free(pe, f"kT{n}")
                        S.out(pe, f"kv{ts[-1]}")
                        for t in ts:
                            mm = nc.tensor.transpose(S.bank(f"kT{n}")[:, (t % 2) * P:(t % 2 + 1) * P],
                                                     kvt[:, 0, t, :], ident)
                        mm.then_inc(pr_done, 1)

                def tbank(S, u):
                    return bank[5 + (S.par * NT + u) % 2]

                def turn_bank(S, u):
                    need(pe, pt_out, S.h * NT + (u - 1))
                    return tbank(S, u)

                def turn_weights(S, qt):
                    pe.wait_ge(comb_ready, S.h * NQ + (qt + 1))
                    b = turn_bank(S, 5 + qt)
                    for k in range(qt + 1):
                        mm = nc.tensor.transpose(b[:, k * P:(k + 1) * P],
                                                 ebuf[(qt + 1) % 2][:, 0, k * P:(k + 1) * P], ident)
                    mm.then_inc(pt_done, 1)

                def values(S, qt):
                    pe.wait_ge(pt_out, S.h * NT + (6 + qt))
                    if qt == 0:
                        pe.wait_ge(os_out, S.h + 1)
                    for k in range(qt + 1):
                        mm = nc.tensor.matmul(bank[7][:, qt * P:(qt + 1) * P], wT[qt % 2][:, k * P:(k + 1) * P],
                                              kvt[:, 1 + S.par, k, :], start=(k == 0), stop=(k == qt))
                    if qt == NQ - 1:
                        mm.then_inc(op_done, 1)

                def scores(S, qt):
                    n = (qt + 1) * P
                    pe.wait_ge(exp_done, S.h * 5 + (qt + 1))
                    for m in range(2):
                        rows = slice(m * DH, (m + 1) * DH)
                        nc.tensor.matmul(bank[3 + m][:, 0:n], qT[rows, qt * P:(qt + 1) * P], kT[rows, 0:n],
                                         start=True, stop=False)
                        mm = nc.tensor.matmul(bank[3 + m][:, n - 64:n], cst[0:1, K_MASKQ:K_MASKQ + P],
                                              cst[0:1, K_MASKV:K_MASKV + 64], start=False, stop=True)
                    mm.then_inc(sc_done, 1)

                def body(S):
                    h, par, n = S.h, S.par, S.h * 5
                    ahead = not S.last
                    pe.wait_ge(kc_in, h * 16 + 16)
                    for u in range(4):
                        b = turn_bank(S, u)
                        for x in range(4):
                            mm = nc.tensor.transpose(b[:, x * P:(x + 1) * P], kc[:, 4 * u + x, :], ident)
                        mm.then_inc(pt_done, 1)
                    if S.first:
                        AHEAD_STEP.out(pe, "kT2")
                    else:
                        pe.wait_ge(pr_act, S.a0)
                    need(pe, exp_done, h * 5)
                    for g in range(2):
                        nc.tensor.matmul(bank[3 + g][:, KNEW:SKEYS],
                                         qbd[:, 4 * g:4 * g + 4, :, :].rearrange("p b m q -> p (b m q)"),
                                         kT[:, SEQ:TOK], start=True, stop=False)
                        nc.tensor.matmul(bank[3 + g][:, KNEW:SKEYS], cst[0:NS, K_IND + g * P:K_IND + (g + 1) * P],
                                         cst[0:NS, K_MST:K_MST + P], start=False, stop=True)
                    pe.wait_ge(pt_out, h * NT + 4)
                    for b in range(NS):
                        r = 32 * (b % 4)
                        mm = nc.tensor.matmul(bank[3 + b // 4][r:r + 32, 0:PAST],
                                              qbd[:, b, :, :].rearrange("p m q -> p (m q)"),
                                              kc[:, 2 * b:2 * b + 2, :].rearrange("p k c -> p (k c)"),
                                              start=True, stop=True)
                    mm.then_inc(ss_done, 1)
                    pe.wait_ge(split, n + 4)
                    features(S, "xr0", XR)
                    features(S, "xr1", XR)
                    pe.wait_ge(selc_ready, h + 1)
                    tb = turn_bank(S, 4)
                    for k in range(3):
                        for g in range(2):
                            mm = nc.tensor.matmul(tb[:, k * P + g * 64:k * P + g * 64 + 64],
                                                  ebuf[0][:, g, k * P:(k + 1) * P], selc[:, g, :],
                                                  start=True, stop=True)
                    mm.then_inc(pt_done, 1)
                    scores(S, 0)
                    if ahead:
                        pe.wait_ge(split, n + 7)
                        keys_values(S, "kv0")
                    pe.wait_ge(pt_out, h * NT + 5)
                    pe.wait_ge(vc_in, h * 16 + 16)
                    need(pe, op_out, h)
                    nc.tensor.matmul(bank[7][:, 0:P], kvt[:, 1 + par, NQ, :], wTs[:, 2, :], start=True, stop=True)
                    for b in range(NS):
                        for k in range(2):
                            mm = nc.tensor.matmul(bank[7][:, b * DS:(b + 1) * DS], vc[:, 2 * b + k, :],
                                                  wTs[:, k, b * DS:(b + 1) * DS], start=False,
                                                  stop=True, skip_group_check=True)
                    mm.then_inc(os_done, 1)
                    if ahead:
                        keys_values(S, "kv1")
                        keys_values(S, "kv2")
                    turn_weights(S, 0)
                    scores(S, 1)
                    pe.wait_ge(split, n + 5)
                    features(S, "gr0", GR)
                    values(S, 0)
                    turn_weights(S, 1)
                    scores(S, 2)
                    features(S, "gr1", GR)
                    values(S, 1)
                    if ahead:
                        keys_values(S, "kv3")
                    turn_weights(S, 2)
                    scores(S, 3)
                    pe.wait_ge(conv_done, h + 1)
                    for j, name in enumerate(("ra0", "ra1", "ri0", "ri1")):
                        if name == "ri1" and ahead:
                            keys_values(S, "kv4")
                        S.free(pe, name)
                        nc.tensor.matmul(S.bank(name)[:, 0:HALF], wrg[par][:, j // 2, :],
                                         xc[:, (j % 2) * HALF:(j % 2 + 1) * HALF],
                                         start=True, stop=True).then_inc(pr_done, 1)
                    values(S, 2)
                    if ahead:
                        pe.wait_ge(split, n + 8)
                        features(S, "q0", Q)
                        features(S, "q1", Q)
                    turn_weights(S, 3)
                    if ahead:
                        turn_keys(S)
                    values(S, 3)

                pe.wait_ge(init2, 2)
                pe.wait_ge(split, 2)
                for t in range(TT):
                    keys_values(AHEAD_STEP, f"kv{t}")
                pe.wait_ge(split, 3)
                features(AHEAD_STEP, "q0", Q)
                features(AHEAD_STEP, "q1", Q)
                turn_keys(AHEAD_STEP)
                body(FIRST)
                with pe.Fori(0, H // 2 - 1) as i:
                    body(Step(i, 1))
                    body(Step(i, 2))
                body(FINAL)

            @block.scalar
            def _(act):
                def softmax_exp(S, u, n):
                    act.wait_ge(max_ready, S.h * 5 + (u + 1))
                    for m in range(2):
                        ins = nc.scalar.activation(ebuf[u % 2][:, m, 0:n], bank[3 + m][:, 0:n], ACT.Exp,
                                                   bias=stat[:, u, 2 + m:3 + m], scale=SCALE,
                                                   accum_out=stat[:, u, 4 + m:5 + m])
                    ins.then_inc(exp_done, 1)

                def turned(S, u, out, n):
                    act.wait_ge(pt_done, S.h * NT + (u + 1))
                    nc.scalar.activation(out, bank[5 + (S.par * NT + u) % 2][:, 0:n], ACT.Copy).then_inc(pt_out, 1)

                def queries(S):
                    S.done(act, "q0")
                    nc.scalar.activation(qT[:, 0:HALF], S.bank("q0")[:, 0:HALF], ACT.Copy).then_inc(pr_act, 1)
                    S.done(act, "q1")
                    qs = S.bank("q1")[:, SEQ - HALF:HALF].rearrange("p (b q) -> p b q", q=DS)
                    for m in range(2):
                        rows = slice(m * DH, (m + 1) * DH)
                        nc.scalar.activation(qbd[rows, :, m, :], qs[rows], ACT.Copy)
                    nc.scalar.activation(qT[:, HALF:TOK], S.bank("q1")[:, 0:HALF], ACT.Copy).then_inc(pr_act, 1)

                def keys(S):
                    for n, (c0, c1) in enumerate(((0, 256), (256, 512), (512, 640))):
                        S.done(act, f"kT{n}")
                        nc.scalar.activation(kT[:, c0:c1], S.bank(f"kT{n}")[:, 0:c1 - c0], ACT.Copy) \
                            .then_inc(pr_act, 1)

                def tail(h, par):
                    nc.scalar.activation(ra[:, :], thr[:, :], ACT.Tanh, bias=hcol[par][:, C_SP2:C_SP2 + 1],
                                         scale=hcol[par][:, C_SP2:C_SP2 + 1]).then_inc(decay, 1)
                    act.wait_ge(gcube, h + 1)
                    nc.scalar.activation(gw[:, :], gw[:, :], ACT.Tanh, scale=GELU_C).then_inc(gtanh, 1)
                    act.wait_ge(decay, h + 1)
                    nc.scalar.activation(rw[:, :], ra[:, :], ACT.Sqrt).then_inc(roots2, 1)
                    act.wait_ge(ms_ready, h + 1)
                    nc.scalar.activation(oms[:, NQ:2 * NQ], oms[:, 0:NQ], ACT.Sqrt, scale=1.0 / DV,
                                         bias=eps_t[:, 0:1]).then_inc(roots2, 1)

                def body(S):
                    h, par = S.h, S.par
                    for u in range(4):
                        turned(S, u, kc[:, 4 * u:4 * u + 4, :].rearrange("p b k -> p (b k)"), 512)
                    act.wait_ge(ss_done, h + 1)
                    softmax_exp(S, 0, SKEYS)
                    if not S.first:
                        tail(h - 1, 1 - par)
                    turned(S, 4, wTs[:, :, :].rearrange("p k q -> p (k q)"), 3 * P)
                    softmax_exp(S, 1, P)
                    turned(S, 5, wT[0][:, 0:P], P)
                    softmax_exp(S, 2, 2 * P)
                    for half in range(2):
                        S.done(act, f"gr{half}")
                        nc.scalar.activation(gr[par][:, half * HALF:(half + 1) * HALF],
                                             S.bank(f"gr{half}")[:, 0:HALF], ACT.Copy).then_inc(pr_act, 1)
                        if half == 0:
                            turned(S, 6, wT[1][:, 0:2 * P], 2 * P)
                            softmax_exp(S, 3, 3 * P)
                    turned(S, 7, wT[0][:, 0:3 * P], 3 * P)
                    softmax_exp(S, 4, 4 * P)
                    act.wait_ge(col_in[par], S.i * 64 + (S.h0 // 2 * 64 + 64))
                    need(act, rnn_done, h)
                    for name, out, c in (("ra0", thr, R_BA), ("ra1", thr, R_BA), ("ri0", thi, R_BI), ("ri1", thi, R_BI)):
                        S.done(act, name)
                        s = slice(HALF * int(name[2]), HALF * int(name[2]) + HALF)
                        nc.scalar.activation(out[:, s], S.bank(name)[:, 0:HALF], ACT.Tanh,
                                             bias=hcol[par][:, c:c + 1], scale=0.5).then_inc(pr_act, 1)
                    if not S.last:
                        queries(S)
                    turned(S, 8, wT[1][:, 0:4 * P], 4 * P)
                    if not S.last:
                        keys(S)
                    else:
                        S.out(act, "ri1")

                act.wait_ge(init2, 2)
                queries(AHEAD_STEP)
                keys(AHEAD_STEP)
                body(FIRST)
                with act.Fori(0, H // 2 - 1) as i:
                    body(Step(i, 1))
                    body(Step(i, 2))
                body(FINAL)
                tail(H - 1, 1)

            @block.vector
            def _(dve):
                chain = Chain(dve, dve2)

                def row_max(S, u, n):
                    for m in range(2):
                        ins = nc.vector.tensor_reduce(stat[:, u, m:m + 1], bank[3 + m][:, 0:n], AX.X, ALU.max)
                    chain(ins)
                    nc.vector.tensor_scalar(stat[:, u, 2:4], stat[:, u, 0:2], -SCALE, None, ALU.mult) \
                        .then_inc(max_ready, 1)

                def prompt_max(S, qt):
                    dve.wait_ge(sc_done, S.h * NQ + (qt + 1))
                    row_max(S, qt + 1, (qt + 1) * P)

                def combine(S, qt):
                    u = qt + 1
                    n = (qt + 1) * P
                    dve.wait_ge(exp_done, S.h * 5 + (u + 1))
                    chain(nc.vector.reciprocal(stat[:, u, 6:8], stat[:, u, 4:6]))
                    chain(nc.vector.scalar_tensor_tensor(stat[:, u, 8:9], stat[:, u, 4:5], stat[:, u, 7:8], neglam,
                                                         ALU.mult, ALU.mult))
                    nc.vector.scalar_tensor_tensor(ebuf[u % 2][:, 0, 0:n], ebuf[u % 2][:, 1, 0:n], stat[:, u, 8:9],
                                                   ebuf[u % 2][:, 0, 0:n], ALU.mult, ALU.add).then_inc(comb_ready, 1)

                def copy_kv(S, t, par, h):
                    S.done(dve, f"kv{t}")
                    if t == 0:
                        need(dve, kv_stored, h * 64)
                    nc.vector.tensor_copy(kvt[:, 0:2 + par:1 + par, t, :],
                                          S.bank(f"kv{t}")[:, 0:2 * P].rearrange("p (j c) -> p j c", c=P)) \
                        .then_inc(pr_dve, 1)

                def conv(S):
                    cw = hcol[S.par]
                    xcs = xc[:, SEQ:TOK].rearrange("p (b q) -> p b q", q=DS)
                    for j in range(CW):
                        if j == 0:
                            nc.vector.tensor_scalar(xc[:, 0:SEQ], xpad[:, 0:SEQ], cw[:, R_CW:R_CW + 1],
                                                    cw[:, R_CB:R_CB + 1], ALU.mult, ALU.add)
                            chain(nc.vector.tensor_scalar(xcs, spad[:, :, 0:DS], cw[:, R_CW:R_CW + 1],
                                                          cw[:, R_CB:R_CB + 1], ALU.mult, ALU.add))
                            continue
                        nc.vector.scalar_tensor_tensor(xc[:, 0:SEQ], xpad[:, j:j + SEQ], cw[:, j:j + 1],
                                                       xc[:, 0:SEQ], ALU.mult, ALU.add)
                        ins = nc.vector.scalar_tensor_tensor(xcs, spad[:, :, j:j + DS], cw[:, j:j + 1],
                                                             xcs, ALU.mult, ALU.add)
                        if j < CW - 1:
                            chain(ins)
                        else:
                            ins.then_inc(conv_done, 1)

                def tail_a(h):
                    dve.wait_ge(decay, h + 1)
                    chain(nc.vector.tensor_scalar(thr[:, :], ra[:, :], 1.0, None, ALU.add))
                    chain(nc.vector.reciprocal(thr[:, :], thr[:, :]))
                    dve.wait_ge(roots2, h * 2 + 1)
                    nc.vector.tensor_scalar(ra[:, :], thr[:, :], 2.0, -1.0, ALU.mult, ALU.add)
                    chain(nc.vector.tensor_tensor(rw[:, :], rw[:, :], thr[:, :], ALU.mult))
                    chain(nc.vector.tensor_tensor(rw[:, :], rw[:, :], thi[:, :], ALU.mult))

                def tail_b(h, par):
                    a0 = ra[:, SEQ:TOK].rearrange("p (b q) -> p b q", q=DS)[:, :, 0]
                    b0 = rw[:, SEQ:TOK].rearrange("p (b q) -> p b q", q=DS)[:, :, 0]
                    chain(nc.vector.tensor_tensor(h0t[:, :], a0, hcol[par][:, NCOL + 24:NCOL + 32], ALU.mult))
                    nc.vector.tensor_tensor(b0, b0, h0t[:, :], ALU.add)
                    chain(nc.vector.memset(a0, 0.0))
                    chain(nc.vector.tensor_tensor_scan(rh[:, :], ra[:, :], rw[:, :], 0.0, ALU.mult, ALU.add))
                    nc.vector.tensor_scalar(stc[:, bass.ds(h, 1), 27:28], rh[:, SEQ - 1:SEQ]
                                            .rearrange("p (o c) -> p o c", o=1), 1.0, None, ALU.mult)
                    nc.vector.tensor_scalar(
                        stc[:, bass.ds(h, 1), 28:36],
                        rh[:, SEQ:TOK].rearrange("p (o b q) -> p o b q", o=1, q=DS)[:, :, :, DS - 1],
                        1.0, None, ALU.mult)

                def tail_c(h, par):
                    dve.wait_ge(gtanh, h + 1)
                    chain(nc.vector.scalar_tensor_tensor(gw[:, :], gw[:, :], 1.0, gr[par][:, :], ALU.add, ALU.mult))
                    chain(nc.vector.scalar_tensor_tensor(
                        yT[:, bass.ds(h, 1), :], rh[:, :].rearrange("p (o c) -> p o c", o=1), 0.5,
                        gw[:, :].rearrange("p (o c) -> p o c", o=1), ALU.mult, ALU.mult))
                    dve.wait_ge(roots2, h * 2 + 2)
                    chain(nc.vector.reciprocal(oms[:, 2 * NQ:3 * NQ], oms[:, NQ:2 * NQ]))
                    nc.vector.tensor_tensor(
                        on[:, bass.ds(h, 1), :, :].rearrange("p o t c -> p (o t) c"), oraw[:, :, :],
                        oms[:, 2 * NQ:3 * NQ].rearrange("p (t o) -> p t o", o=1).to_broadcast([P, NQ, DV]),
                        ALU.mult).then_inc(rnn_done, 1)

                def body(S):
                    h, par = S.h, S.par
                    base = 0 if S.first else h * (BODY_STEPS + TAIL_STEPS) - TAIL_STEPS
                    chain.at(base)
                    dve.wait_ge(ss_done, h + 1)
                    row_max(S, 0, SKEYS)
                    S.done(dve, "xr0")
                    nc.vector.tensor_copy(xpad[:, 3:3 + HALF], S.bank("xr0")[:, 0:HALF]).then_inc(pr_dve, 1)
                    dve.wait_ge(exp_done, h * 5 + 1)
                    chain(nc.vector.reciprocal(stat[:, 0, 6:8], stat[:, 0, 4:6]))
                    chain(nc.vector.tensor_scalar(stat[:, 0, 8:10], stat[:, 0, 6:8], msign, None, ALU.mult))
                    for g in range(2):
                        ins = nc.vector.tensor_scalar(selc[:, g, :], cst[:, K_SEL:K_SEL + 64],
                                                      stat[:, 0, 8 + g:9 + g], None, ALU.mult)
                    ins.then_inc(selc_ready, 1)
                    S.done(dve, "xr1")
                    nc.vector.tensor_copy(xpad[:, 3 + HALF:3 + SEQ], S.bank("xr1")[:, 0:SEQ - HALF])
                    nc.vector.tensor_copy(spad[:, :, 3:], S.bank("xr1")[:, SEQ - HALF:HALF]
                                          .rearrange("p (b q) -> p b q", q=DS)).then_inc(pr_dve, 1)
                    dve.wait_ge(col_in[par], S.i * 64 + (S.h0 // 2 * 64 + 64))
                    chain(nc.vector.tensor_copy(spad[:, :, 0:3],
                                                hcol[par][:, NCOL:NCOL + 24].rearrange("p (b w) -> p b w", w=3)))
                    prompt_max(S, 0)
                    if not S.first:
                        tail_a(h - 1)
                    if not S.last:
                        copy_kv(S, 0, 1 - par, h + 1)
                    dve.wait_ge(os_done, h + 1)
                    nc.vector.tensor_scalar(oTs[:, bass.ds(h, 1), :], bank[7][:, 0:P]
                                            .rearrange("p (o c) -> p o c", o=1), 1.0, None, ALU.mult) \
                        .then_inc(os_out, 1)
                    combine(S, 0)
                    if not S.last:
                        copy_kv(S, 1, 1 - par, h + 1)
                        copy_kv(S, 2, 1 - par, h + 1)
                    prompt_max(S, 1)
                    if not S.first:
                        tail_b(h - 1, 1 - par)
                    combine(S, 1)
                    if not S.first:
                        tail_c(h - 1, 1 - par)
                    prompt_max(S, 2)
                    conv(S)
                    combine(S, 2)
                    if not S.last:
                        copy_kv(S, 3, 1 - par, h + 1)
                    prompt_max(S, 3)
                    nc.vector.tensor_scalar(stc[:, bass.ds(h, 1), 0:3], xpad[:, SEQ:SEQ + 3]
                                            .rearrange("p (o c) -> p o c", o=1), 1.0, None, ALU.mult)
                    nc.vector.tensor_scalar(stc[:, bass.ds(h, 1), 3:27].rearrange("p o (b w) -> p (o b) w", w=3),
                                            spad[:, :, DS:DS + 3], 1.0, None, ALU.mult)
                    if not S.last:
                        copy_kv(S, 4, 1 - par, h + 1)
                    combine(S, 3)
                    S.out(dve, "gr1")
                    chain(nc.vector.tensor_tensor(gw[:, :], gr[par][:, :], gr[par][:, :], ALU.mult))
                    chain(nc.vector.tensor_scalar(gw[:, :], gw[:, :], 0.044715, 1.0, ALU.mult, ALU.add))
                    nc.vector.tensor_tensor(gw[:, :], gw[:, :], gr[par][:, :], ALU.mult).then_inc(gcube, 1)
                    S.out(dve, "ri1")
                    nc.vector.scalar_tensor_tensor(thi[:, :], thi[:, :], 1.0, xc[:, :], ALU.add, ALU.mult)
                    dve.wait_ge(op_done, h + 1)
                    nc.vector.tensor_tensor(oraw[:, :, :], bank[7][:, :].rearrange("p (t c) -> p t c", c=DV),
                                            stat[:, 1:5, 6:7].to_broadcast([P, NQ, DV]), ALU.mult).then_inc(op_out, 1)
                    dve.wait_ge(op_out, h + 1)
                    chain(nc.vector.tensor_tensor(osq, oraw[:, :, :], oraw[:, :, :], ALU.mult))
                    nc.vector.tensor_reduce(oms[:, 0:NQ], osq, AX.X, ALU.add).then_inc(ms_ready, 1)
                    want = BODY_STEPS + (0 if S.first else TAIL_STEPS)
                    assert chain.n == want, (chain.n, want)

                dve.wait_ge(init2, 2)
                for t in range(TT):
                    copy_kv(AHEAD_STEP, t, 0, 0)
                body(FIRST)
                with dve.Fori(0, H // 2 - 1) as i:
                    body(Step(i, 1))
                    body(Step(i, 2))
                body(FINAL)
                chain.at(H * (BODY_STEPS + TAIL_STEPS) - TAIL_STEPS)
                tail_a(H - 1)
                tail_b(H - 1, 1)
                tail_c(H - 1, 1)
        st2.close()
        early.close()
        build_rest(nc, A, O, locals())
        mid.close()


def build_rest(nc, A, O, v):
    top, mid, bank, cst, ident, ones = (v[n] for n in ("top", "mid", "bank", "cst", "ident", "ones"))
    sb, sem, eps_t, pcol, subln = (v[n] for n in ("sb", "sem", "eps_t", "pcol", "subln"))
    xh, xl, yT, on, oTs, stc = (v[n] for n in ("xh", "xl", "yT", "on", "oTs", "stc"))
    xn2_d, idx_d, y_d, xp, xs = (v[n] for n in ("xn2_d", "idx_d", "y_d", "xp", "xs"))

    def sbr(name, shape, ctx, dt=F32):
        return ctx.enter_context(nc.sbuf_tensor(name, shape, dt, side="right"))

    x2 = sbr("x2", [P, TT, D], top)
    late = ExitStack()
    mT = sbr("mT", [P, KT, TOK], late)
    st3 = ExitStack()
    attnT = sb("attnT", [P, KT, TOK], ctx=st3)
    graw = sb("graw", [P, 2, KT, P], ctx=st3)
    gh = sb("gh", [P, 2, KT, P], F32R, ctx=st3)
    gl = sb("gl", [P, 2, KT, P], F32R, ctx=st3)
    wp = [sb(f"wp{i}", [P, 2, KT, P], ctx=st3) for i in range(2)]
    gcol = [sb(f"gcol{i}", [P, 2], ctx=st3) for i in range(2)]
    tg = sb("tg", [P, 2, TOK], ctx=st3)
    m1 = sb("m1", [P, TOK], ctx=st3)
    m2 = sb("m2", [P, TOK], ctx=st3)
    srow2 = sb("srow2", [36, D], ctx=st3)
    zcol3 = sb("zcol3", [P, 1], ctx=st3)
    zero = sb("zero", [P, D], ctx=st3)
    zero_set, y_zeroed = sem("zero_set"), sem("y_zeroed")
    graw_in = [sem(f"graw_in{i}") for i in range(2)]
    wp_in = [sem(f"wp_in{i}") for i in range(2)]
    g_highs, g_split, zcol3_set = sem("g_highs"), sem("g_split"), sem("zcol3_set")
    x2_in, wo_in = sem("x2_in"), sem("wo_in")
    at_done, at_out, osq_ready, oms_done = sem("at_done"), sem("at_out"), sem("osq_ready"), sem("oms_done")
    oroot, os_norm, st_out, st_stored = sem("oroot"), sem("os_norm"), sem("st_out"), sem("st_stored")
    mg_done, mg_act, mg_dve, merged = sem("mg_done"), sem("mg_act"), sem("mg_dve"), sem("merged")
    dve3 = sem("dve3")
    w_out = A["w_out"][0].rearrange("(k p) n -> p k n", p=P)
    KINDS = ("ga", "gr", "ap", "rp")
    NM = 2 * len(KINDS)
    w_cols = A["w_in"][0].rearrange("(k p) n -> p k n", p=P)
    gate0 = 5 * D

    with nc.Block() as block:
        @block.sync
        def _(sp_):
            def load_gates(n):
                for j in range(2):
                    if not (isinstance(n, int) and n == 0):
                        sp_.wait_ge(g_split, n * 2 + (j - 1))
                    sp_.dma_start(graw[:, j, :, :], w_cols[:, :, bass.ds(gate0 + j * D + n * P, P)]) \
                        .then_inc(graw_in[j], 16)

            def load_proj(n, par):
                for j, w in enumerate(("w_attn_proj", "w_rnn_proj")):
                    src = A[w][0].rearrange("(k p) n -> p k n", p=P)[:, :, bass.ds(n * P, P)]
                    sp_.dma_start(wp[par][:, j, :, :], src).then_inc(wp_in[par], 16)
                sp_.dma_start(gcol[par][:, :], pcol[:, bass.ds(n, 1), R_GA:R_GR + 1]
                              .rearrange("p o c -> p (o c)")).then_inc(wp_in[par], 16)

            load_gates(0)
            load_proj(0, 0)
            load_gates(1)
            load_proj(1, 1)
            for t in range(TT):
                sp_.dma_start(x2[:, t, :], xp[:, t, :] if t < NQ else xs).then_inc(x2_in, 16)
            sp_.wait_ge(at_done, H)
            sp_.dma_start(on[:, :, :, :].rearrange("p k t c -> p k (t c)"), w_out[:, :, 0:D // 2]).then_inc(wo_in, 16)
            with sp_.Fori(0, KT // 2 - 1) as i:
                for par in range(2):
                    n = i * 2 + (2 + par)
                    load_gates(n)
                    sp_.wait_ge(wp_in[par], 48)
                    sp_.wait_ge(merged, CREDIT + i * 2 + (1 + par))
                    load_proj(n, par)
            sp_.wait_ge(st_out, 2)
            for dst, r0, r1 in ((O["new_conv_prompt"][0, 0], 0, 3),
                                (O["new_conv_sample"][0].rearrange("b w d -> (b w) d"), 3, 27),
                                (O["new_rnn_prompt"][0], 27, 28), (O["new_rnn_sample"][0], 28, 36)):
                sp_.dma_start(dst, srow2[r0:r1, :]).then_inc(st_stored, 16)
            sp_.wait_ge(st_stored, 64)

        @block.tensor
        def _(pe):
            for g in range(2):
                pe.wait_ge(osq_ready, g + 1)
                nc.tensor.matmul(bank[g][:, :], ones, attnT[:, 4 * g:4 * g + 4, 0:P], start=True, stop=True) \
                    .then_inc(oms_done, 1)
            for g in range(2):
                for k in range(4):
                    mm = nc.tensor.transpose(bank[2 + g][0:36, k * P:(k + 1) * P], stc[:, 4 * g + k, :], ident)
                mm.then_inc(oms_done, 1)
            for h in range(H):
                if h >= 4:
                    pe.wait_ge(at_out, h - 3)
                if h == 0:
                    pe.wait_ge(osq_ready, 2)
                for t in range(NQ):
                    mm = nc.tensor.transpose(bank[4 + h % 4][:, t * P:(t + 1) * P], on[:, h, t, :], ident)
                mm.then_inc(at_done, 1)
            pe.wait_ge(oroot, 2)
            pe.wait_ge(st_out, 2)
            with pe.Fori(0, KT // 2) as i:
                for par in range(2):
                    n = i * 2 + par
                    for j, kind in enumerate(KINDS):
                        if kind[0] == "g":
                            pe.wait_ge(mg_act, CREDIT + n * 4)
                            pe.wait_ge(g_split, n * 2 + (j + 1))
                        else:
                            if kind == "ap":
                                pe.wait_ge(at_out, H)
                                pe.wait_ge(os_norm, 2)
                                pe.wait_ge(wp_in[par], i * 48 + 48)
                            pe.wait_ge(mg_dve, CREDIT + n * 4)
                        for half in range(2):
                            out, s = bank[2 * j + half][:, 0:HALF], slice(half * HALF, (half + 1) * HALF)
                            for k in range(KT):
                                first, last = k == 0, k == KT - 1
                                if kind[0] == "g":
                                    nc.tensor.matmul(out, gh[:, j, k, :], xh[:, k, s], start=first, stop=False)
                                    nc.tensor.matmul(out, gh[:, j, k, :], xl[:, k, s], start=False, stop=False)
                                    mm = nc.tensor.matmul(out, gl[:, j, k, :], xh[:, k, s], start=False, stop=last)
                                else:
                                    mm = nc.tensor.matmul(out, wp[par][:, j - 2, k, :],
                                                          (attnT if kind == "ap" else yT)[:, k, s],
                                                          start=first, stop=last)
                            mm.then_inc(mg_done, 1)

        @block.gpsimd
        def _(pool):
            for s in (mg_act, mg_dve, merged):
                pool.sem_inc(s, CREDIT)
            nc.gpsimd.memset(zcol3[:, :], 0.0).then_inc(zcol3_set, 1)
            nc.gpsimd.memset(zero[:, :], 0.0).then_inc(zero_set, 1)
            pool.wait_ge(zcol3_set, 1)

            def split_gate(n, j):
                pool.wait_ge(graw_in[j], n * 16 + 16)
                nc.gpsimd.tensor_tensor(gh[:, j, :, :], graw[:, j, :, :],
                                        zcol3[:, 0:1].rearrange("p (a b) -> p a b", a=1).to_broadcast([P, KT, P]),
                                        ALU.add).then_inc(g_highs, 1)
                pool.wait_ge(g_highs, n * 2 + (j + 1))
                nc.gpsimd.tensor_tensor(gl[:, j, :, :], graw[:, j, :, :], gh[:, j, :, :].bitcast(F32),
                                        ALU.subtract).then_inc(g_split, 1)

            for j in range(2):
                split_gate(0, j)
            with pool.Fori(0, KT - 1) as n:
                for j in range(2):
                    pool.wait_ge(mg_done, n * NM + (2 * j + 2))
                    split_gate(n + 1, j)

        @block.scalar
        def _(act):
            for g in range(2):
                act.wait_ge(oms_done, g + 1)
                nc.scalar.activation(tg[:, g, 0:512], bank[g][:, :], ACT.Sqrt, scale=1.0 / DV,
                                     bias=eps_t[:, 0:1]).then_inc(oroot, 1)
            for h in range(H):
                act.wait_ge(at_done, h + 1)
                if h == 0:
                    act.wait_ge(oms_done, 2)
                nc.scalar.activation(attnT[:, h, 0:SEQ], bank[4 + h % 4][:, :], ACT.Copy,
                                     scale=subln[:, 0:1]).then_inc(at_out, 1)
            act.wait_ge(os_norm, 2)
            act.wait_ge(zero_set, 1)
            for b in range(NE + 1, NBLK + 1):
                act.dma_start(y_d[b * P:(b + 1) * P, :], zero[:, :]).then_inc(y_zeroed, 16)
            with act.Fori(0, KT // 2) as i:
                for par in range(2):
                    n = i * 2 + par
                    act.wait_ge(wp_in[par], i * 48 + 48)
                    act.wait_ge(merged, CREDIT + n)
                    for j, kind in enumerate(KINDS):
                        for half in range(2):
                            if kind[0] != "g":
                                continue
                            act.wait_ge(mg_done, n * NM + (2 * j + half + 1))
                            nc.scalar.activation(tg[:, j, half * HALF:(half + 1) * HALF],
                                                 bank[2 * j + half][:, 0:HALF], ACT.Tanh,
                                                 bias=gcol[par][:, j:j + 1], scale=0.5).then_inc(mg_act, 1)
            act.wait_ge(y_zeroed, 16 * OVMAX)

        @block.vector
        def _(dve):
            chain = Chain(dve, dve3)
            for g in range(2):
                nc.vector.tensor_tensor(attnT[:, 4 * g:4 * g + 4, 0:P], oTs[:, 4 * g:4 * g + 4, :],
                                        oTs[:, 4 * g:4 * g + 4, :], ALU.mult).then_inc(osq_ready, 1)
            for g in range(2):
                dve.wait_ge(oms_done, 2 + g + 1)
                nc.vector.tensor_copy(srow2[:, g * 512:(g + 1) * 512], bank[2 + g][0:36, :]).then_inc(st_out, 1)
            for g in range(2):
                dve.wait_ge(oroot, g + 1)
                chain(nc.vector.reciprocal(tg[:, g, 0:512], tg[:, g, 0:512]))
                nc.vector.scalar_tensor_tensor(attnT[:, 4 * g:4 * g + 4, SEQ:TOK], oTs[:, 4 * g:4 * g + 4, :],
                                               subln[:, 0:1], tg[:, g, 0:512].rearrange("p (k q) -> p k q", q=P),
                                               ALU.mult, ALU.mult).then_inc(os_norm, 1)
            with dve.Fori(0, KT // 2) as i:
                for par in range(2):
                    n = i * 2 + par
                    for j, kind in enumerate(KINDS):
                        if kind[0] == "g":
                            continue
                        dst = m1 if kind[0] == "a" else m2
                        for half in range(2):
                            s = slice(half * HALF, (half + 1) * HALF)
                            dve.wait_ge(mg_done, n * NM + (2 * j + half + 1))
                            dve.wait_ge(mg_act, CREDIT + n * 4 + (2 * (j - 2) + half + 1))
                            nc.vector.scalar_tensor_tensor(dst[:, s], tg[:, j - 2, s], 1.0,
                                                           bank[2 * j + half][:, 0:HALF], ALU.add, ALU.mult) \
                                .then_inc(mg_dve, 1)
                    dve.wait_ge(mg_dve, CREDIT + n * 4 + 4)
                    nc.vector.tensor_tensor(mT[:, bass.ds(n, 1), :], m1[:, :].rearrange("p (o c) -> p o c", o=1),
                                            m2[:, :].rearrange("p (o c) -> p o c", o=1), ALU.add).then_inc(merged, 1)
    st3.close()
    mid.close()

    w13 = [sb(f"w13_{i}", [P, 2, KT, FE]) for i in range(2)]
    w2b = [sb(f"w2_{i}", [P, FE // P, D]) for i in range(2)]
    wgt = sb("wgt", [P, 2, TT])
    slot = sb("slot", [P, 2, TT], I32)
    ovc = sb("ovc", [1, NE], I32)
    ovp = sb("ovp", [1, NE + 1], I32)
    w13_in = [[sem(f"w13_in{half}{i}") for i in range(2)] for half in range(2)]
    w2_in = [sem(f"w2_in{i}") for i in range(2)]

    OUT_UNITS = [(0, 0), (1, 0), (0, 1), (1, 1)] + [(t, half) for t in range(2, TT) for half in range(2)]
    w1s = A["w1"][0].rearrange("e (k p) f -> e p k f", p=P)
    w3s = A["w3"][0].rearrange("e (k p) f -> e p k f", p=P)
    w2s = A["w2"][0].rearrange("e (k p) n -> e p k n", p=P)

    def load13(eng, e, par, half):
        k = slice(half * KT // 2, (half + 1) * KT // 2)
        for j, src in enumerate((w1s, w3s)):
            eng.dma_start(w13[par][:, j, k, :], src[bass.ds(e, 1), :, k, :].rearrange("o p k f -> p (o k) f")) \
                .then_inc(w13_in[half][par], 16)

    def load2(eng, e, par, s):
        eng.dma_start(w2b[par][:, :, :], w2s[bass.ds(e, 1)].rearrange("o p k n -> p (o k) n")).then_inc(s, 16)

    wo = (on[:, :, :, :].rearrange("p k t c -> p k (t c)"),
          sbr("wo1", [P, KT, D // 2], late)[:, :, :])
    st4 = ExitStack()
    g2 = sb("g2", [P, D], ctx=st4)
    xn2 = [sb(f"xn2_{i}", [P, D], ctx=st4) for i in range(2)]
    xn2T = sb("xn2T", [P, KT, P], ctx=st4)
    sq4 = sb("sq4", [P, 512], ctx=st4)
    wr = sb("wr", [P, KT, NG + NE], ctx=st4)
    rb = sb("rb", [P, NG + NE], ctx=st4)
    lg = sb("lg", [P, TT, NG + NE], ctx=st4)
    ss4 = sb("ss4", [P, 4, TT], ctx=st4)
    sm = sb("sm", [P, TT, 64], ctx=st4)
    oh = sb("oh", [P, 3, TT, NE], ctx=st4)
    rk = sb("rk", [P, 2, TT, NE], ctx=st4)
    ex = sb("ex", [P, 8, NE], ctx=st4)
    toki = sb("toki", [P, TT], I32, ctx=st4)
    r_in, mo_done, x2_ready = sem("r_in"), sem("mo_done"), sem("x2_ready")
    ss_ready, root4, rec4, xn2_ready = sem("ss_ready"), sem("root4"), sem("rec4"), sem("xn2_ready")
    xn2_stored = [sem(f"xn2_stored{i}") for i in range(2)]
    x2t_done, x2t_out, rt_done, rt_out = sem("x2t_done"), sem("x2t_out"), sem("rt_done"), sem("rt_out")
    gl_ready, ge_ready, ranks_done, oh_ready = sem("gl_ready"), sem("ge_ready"), sem("ranks_done"), sem("oh_ready")
    slots_ready, scattered, dve4, act4 = sem("slots_ready"), sem("scattered"), sem("dve4"), sem("act4")

    with nc.Block() as block:
        @block.sync
        def _(sp_):
            sp_.dma_start(wo[1], w_out[:, :, D // 2:]).then_inc(wo_in, 16)
            sp_.dma_start(g2[:, :], A["norm2_g"].to_broadcast([P, D])).then_inc(r_in, 16)
            sp_.dma_start(wr[:, :, 0:NG], A["w_group"][0].rearrange("(k p) n -> p k n", p=P)).then_inc(r_in, 16)
            sp_.dma_start(wr[:, :, NG:], A["w_router"][0].rearrange("(k p) n -> p k n", p=P)).then_inc(r_in, 16)
            sp_.dma_start(rb[:, 0:NG], A["b_group"].to_broadcast([P, NG])).then_inc(r_in, 16)
            sp_.dma_start(rb[:, NG:], A["b_router"].to_broadcast([P, NE])).then_inc(r_in, 16)
            for e in range(2):
                load13(sp_, e, e, 0)
                load13(sp_, e, e, 1)
                load2(sp_, e, e, w2_in[e])
            for t in range(TT):
                sp_.wait_ge(xn2_ready, t + 1)
                sp_.dma_start(xn2_d[t * P:(t + 1) * P, :], xn2[t % 2][:, :]).then_inc(xn2_stored[t % 2], 16)
            sp_.wait_ge(xn2_stored[0], 48)
            sp_.wait_ge(xn2_stored[1], 32)

        @block.gpsimd
        def _(pool):
            pool.wait_ge(slots_ready, 1)
            for t in range(TT):
                for k in range(2):
                    pool.indirect_dma_start(idx_d, bass.IndirectOffsetOnAxis(ap=slot[:, k, t:t + 1], axis=0),
                                            toki[:, t:t + 1], None).then_inc(scattered, 16)
            pool.wait_ge(scattered, 16 * 2 * TT)

        @block.tensor
        def _(pe):
            pe.wait_ge(x2_in, 16 * TT)

            def route(t):
                pe.wait_ge(r_in, 80)
                pe.wait_ge(xn2_ready, t + 1)
                if t >= 1:
                    pe.wait_ge(x2t_out, 2 * t)
                for half in range(2):
                    for k in range(4):
                        c = (4 * half + k) * P
                        mm = nc.tensor.transpose(bank[4 + half][:, k * P:(k + 1) * P], xn2[t % 2][:, c:c + P], ident)
                    mm.then_inc(x2t_done, 1)
                pe.wait_ge(x2t_out, 2 * t + 2)
                for k in range(KT):
                    mm = nc.tensor.matmul(bank[6][:, t * 32:t * 32 + NG + NE], xn2T[:, k, :], wr[:, k, :],
                                          start=(k == 0), stop=(k == KT - 1))
                mm.then_inc(rt_done, 1)

            for u, (t, half) in enumerate(OUT_UNITS):
                if u < 4 and half != OUT_UNITS[u - 1][1]:
                    pe.wait_ge(wo_in, 16 * (half + 1))
                if u >= 4:
                    pe.wait_ge(x2_ready, u - 3)
                for k in range(KT):
                    mm = nc.tensor.matmul(bank[u % 4][:, :], mT[:, k, t * P:(t + 1) * P], wo[half][:, k, :],
                                          start=(k == 0), stop=(k == KT - 1))
                mm.then_inc(mo_done, 1)
                if half == 0:
                    continue
                if t >= 1:
                    route(t - 1)
            route(TT - 1)
            pe.wait_ge(oh_ready, 1)
            for t in range(TT):
                for s in range(t + 1):
                    nc.tensor.matmul(bank[7][:, t * NE:(t + 1) * NE], ones if s < t else cst[:, K_TRI:K_TRI + P],
                                     oh[:, 2, s, :], start=(s == 0), stop=(s == t))
            for s in range(TT):
                mm = nc.tensor.matmul(bank[7][:, TT * NE:(TT + 1) * NE], ones, oh[:, 2, s, :],
                                      start=(s == 0), stop=(s == TT - 1))
            mm.then_inc(ranks_done, 1)

        @block.scalar
        def _(act):
            for t in range(TT):
                act.wait_ge(x2_ready, OUT_UNITS.index((t, 1)) + 1)
                if t >= 1:
                    act.wait_ge(act4, t)
                for half in range(2):
                    ins = nc.scalar.activation(sq4[:, :], x2[:, t, half * 512:(half + 1) * 512], ACT.Square,
                                               accum_out=ss4[:, half, t:t + 1])
                    ins.then_inc(act4, 1) if half else ins.then_inc(ss_ready, 1)
                    if half == 0:
                        act.wait_ge(ss_ready, 2 * t + 1)
                act.wait_ge(act4, t + 1)
                nc.scalar.activation(ss4[:, 2, t:t + 1], ss4[:, 0, t:t + 1], ACT.Identity,
                                     bias=ss4[:, 1, t:t + 1]).then_inc(ss_ready, 1)
                act.wait_ge(ss_ready, 2 * t + 2)
                nc.scalar.activation(ss4[:, 3, t:t + 1], ss4[:, 2, t:t + 1], ACT.Sqrt, scale=1.0 / D,
                                     bias=eps_t[:, 0:1]).then_inc(root4, 1)
                act.wait_ge(x2t_done, 2 * t + 1)
                if t >= 1:
                    act.wait_ge(rt_done, t)
                nc.scalar.activation(xn2T[:, 0:4, :].rearrange("p k q -> p (k q)"), bank[4][:, :], ACT.Copy) \
                    .then_inc(x2t_out, 1)
                act.wait_ge(x2t_done, 2 * t + 2)
                nc.scalar.activation(xn2T[:, 4:8, :].rearrange("p k q -> p (k q)"), bank[5][:, :], ACT.Copy) \
                    .then_inc(x2t_out, 1)
            act.wait_ge(gl_ready, 1)
            nc.scalar.activation(sm[:, :, 8:13], sm[:, :, 0:5], ACT.Exp).then_inc(ge_ready, 1)

        @block.vector
        def _(dve):
            chain = Chain(dve, dve4)
            for u, (t, half) in enumerate(OUT_UNITS):
                s = slice(half * 512, (half + 1) * 512)
                dve.wait_ge(mo_done, u + 1)
                nc.vector.scalar_tensor_tensor(x2[:, t, s], bank[u % 4][:, :], 0.5, x2[:, t, s],
                                               ALU.mult, ALU.add).then_inc(x2_ready, 1)
                if half == 0:
                    continue
                dve.wait_ge(r_in, 80)
                dve.wait_ge(root4, t + 1)
                chain(nc.vector.reciprocal(ss4[:, 2, t:t + 1], ss4[:, 3, t:t + 1]))
                if t >= 2:
                    dve.wait_ge(xn2_stored[t % 2], 16 * (t // 2))
                nc.vector.scalar_tensor_tensor(xn2[t % 2][:, :], x2[:, t, :], ss4[:, 2, t:t + 1], g2[:, :],
                                               ALU.mult, ALU.mult).then_inc(xn2_ready, 1)
            dve.wait_ge(rt_done, TT)
            chain(nc.vector.tensor_tensor(
                lg[:, :, :], bank[6][:, 0:TT * 32].rearrange("p (t c) -> p t c", c=32)[:, :, 0:NG + NE],
                rb[:, :].rearrange("p (o c) -> p o c", o=1).to_broadcast([P, TT, NG + NE]), ALU.add))

            def col(i, n=1):
                return sm[:, :, i:i + n]

            def tt(out, a, b, op):
                chain(nc.vector.tensor_tensor(out, a, b, op))

            def ts(out, a, s1, s2, op0, op1=None):
                if op1 is None:
                    chain(nc.vector.tensor_scalar(out, a, s1, None, op0))
                else:
                    chain(nc.vector.tensor_scalar(out, a, s1, s2, op0, op1))

            def first_max(src, top_, hot, t0):
                chain(nc.vector.tensor_reduce(top_, src, AX.X, ALU.max))
                tt(hot, src, top_.to_broadcast([P, TT, 4]), ALU.is_equal)
                seen = col(t0)
                ts(seen, hot[:, :, 0:1], -1.0, 1.0, ALU.mult, ALU.add)
                for j in range(1, 4):
                    tt(hot[:, :, j:j + 1], hot[:, :, j:j + 1], seen, ALU.mult)
                    if j < 3:
                        tt(seen, seen, hot[:, :, j:j + 1], ALU.subtract)

            gmax, ghot, ein, e1, f1, em, e2, f2 = col(16), col(20, 4), col(24, 4), col(28), col(32, 4), col(36, 4), \
                col(40), col(44, 4)
            first_max(lg[:, :, 0:NG], gmax, ghot, 17)
            tt(col(0, 4), lg[:, :, 0:NG], gmax.to_broadcast([P, TT, 4]), ALU.subtract)
            tt(ein, lg[:, :, NG:NG + EG], ghot[:, :, 0:1].to_broadcast([P, TT, EG]), ALU.mult)
            for g in range(1, NG):
                tt(col(48, 4), lg[:, :, NG + g * EG:NG + (g + 1) * EG],
                   ghot[:, :, g:g + 1].to_broadcast([P, TT, EG]), ALU.mult)
                tt(ein, ein, col(48, 4), ALU.add)
            first_max(ein, e1, f1, 18)
            ts(col(48, 4), f1, -1.0, 1.0, ALU.mult, ALU.add)
            tt(em, ein, col(48, 4), ALU.mult)
            ts(col(52, 4), f1, -BIG, None, ALU.mult)
            tt(em, em, col(52, 4), ALU.add)
            first_max(em, e2, f2, 19)
            nc.vector.tensor_tensor(col(4), e2, e1, ALU.subtract).then_inc(gl_ready, 1)
            for g in range(NG):
                for k, f in enumerate((f1, f2)):
                    ins = nc.vector.tensor_tensor(oh[:, k, :, g * EG:(g + 1) * EG], f,
                                                  ghot[:, :, g:g + 1].to_broadcast([P, TT, EG]), ALU.mult)
            chain(ins)
            nc.vector.tensor_tensor(oh[:, 2, :, :], oh[:, 0, :, :], oh[:, 1, :, :], ALU.add).then_inc(oh_ready, 1)
            dve.wait_ge(ge_ready, 1)
            chain(nc.vector.tensor_reduce(col(56), col(8, 4), AX.X, ALU.add))
            ts(col(57), col(12), 1.0, None, ALU.add)
            tt(col(56), col(56), col(57), ALU.mult)
            chain(nc.vector.reciprocal(col(58), col(56)))
            ts(wgt[:, 0, :], sm[:, :, 58], 1.0, None, ALU.mult)
            tt(wgt[:, 1, :], sm[:, :, 58], sm[:, :, 12], ALU.mult)
            dve.wait_ge(ranks_done, 1)
            cnt, ov, pre, tmp = (ex[:, i, :] for i in range(4))
            chain(nc.vector.tensor_copy(cnt, bank[7][:, TT * NE:(TT + 1) * NE]))
            ts(ov, cnt, float(P), None, ALU.is_gt)
            for j in range(2, TT):
                ts(tmp, cnt, float(j * P), None, ALU.is_gt)
                tt(ov, ov, tmp, ALU.add)
            a, b = ex[:, 4, :], ex[:, 5, :]
            chain(nc.vector.tensor_copy(a, ov))
            for d in (1, 2, 4, 8):
                chain(nc.vector.tensor_copy(b[:, 0:d], a[:, 0:d]))
                tt(b[:, d:], a[:, d:], a[:, 0:NE - d], ALU.add)
                a, b = b, a
            tt(pre, a, ov, ALU.subtract)
            incl = a
            r, z = rk[:, 0, :, :], rk[:, 1, :, :]
            chain(nc.vector.tensor_copy(r, bank[7][:, 0:TT * NE].rearrange("p (t e) -> p t e", e=NE)))
            tt(tmp, pre, cst[:, K_EID:K_EID + NE], ALU.add)
            ts(tmp, tmp, float(P), float(P), ALU.mult, ALU.add)
            tt(r, r, tmp.rearrange("p (o e) -> p o e", o=1).to_broadcast([P, TT, NE]), ALU.add)
            for k in range(2):
                tt(z, r, oh[:, k, :, :], ALU.mult)
                chain(nc.vector.tensor_reduce(col(60 + k), z, AX.X, ALU.add))
                chain(nc.vector.tensor_copy(slot[:, k, :], sm[:, :, 60 + k]))
            chain(nc.vector.tensor_copy(ovc[:, :], ov[0:1]))
            chain(nc.vector.tensor_copy(ovp[:, 0:NE], pre[0:1]))
            chain(nc.vector.tensor_copy(ovp[:, NE:], incl[0:1, NE - 1:NE]))
            chain(nc.vector.tensor_copy(toki[:, :], cst[:, K_TOK:K_TOK + TT]))
            nc.vector.memset(ex[:, 7, :], 0.0).then_inc(slots_ready, 1)
    st4.close()
    late.close()

    gf = sb("gf", [P, D])
    st5 = ExitStack()
    UPC, DNC = KT, FE // P
    NCH = UPC + DNC
    RING5 = 4
    assert UPC % RING5 == 0 and NCH % RING5 == 0
    PER_DVE, PER_POOL = NCH // RING5 * (RING5 - 1), NCH // RING5
    UP_DVE, UP_POOL = UPC // RING5 * (RING5 - 1), UPC // RING5

    NIDX = NBLK + 3
    idxr = sb("idxr", [NIDX, P], I32, ctx=st5)
    idxf = sb("idxf", [NIDX, P], ctx=st5)
    idxt = sb("idxt", [P, NIDX], ctx=st5)
    idx = sb("idx", [P, 1], I32, ctx=st5)
    xg = sb("xg", [P, D], ctx=st5)
    xeh = sb("xeh", [P, KT, P], F32R, ctx=st5)
    xel = sb("xel", [P, KT, P], F32R, ctx=st5)
    th = sb("th", [P, FE], ctx=st5)
    gg = sb("gg", [P, FE], ctx=st5)
    hTh = sb("hTh", [P, FE], F32R, ctx=st5)
    hTl = sb("hTl", [P, FE], F32R, ctx=st5)
    yb = sb("yb", [P, D], ctx=st5)
    ch = sb("ch", [P, RING5, 2, 512], F32R, ctx=st5)
    cl = sb("cl", [P, RING5, 2, 512], F32R, ctx=st5)
    gate = sb("gate", [P, 3], ctx=st5)

    gf_in, idx_in, xg_in, y_stored = sem("gf_in"), sem("idx_in"), sem("xg_in"), sem("y_stored")
    idxr_in, idxf_ready, idxt_done, idxt_ready = sem("idxr_in"), sem("idxf_ready"), sem("idxt_done"), sem("idxt_ready")
    xt_done, xt_high, xt_low = sem("xt_done"), sem("xt_high"), sem("xt_low")
    used, ch_high, ch_low_dve, ch_low_pool = sem("used"), sem("ch_high"), sem("ch_low_dve"), sem("ch_low_pool")
    th_ready, s_ready, gg_ready = sem("th_ready"), sem("s_ready"), sem("gg_ready")
    ht_done, ht_high, ht_low = sem("ht_done"), sem("ht_high"), sem("ht_low")
    y_act, y_dve, held, gate_set = sem("y_act"), sem("y_dve"), sem("held"), sem("gate_set")

    class Turn:
        def __init__(self, b, up, down):
            self.b, self.up, self.down = b, up, down
            if down is None:
                self.n, self.nd, self.np = 0, 0, 0
            elif up is None:
                self.n, self.nd, self.np = b * NCH - NCH, b * PER_DVE - PER_DVE, b * PER_POOL - PER_POOL
            else:
                self.n = b * NCH - DNC
                self.nd, self.np = b * PER_DVE - (PER_DVE - UP_DVE), b * PER_POOL - (PER_POOL - UP_POOL)

        def raw(self, c):
            if c < UPC:
                return w13[self.up[0]][:, :, c, :]
            return w2b[self.down[0]][:, c - UPC, :].rearrange("p (j n) -> p j n", j=2)

        def high(self, eng, c):
            eng.wait_ge(ch_high, self.n + (c + 1))

        def low(self, eng, c):
            if c % RING5 == RING5 - 1:
                eng.wait_ge(ch_low_pool, self.np + (c // RING5 + 1))
            else:
                eng.wait_ge(ch_low_dve, self.nd + (c // RING5 * (RING5 - 1) + c % RING5 + 1))

        def outputs_made(self, eng):
            eng.wait_ge(used, self.b * NCH - DNC)

    def each_block(eng, step, last):
        def count(row, e, top_):
            return eng.value_load(row[0:1, bass.ds(e, 1)], min_val=0, max_val=top_)

        def expert(e, up, down):
            if down is None:
                step(Turn(0, up, None))
            else:
                step(Turn(count(ovp, e, OVMAX) + e, up, down))
            n = count(ovc, e, TT - 1)
            with eng.If(n > 0):
                with eng.Fori(count(ovp, e, OVMAX - 1), count(ovp, e + 1, OVMAX)) as j:
                    step(Turn(j + (e + 1), up, up))

        expert(0, (0, 1), None)
        with eng.Fori(0, NE // 2 - 1) as i:
            expert(i * 2 + 1, (1, i + 1), (0, i + 1))
            expert(i * 2 + 2, (0, i + 2), (1, i + 1))
        expert(NE - 1, (1, NE // 2), (0, NE // 2))
        last(Turn(count(ovp, NE, OVMAX) + NE, None, (1, NE // 2)))

    with nc.Block() as block:
        @block.sync
        def _(sp_):
            sp_.dma_start(idxr[:, :], idx_d.rearrange("(b p) o -> b (p o)", p=P)).then_inc(idxr_in, 16)
            sp_.dma_start(gf[:, :], A["final_norm_g"].rearrange("(o d) -> o d", o=1).to_broadcast([P, D])) \
                .then_inc(gf_in, 16)
            with sp_.Fori(0, NE // 2 - 1) as i:
                for par in range(2):
                    e = i * 2 + (2 + par)
                    b = sp_.value_load(ovp[0:1, bass.ds(e - 1, 1)], min_val=0, max_val=OVMAX) + (i * 2 + par)
                    sp_.wait_ge(used, b * NCH + UPC // 2)
                    load13(sp_, e, par, 0)
                    sp_.wait_ge(used, b * NCH + UPC)
                    load13(sp_, e, par, 1)
                    sp_.wait_ge(used, b * NCH + (UPC + NCH))
                    load2(sp_, e, par, w2_in[par])

        @block.gpsimd
        def _(pool):
            for s in (y_stored, held):
                pool.sem_inc(s, CREDIT)
            nc.gpsimd.memset(gate[:, 0:1], 0.0).then_inc(gate_set, 1)
            pool.wait_ge(gate_set, 1)

            def gather(b):
                if not isinstance(b, int) or b > 0:
                    pool.wait_ge(xt_done, b)
                pool.wait_ge(idx_in, b + 1)
                if not isinstance(b, int):
                    hold(b - 3)
                pool.indirect_dma_start(xg[:, :], None, xn2_d, bass.IndirectOffsetOnAxis(ap=idx[:, 0:1], axis=0)) \
                    .then_inc(xg_in, 16)

            def hold(n):
                pool.wait_ge(held, n + CREDIT)
                nc.gpsimd.tensor_tensor(gate[:, 1:2], gate[:, 0:1], gate[:, 0:1], ALU.add).then_inc(held, 1)

            def low(S, c):
                S.high(pool, c)
                nc.gpsimd.tensor_tensor(cl[:, c % RING5, :, :], S.raw(c), ch[:, c % RING5, :, :].bitcast(F32),
                                        ALU.subtract).then_inc(ch_low_pool, 1)

            def step(S):
                for c in range(RING5 - 1, UPC if S.down is None else NCH, RING5):
                    low(S, c)
                gather(S.b + 2)

            def last(S):
                low(S, NCH - 1)
                pool.wait_ge(xg_in, S.b * 16 + 32)
                hold(S.b - 1)

            gather(0)
            gather(1)
            each_block(pool, step, last)

        @block.tensor
        def _(pe):
            def chunk(S, c):
                S.low(pe, c)
                first, end = c in (0, UPC), c in (UPC - 1, NCH - 1)
                k = c if c < UPC else c - UPC
                ah, al = (xeh[:, k, :], xel[:, k, :]) if c < UPC else \
                    (hTh[:, k * P:(k + 1) * P], hTl[:, k * P:(k + 1) * P])
                for j in range(2):
                    out = bank[(2 if c < UPC else 5) + j][:, :]
                    high, low = ch[:, c % RING5, j, :], cl[:, c % RING5, j, :]
                    nc.tensor.matmul(out, ah, high, start=first, stop=False)
                    nc.tensor.matmul(out, ah, low, start=False, stop=False)
                    mm = nc.tensor.matmul(out, al, high, start=False, stop=end)
                mm.then_inc(used, 1)

            def turn_tokens(b):
                pe.wait_ge(xg_in, b * 16 + 16)
                if not isinstance(b, int) or b > 0:
                    pe.wait_ge(xt_high, b)
                    pe.wait_ge(xt_low, b)
                for k in range(KT):
                    mm = nc.tensor.transpose(bank[k // 4][:, k % 4 * P:(k % 4 + 1) * P], xg[:, k * P:(k + 1) * P],
                                             ident)
                mm.then_inc(xt_done, 1)

            def turn_hidden():
                for k in range(DNC):
                    mm = nc.tensor.transpose(bank[4][:, k * P:(k + 1) * P], gg[:, k * P:(k + 1) * P], ident)
                mm.then_inc(ht_done, 1)

            def down(S):
                pe.wait_ge(y_act, S.b)
                pe.wait_ge(y_dve, S.b)
                pe.wait_ge(ht_high, S.b)
                pe.wait_ge(ht_low, S.b)
                for c in range(UPC, NCH):
                    chunk(S, c)

            def step(S):
                if S.down is not None:
                    pe.wait_ge(gg_ready, S.b)
                pe.wait_ge(xt_high, S.b + 1)
                pe.wait_ge(xt_low, S.b + 1)
                for c in range(UPC):
                    if c == UPC // 2 and S.down is not None:
                        turn_hidden()
                    chunk(S, c)
                turn_tokens(S.b + 1)
                if S.down is not None:
                    down(S)

            def last(S):
                pe.wait_ge(gg_ready, S.b)
                turn_hidden()
                down(S)

            for half in range(2):
                nc.tensor.matmul(bank[5 + half][:, :], ident, cst[:, 0:512], start=True, stop=True)
            pe.wait_ge(idxf_ready, 1)
            nc.tensor.transpose(bank[7][:, 0:NIDX], idxf[:, :], ident[0:NIDX, 0:NIDX]).then_inc(idxt_done, 1)
            turn_tokens(0)
            each_block(pe, step, last)

        @block.scalar
        def _(act):
            def high(S, c):
                if c in (0, UPC // 2):
                    act.wait_ge(w13_in[c // (UPC // 2)][S.up[0]], S.up[1] * 32)
                if c == UPC:
                    act.wait_ge(w2_in[S.down[0]], S.down[1] * 16)
                if S.down is not None or c >= RING5:
                    act.wait_ge(used, S.n + (c - RING5 + 1))
                nc.scalar.activation(ch[:, c % RING5, :, :], S.raw(c), ACT.Copy).then_inc(ch_high, 1)

            def turned(b):
                act.wait_ge(xt_done, b + 1)
                for half in range(2):
                    ins = nc.scalar.activation(xeh[:, 4 * half:4 * half + 4, :].rearrange("p k q -> p (k q)"),
                                               bank[half][:, :], ACT.Copy)
                ins.then_inc(xt_high, 1)

            def outputs(S, final=False):
                n = S.b + 1 if final else S.b
                act.wait_ge(y_stored, n * 16 + (CREDIT - 16))
                act.wait_ge(used, S.b * NCH if final else n * NCH - DNC)
                nc.scalar.activation(yb[:, 0:512], bank[5][:, :], ACT.Copy).then_inc(y_act, 1)

            def store(S, final=False):
                n = S.b + 1 if final else S.b
                act.wait_ge(y_act, n)
                act.wait_ge(y_dve, n)
                act.dma_start(y_d[bass.ds((n - 1) * P, P), :], yb[:, :]).then_inc(y_stored, 16)

            def hidden(S):
                act.wait_ge(ht_done, S.b)
                nc.scalar.activation(hTh[:, :], bank[4][:, :], ACT.Copy).then_inc(ht_high, 1)

            def step(S):
                for c in range(UPC):
                    if c == RING5 - 1 and S.down is not None:
                        outputs(S)
                    high(S, c)
                    if c == RING5 + 1 and S.down is not None:
                        store(S)
                if S.down is not None:
                    hidden(S)
                    for c in range(UPC, NCH):
                        high(S, c)
                turned(S.b + 1)
                if S.down is not None:
                    act.wait_ge(s_ready, S.b)
                nc.scalar.activation(th[:, :], bank[2][:, :], ACT.Tanh, scale=0.5).then_inc(th_ready, 1)

            def last(S):
                outputs(S)
                store(S)
                hidden(S)
                for c in range(UPC, NCH):
                    high(S, c)
                outputs(S, True)
                store(S, True)
                act.wait_ge(y_stored, S.b * 16 + (CREDIT + 16))
                nc.scalar.activation(gate[:, 2:3], eps_t[:, 0:1], ACT.Copy)

            turned(0)
            each_block(act, step, last)

        @block.vector
        def _(dve):
            def low(S, c):
                S.high(dve, c)
                nc.vector.tensor_tensor(cl[:, c % RING5, :, :], S.raw(c), ch[:, c % RING5, :, :].bitcast(F32),
                                        ALU.subtract).then_inc(ch_low_dve, 1)

            def indices(b):
                nc.vector.tensor_scalar(idx[:, :], idxt[:, bass.ds(b + 1, 1)], 1.0, None, ALU.mult) \
                    .then_inc(idx_in, 1)

            def turned(b):
                dve.wait_ge(xt_high, b + 1)
                for half in range(2):
                    s = slice(4 * half, 4 * half + 4)
                    ins = nc.vector.tensor_tensor(xel[:, s, :].rearrange("p k q -> p (k q)"), bank[half][:, :],
                                                  xeh[:, s, :].bitcast(F32).rearrange("p k q -> p (k q)"),
                                                  ALU.subtract)
                ins.then_inc(xt_low, 1)
                indices(b + 1)

            def outputs(S, final=False):
                n = S.b + 1 if final else S.b
                dve.wait_ge(y_stored, n * 16 + (CREDIT - 16))
                dve.wait_ge(used, S.b * NCH if final else n * NCH - DNC)
                nc.vector.tensor_copy(yb[:, 512:D], bank[6][:, :]).then_inc(y_dve, 1)

            def hidden(S):
                dve.wait_ge(ht_high, S.b)
                nc.vector.tensor_tensor(hTl[:, :], bank[4][:, :], hTh[:, :].bitcast(F32), ALU.subtract) \
                    .then_inc(ht_low, 1)

            def step(S):
                for c in range(UPC):
                    if c % RING5 < RING5 - 1:
                        low(S, c)
                    elif c < RING5 and S.down is not None:
                        outputs(S)
                if S.down is not None:
                    hidden(S)
                    for c in range(UPC, NCH):
                        if c % RING5 < RING5 - 1:
                            low(S, c)
                turned(S.b + 1)
                dve.wait_ge(th_ready, S.b + 1)
                nc.vector.scalar_tensor_tensor(gg[:, :], th[:, :], 1.0, bank[2][:, :], ALU.add, ALU.mult) \
                    .then_inc(s_ready, 1)
                dve.wait_ge(s_ready, S.b + 1)
                nc.vector.scalar_tensor_tensor(gg[:, :], gg[:, :], 0.5, bank[3][:, :], ALU.mult, ALU.mult) \
                    .then_inc(gg_ready, 1)

            def last(S):
                outputs(S)
                hidden(S)
                for c in range(UPC, NCH - 1):
                    low(S, c)
                outputs(S, True)

            dve.wait_ge(idxr_in, 16)
            nc.vector.tensor_copy(idxf[:, :], idxr[:, :]).then_inc(idxf_ready, 1)
            dve.wait_ge(idxt_done, 1)
            nc.vector.tensor_copy(idxt[:, :], bank[7][:, 0:NIDX]).then_inc(idxt_ready, 1)
            dve.wait_ge(idxt_ready, 1)
            indices(0)
            turned(0)
            each_block(dve, step, last)
    st5.close()

    st6 = ExitStack()
    yg = [sb(f"yg{i}", [P, 2, D], ctx=st6) for i in range(2)]
    sq6 = sb("sq6", [P, D], ctx=st6)
    yo = [sb(f"yo{i}", [P, D], ctx=st6) for i in range(2)]
    ss6 = sb("ss6", [P, 3, TT], ctx=st6)
    yg_in = [sem(f"yg_in{i}") for i in range(2)]
    yo_stored = [sem(f"yo_stored{i}") for i in range(2)]
    x3_ready, sq6_ready, root6, yo_ready, dve6 = sem("x3_ready"), sem("sq6_ready"), sem("root6"), sem("yo_ready"), sem("dve6")
    yp = O["y_prompt"].rearrange("b (t p) d -> p (b t) d", p=P)
    ysm = O["y_sample"].rearrange("b s d -> (b s) d")

    with nc.Block() as block:
        @block.gpsimd
        def _(pool):
            for t in range(TT):
                if t >= 2:
                    pool.wait_ge(x3_ready, t - 1)
                for k in range(2):
                    pool.indirect_dma_start(yg[t % 2][:, k, :], None, y_d,
                                            bass.IndirectOffsetOnAxis(ap=slot[:, k, t:t + 1], axis=0)) \
                        .then_inc(yg_in[t % 2], 16)

        @block.vector
        def _(dve):
            chain = Chain(dve, dve6)

            def scale_out(t):
                dve.wait_ge(root6, t + 1)
                chain(nc.vector.reciprocal(ss6[:, 2, t:t + 1], ss6[:, 1, t:t + 1]))
                if t >= 2:
                    dve.wait_ge(yo_stored[t % 2], 16 * (t // 2))
                nc.vector.scalar_tensor_tensor(yo[t % 2][:, :], x2[:, t, :], ss6[:, 2, t:t + 1], gf[:, :],
                                               ALU.mult, ALU.mult).then_inc(yo_ready, 1)

            for t in range(TT):
                dve.wait_ge(yg_in[t % 2], 32 * (t // 2 + 1))
                chain(nc.vector.scalar_tensor_tensor(x2[:, t, :], yg[t % 2][:, 0, :], wgt[:, 0, t:t + 1],
                                                     x2[:, t, :], ALU.mult, ALU.add))
                nc.vector.scalar_tensor_tensor(x2[:, t, :], yg[t % 2][:, 1, :], wgt[:, 1, t:t + 1],
                                               x2[:, t, :], ALU.mult, ALU.add).then_inc(x3_ready, 1)
                if t >= 1:
                    scale_out(t - 1)
            scale_out(TT - 1)

        @block.scalar
        def _(act):
            for t in range(TT):
                act.wait_ge(x3_ready, t + 1)
                nc.scalar.activation(sq6[:, :], x2[:, t, :], ACT.Square, accum_out=ss6[:, 0, t:t + 1]) \
                    .then_inc(sq6_ready, 1)
                act.wait_ge(sq6_ready, t + 1)
                nc.scalar.activation(ss6[:, 1, t:t + 1], ss6[:, 0, t:t + 1], ACT.Sqrt, scale=1.0 / D,
                                     bias=eps_t[:, 0:1]).then_inc(root6, 1)

        @block.sync
        def _(sp_):
            sp_.wait_ge(gf_in, 16)
            for t in range(TT):
                sp_.wait_ge(yo_ready, t + 1)
                sp_.dma_start(yp[:, t, :] if t < NQ else ysm, yo[t % 2][:, :]).then_inc(yo_stored[t % 2], 16)
            sp_.wait_ge(yo_stored[0], 48)
            sp_.wait_ge(yo_stored[1], 32)
    st6.close()


_INS = ["x_prompt", "x_sample", "cache_k", "cache_v", "state_conv", "state_rnn", "norm1_g", "w_in",
        "lambda_q1", "lambda_k1", "lambda_q2", "lambda_k2", "subln_g", "w_attn_proj", "conv_w", "conv_b",
        "w_rg_a", "b_rg_a", "w_rg_i", "b_rg_i", "rg_lambda", "w_rnn_proj", "b_gate", "w_out", "norm2_g",
        "w_group", "b_group", "w_router", "b_router", "w1", "w3", "w2", "final_norm_g"]
_OUTS = [("y_prompt", (1, SEQ, D)), ("y_sample", (NS, DS, D)),
         ("new_k_prompt", (1, 1, SEQ, H, 2, DH)), ("new_v_prompt", (1, 1, SEQ, H, DV)),
         ("new_conv_prompt", (1, 1, CW - 1, D)), ("new_rnn_prompt", (1, 1, D)),
         ("new_k_sample", (1, NS, DS, H, 2, DH)), ("new_v_sample", (1, NS, DS, H, DV)),
         ("new_conv_sample", (1, NS, CW - 1, D)), ("new_rnn_sample", (1, NS, D))]


def kernel(**inputs):
    import concourse.bacc as bacc
    from concourse.bass_utils import run_bass_kernel_spmd

    nc = bacc.Bacc("TRN2", target_bir_lowering=False, num_devices=1)
    arrays = {name: np.ascontiguousarray(inputs[name]) for name in _INS}
    arrays["shape_constants"] = shape_constants()
    A = {n: nc.dram_tensor(f"in_{n}", a.shape, mybir.dt.from_np(a.dtype), kind="ExternalInput").ap()
         for n, a in arrays.items()}
    O = {n: nc.dram_tensor(f"out_{n}", s, F32, kind="ExternalOutput").ap() for n, s in _OUTS}
    build(nc, A, O)
    r = run_bass_kernel_spmd(nc, [{f"in_{n}": a for n, a in arrays.items()}], core_ids=[0])
    return tuple(r.results[0][f"out_{n}"] for n, _ in _OUTS)
```

```python
from contextlib import ExitStack

import numpy as np

import concourse.bass as bass
from concourse import mybir

F32 = mybir.dt.float32
I32 = mybir.dt.int32
F32R = mybir.dt.float32r
ACT = mybir.ActivationFunctionType
ALU = mybir.AluOpType
AX = mybir.AxisListType

P = 128
D = 1024
KT = D // P
SEQ, NS, DS, PAST = 512, 8, 16, 256
NQ = SEQ // P
TOK = SEQ + NS * DS
TT = TOK // P
HALF = TOK // 2
H, DH, DV = 8, 64, 128
CW = 4
NG, EG = 4, 4
NE = NG * EG
FE = 512
EPS = 1e-6
LAM0 = 0.8 - 0.6
SCALE = DH ** -0.5
BIG = float(2 ** 100)
KNEW = PAST
SKEYS = PAST + P
NSEL = 2 * TOK
OVMAX = (NSEL - NE) // P
NBLK = NE + OVMAX
NROWS = NBLK + 3
CREDIT = 1
GELU_C = float(np.sqrt(2.0 / np.pi))

R_CW, R_CB, R_BA, R_BI, R_LAM, R_GA, R_GR, R_N1 = 0, 4, 5, 6, 7, 8, 9, 10
NROW = 11
C_SP2 = 11
NCOL = 12

K_ID, K_ONE, K_TRI, K_SEL, K_M0, K_M1, K_MASKQ, K_MASKV, K_IND, K_MST, K_RAMP, K_DOWN, K_TOK = (
    0, 128, 256, 384, 448, 449, 450, 578, 642, 898, 1026, 1154, 1158)
NK = K_TOK + TT


def shape_constants():
    c = np.zeros((P, NK), np.float32)
    p = np.arange(P)
    c[:, K_ID:K_ID + P] = np.eye(P)
    c[:, K_ONE:K_ONE + P] = 1.0
    c[:, K_TRI:K_TRI + P] = p[:, None] < p[None, :]
    b4, m, q = p // 32, (p // 16) % 2, p % 16
    c[p, K_SEL + b4 * 16 + q] = 1.0
    c[:, K_M0] = m == 0
    c[:, K_M1] = m == 1
    c[0, K_MASKQ:K_MASKQ + 64] = 1.0
    c[0, K_MASKV:K_MASKV + 64] = -BIG
    for g in range(2):
        for r in range(P):
            c[4 * g + b4[r], K_IND + g * P + r] = 1.0
    for b in range(NS):
        c[b, K_MST:K_MST + P] = np.where(p // DS == b, 0.0, -BIG)
    c[:, K_RAMP:K_RAMP + P] = p
    c[:, K_DOWN:K_DOWN + 4] = 4 - np.arange(4)
    c[:, K_TOK:K_TOK + TT] = p[:, None] + P * np.arange(TT)
    return c


class Chain:

    def __init__(self, eng, sem, start=0):
        self.eng, self.sem, self.base, self.n = eng, sem, start, 0

    def at(self, base):
        self.base, self.n = base, 0

    def __call__(self, ins):
        self.n += 1
        ins.then_inc(self.sem, 1)
        self.eng.wait_ge(self.sem, self.base + self.n)


def build(nc, A, O):
    top = ExitStack()
    with top:
        def sb(name, shape, dt=F32, ctx=top):
            return ctx.enter_context(nc.sbuf_tensor(name, shape, dt))

        def sem(name):
            return top.enter_context(nc.semaphore(name))

        bank = [top.enter_context(nc.psum_tensor(f"bank{i}", [P, 512], F32)) for i in range(8)]
        cst = sb("cst", [P, NK])
        ident = cst[:, K_ID:K_ID + P]
        ones = cst[:, K_ONE:K_ONE + P]
        pcol = sb("pcol", [P, KT, NCOL])
        scol = sb("scol", [P, KT, 32])
        subln = sb("subln", [P, 1])
        lam = sb("lam", [P, 8])
        neglam, msign = lam[:, 0:1], lam[:, 1:2]
        eps_t = sb("eps_t", [P, 1])

        xn2_d = nc.dram_tensor("xn2_scratch", (TOK, D), F32, kind="Internal").ap()
        y_d = nc.dram_tensor("block_outputs", ((NBLK + 1) * P, D), F32, kind="Internal").ap()

        xp = A["x_prompt"].rearrange("b (t p) d -> p (b t) d", p=P)
        xs = A["x_sample"].rearrange("b s d -> (b s) d")

        on = sb("on", [P, H, NQ, DV])
        mid = ExitStack()
        xh = sb("xh", [P, KT, TOK], F32R, ctx=mid)
        xl = sb("xl", [P, KT, TOK], F32R, ctx=mid)
        early = ExitStack()

        def sbe(name, shape, dt=F32):
            return early.enter_context(nc.sbuf_tensor(name, shape, dt, side="right"))

        raw = [sbe(f"raw{i}", [P, KT, P]) for i in range(2)]
        wh = sbe("wh", [P, KT, 5, P], F32R)
        wl = sbe("wl", [P, KT, 5, P], F32R)
        zcol = sbe("zcol", [P, 1])
        raw_in = [sem(f"raw_in{i}") for i in range(2)]
        highs, split, zcol_set = sem("highs"), sem("split"), sem("zcol_set")
        Q, K, V, XR, GR = range(5)
        ORDER = ((K, 0), (V, 0), (Q, 0), (XR, 0), (GR, 0), (K, 1), (V, 1), (Q, 1))
        EARLY = 3
        w_cols = A["w_in"][0].rearrange("(k p) n -> p k n", p=P)

        def need(eng, s, n):
            if not (isinstance(n, int) and n <= 0):
                eng.wait_ge(s, n)

        def load_tile(eng, n_static, n, j, h):
            refill(eng, raw_in[n_static % 2], split, n - 1)
            eng.dma_start(raw[n_static % 2][:, :, :], w_cols[:, :, j * D:][:, :, bass.ds(h * P, P)]) \
                .then_inc(raw_in[n_static % 2], 16)

        def refill(eng, arrived, s, n):
            if not isinstance(n, int):
                n = nc.snap(n)
                eng.wait_ge(arrived, 16)
            need(eng, s, n)

        def split_tile(pool, n_static, n, c, j):
            r = raw[n_static % 2]
            pool.wait_ge(raw_in[n_static % 2], c * 16)
            nc.gpsimd.tensor_tensor(wh[:, :, j, :], r[:, :, :], zcol[:, 0:1].rearrange("p (a b) -> p a b", a=1)
                                    .to_broadcast([P, KT, P]), ALU.add).then_inc(highs, 1)
            pool.wait_ge(highs, n + 1)
            nc.gpsimd.tensor_tensor(wl[:, :, j, :], r[:, :, :], wh[:, :, j, :].bitcast(F32), ALU.subtract) \
                .then_inc(split, 1)

        st1 = ExitStack()
        xt = sb("xt", [P, TT, D], ctx=st1)
        xn = sb("xn", [P, TT, D], ctx=st1)
        xnT = sb("xnT", [P, KT, TOK], ctx=st1)
        prow = sb("prow", [NROW, D], ctx=st1)
        srow = sb("srow", [32, D], ctx=st1)
        lvec = sb("lvec", [P, 4, DH], ctx=st1)
        ljunk = sb("ljunk", [P, 2, DH], ctx=st1)
        lsum = sb("lsum", [P, 4], ctx=st1)
        sq1 = sb("sq1", [P, D], ctx=st1)
        ss1 = sb("ss1", [P, 2, TT], ctx=st1)
        sp = sb("sp", [P, 6, KT], ctx=st1)

        cst_in, rows_in, lam_in = sem("cst_in"), sem("rows_in"), sem("lam_in")
        x_in = [sem(f"x_in{t}") for t in range(TT)]
        eps_set, squares, roots1 = sem("eps_set"), sem("squares"), sem("roots1")
        xn_ready, cols_turned, cols_out = sem("xn_ready"), sem("cols_turned"), sem("cols_out")
        xn_turned, xnT_out, xh_ready = sem("xn_turned"), sem("xnT_out"), sem("xh_ready")
        lam_dots, lam_exps, sp_in, sp_exp = sem("lam_dots"), sem("lam_exps"), sem("sp_in"), sem("sp_exp")
        dve1 = sem("dve1")

        def part(x, u):
            return x[:, 4 * (u % 2):4 * (u % 2) + 4, u // 2 * P:(u // 2 + 1) * P]

        with nc.Block() as block:
            @block.sync
            def _(sp_):
                sp_.dma_start(cst[:, :], A["shape_constants"]).then_inc(cst_in, 16)
                for r, n, src in ((R_CW, 4, A["conv_w"][0]), (R_CB, 1, A["conv_b"]), (R_BA, 1, A["b_rg_a"]),
                                  (R_BI, 1, A["b_rg_i"]), (R_LAM, 1, A["rg_lambda"]),
                                  (R_GA, 2, A["b_gate"].rearrange("l (g d) -> (l g) d", g=2)),
                                  (R_N1, 1, A["norm1_g"])):
                    sp_.dma_start(prow[r:r + n, :], src).then_inc(rows_in, 16)
                sp_.dma_start(srow[0:24, :], A["state_conv"].rearrange("l b w d -> (l b w) d")).then_inc(rows_in, 16)
                sp_.dma_start(srow[24:32, :], A["state_rnn"][0]).then_inc(rows_in, 16)
                for i, n in enumerate(("lambda_q1", "lambda_k1", "lambda_q2", "lambda_k2")):
                    sp_.dma_start(lvec[:, i, :], A[n].to_broadcast([P, DH])).then_inc(lam_in, 16)
                sp_.dma_start(subln[:, :], A["subln_g"].rearrange("l d -> d l")).then_inc(lam_in, 16)
                for t in range(TT):
                    src = xp[:, t, :] if t < NQ else xs
                    sp_.dma_start(xt[:, t, :], src).then_inc(x_in[t], 16)
                for n, (j, h) in enumerate(ORDER[:EARLY + 1]):
                    load_tile(sp_, n, n, j, h)

            @block.gpsimd
            def _(pool):
                nc.gpsimd.memset(zcol[:, :], 0.0).then_inc(zcol_set, 1)
                pool.wait_ge(zcol_set, 1)
                for n, (j, _) in enumerate(ORDER[:EARLY]):
                    split_tile(pool, n, n, n // 2 + 1, j)

            @block.scalar
            def _(act):
                act.wait_ge(lam_dots, 2)
                nc.scalar.activation(lsum[:, 2:4], lsum[:, 0:2], ACT.Exp).then_inc(lam_exps, 1)
                act.wait_ge(sp_in, 1)
                nc.scalar.activation(sp[:, 1, :], sp[:, 0, :], ACT.Exp).then_inc(sp_exp, 1)
                for t in range(TT):
                    act.wait_ge(x_in[t], 16)
                    nc.scalar.activation(sq1[:, :], xt[:, t, :], ACT.Square, accum_out=ss1[:, 0, t:t + 1]) \
                        .then_inc(squares, 1)
                    act.wait_ge(squares, t + 1)
                act.wait_ge(eps_set, 1)
                nc.scalar.activation(ss1[:, 1, :], ss1[:, 0, :], ACT.Sqrt, scale=1.0 / D,
                                     bias=eps_t[:, 0:1]).then_inc(roots1, 1)
                for u in range(2 * TT):
                    act.wait_ge(xnT_out, u + 1)
                    nc.scalar.activation(part(xh, u), part(xnT, u), ACT.Copy).then_inc(xh_ready, 1)

            @block.vector
            def _(dve):
                chain = Chain(dve, dve1)
                nc.vector.memset(eps_t[:, :], EPS).then_inc(eps_set, 1)
                dve.wait_ge(cols_turned, 1)
                nc.vector.tensor_copy(pcol[:, :, 0:NROW],
                                      bank[0][:, 0:KT * 16].rearrange("p (k r) -> p k r", r=16)[:, :, 0:NROW]) \
                    .then_inc(cols_out, 1)
                nc.vector.tensor_copy(scol[:, :, :], bank[1][:, 0:KT * 32].rearrange("p (k r) -> p k r", r=32)) \
                    .then_inc(cols_out, 1)
                dve.wait_ge(cols_out, 2)
                dve.wait_ge(lam_in, 16 * 5)
                for i in range(2):
                    nc.vector.tensor_tensor_reduce(ljunk[:, i, :], lvec[:, 2 * i, :], lvec[:, 2 * i + 1, :], 1.0, 0.0,
                                                   ALU.mult, ALU.add, lsum[:, i:i + 1]).then_inc(lam_dots, 1)
                chain(nc.vector.tensor_scalar(sp[:, 2, :], pcol[:, :, R_LAM], -1.0, None, ALU.mult))
                nc.vector.tensor_tensor(sp[:, 0, :], sp[:, 2, :], pcol[:, :, R_LAM], ALU.min).then_inc(sp_in, 1)
                chain(nc.vector.tensor_scalar(sp[:, 2, :], sp[:, 2, :], 0.0, 2.0, ALU.max, ALU.mult))
                dve.wait_ge(sp_exp, 1)
                chain(nc.vector.tensor_scalar(sp[:, 3, :], sp[:, 1, :], 2.0, None, ALU.add))
                chain(nc.vector.reciprocal(sp[:, 3, :], sp[:, 3, :]))
                chain(nc.vector.tensor_tensor(sp[:, 3, :], sp[:, 3, :], sp[:, 1, :], ALU.mult))
                chain(nc.vector.tensor_tensor(sp[:, 4, :], sp[:, 3, :], sp[:, 3, :], ALU.mult))
                chain(nc.vector.tensor_scalar(sp[:, 5, :], sp[:, 4, :], 1.0 / 19, 1.0 / 17, ALU.mult, ALU.add))
                for n in range(15, 0, -2):
                    chain(nc.vector.tensor_tensor(sp[:, 5, :], sp[:, 5, :], sp[:, 4, :], ALU.mult))
                    chain(nc.vector.tensor_scalar(sp[:, 5, :], sp[:, 5, :], 1.0 / n, None, ALU.add))
                chain(nc.vector.tensor_tensor(sp[:, 5, :], sp[:, 5, :], sp[:, 3, :], ALU.mult))
                nc.vector.scalar_tensor_tensor(pcol[:, :, C_SP2], sp[:, 5, :], 4.0, sp[:, 2, :], ALU.mult, ALU.add)
                nc.vector.tensor_scalar(pcol[:, :, R_BA:R_BI + 1], pcol[:, :, R_BA:R_BI + 1], 0.5, None, ALU.mult)
                nc.vector.tensor_scalar(pcol[:, :, R_GA:R_GR + 1], pcol[:, :, R_GA:R_GR + 1], 0.5, None, ALU.mult)
                nc.vector.tensor_scalar(subln[:, :], subln[:, :], 1.0 - LAM0, None, ALU.mult)
                dve.wait_ge(lam_exps, 1)
                chain(nc.vector.tensor_tensor(neglam, lsum[:, 3:4], lsum[:, 2:3], ALU.subtract))
                chain(nc.vector.tensor_scalar(neglam, neglam, -LAM0, None, ALU.add))
                dve.wait_ge(cst_in, 16)
                chain(nc.vector.scalar_tensor_tensor(msign, cst[:, K_M1:K_M1 + 1], neglam, cst[:, K_M0:K_M0 + 1],
                                                     ALU.mult, ALU.add))
                dve.wait_ge(roots1, 1)
                chain(nc.vector.reciprocal(ss1[:, 0, :], ss1[:, 1, :]))
                for t in range(TT):
                    nc.vector.tensor_scalar(xn[:, t, :], xt[:, t, :], ss1[:, 0, t:t + 1], None, ALU.mult) \
                        .then_inc(xn_ready, 1)

                def low(u):
                    dve.wait_ge(xh_ready, u + 1)
                    nc.vector.tensor_tensor(part(xl, u), part(xnT, u), part(xh, u).bitcast(F32), ALU.subtract)

                for u in range(2 * TT):
                    half = u % 2
                    dve.wait_ge(xn_turned, u + 1)
                    nc.vector.tensor_tensor(
                        part(xnT, u), bank[2 + u % 4][:, :].rearrange("p (k q) -> p k q", q=P),
                        pcol[:, 4 * half:4 * half + 4, R_N1:R_N1 + 1].to_broadcast([P, 4, P]),
                        ALU.mult).then_inc(xnT_out, 1)
                    if u >= 1:
                        low(u - 1)
                low(2 * TT - 1)

            @block.tensor
            def _(pe):
                pe.wait_ge(cst_in, 16)
                pe.wait_ge(rows_in, 16 * 9)
                for k in range(KT):
                    nc.tensor.transpose(bank[0][:, 16 * k:16 * k + NROW], prow[:, k * P:(k + 1) * P],
                                        ident[0:NROW, 0:NROW])
                    last = nc.tensor.transpose(bank[1][:, 32 * k:32 * k + 32], srow[:, k * P:(k + 1) * P],
                                               ident[0:32, 0:32])
                last.then_inc(cols_turned, 1)
                for t in range(TT):
                    pe.wait_ge(xn_ready, t + 1)
                    for half in range(2):
                        u = 2 * t + half
                        if u >= 4:
                            pe.wait_ge(xnT_out, u - 3)
                        for k in range(4):
                            last = nc.tensor.transpose(bank[2 + u % 4][:, k * P:(k + 1) * P],
                                                       xn[:, t, (4 * half + k) * P:(4 * half + k + 1) * P], ident)
                        last.then_inc(xn_turned, 1)
        st1.close()

        yT = sb("yT", [P, KT, TOK], ctx=mid)
        oTs = sb("oTs", [P, H, P], ctx=mid)
        stc = sb("stc", [P, KT, 36], ctx=mid)
        tail = ExitStack()
        oraw = sb("oraw", [P, NQ, DV], ctx=tail)
        oms = sb("oms", [P, 4 * NQ], ctx=tail)
        thr = sb("thr", [P, TOK], ctx=tail)
        thi = sb("thi", [P, TOK], ctx=tail)
        gr = [sb(f"gr{i}", [P, TOK], ctx=tail) for i in range(2)]
        gw = sb("gw", [P, TOK], ctx=tail)
        ra = sb("ra", [P, TOK], ctx=tail)
        rw = sb("rw", [P, TOK], ctx=tail)
        h0t = sb("h0t", [P, NS], ctx=tail)
        hcol = [sb(f"hcol{i}", [P, NCOL + 32], ctx=tail) for i in range(2)]
        st2 = ExitStack()
        wrg = [sb(f"wrg{i}", [P, 2, P], ctx=st2) for i in range(2)]
        kc = sb("kc", [P, NS * 2, P], ctx=st2)
        vc = sb("vc", [P, NS * 2, P], ctx=st2)
        kvt = sb("kvt", [P, 3, TT, P], ctx=st2)
        qT = sb("qT", [P, TOK], ctx=st2)
        kT = sb("kT", [P, TOK], ctx=st2)
        qbd = sb("qbd", [P, NS, 2, DS], ctx=st2)
        ebuf = [sb(f"ebuf{i}", [P, 2, 512], ctx=st2) for i in range(2)]
        wT = [sb(f"wT{i}", [P, 512], ctx=st2) for i in range(2)]
        wTs = sb("wTs", [P, 3, P], ctx=st2)
        selc = sb("selc", [P, 2, 64], ctx=st2)
        stat = sb("stat", [P, 5, 10], ctx=st2)
        osq = ebuf[0][:, 1, :].rearrange("p (t c) -> p t c", c=DV)
        xpad = sb("xpad", [P, 3 + SEQ], ctx=st2)
        spad = sb("spad", [P, NS, 3 + DS], ctx=st2)
        xc = sb("xc", [P, TOK], ctx=st2)
        rh = thr

        kc_in, vc_in = sem("kc_in"), sem("vc_in")
        col_in = [sem(f"col_in{i}") for i in range(2)]
        kv_stored = sem("kv_stored")
        pr_done, pr_act, pr_dve = sem("pr_done"), sem("pr_act"), sem("pr_dve")
        pt_done, pt_out = sem("pt_done"), sem("pt_out")
        ss_done, sc_done, max_ready, exp_done = sem("ss_done"), sem("sc_done"), sem("max_ready"), sem("exp_done")
        selc_ready, comb_ready = sem("selc_ready"), sem("comb_ready")
        os_done, os_out, op_done, op_out = sem("os_done"), sem("os_out"), sem("op_done"), sem("op_out")
        conv_done, gcube, gtanh = sem("conv_done"), sem("gcube"), sem("gtanh")
        decay, ms_ready, roots2, rnn_done = sem("decay"), sem("ms_ready"), sem("roots2"), sem("rnn_done")
        init2, dve2 = sem("init2"), sem("dve2")
        BODY_STEPS, TAIL_STEPS = 22, 10
        STEPS2 = H * (BODY_STEPS + TAIL_STEPS)

        UNITS = ["xr0", "xr1", "kv0", "kv1", "kv2", "gr0", "gr1", "kv3", "kv4", "ra0", "ra1", "ri0", "ri1",
                 "q0", "q1", "kT0", "kT1", "kT2"]
        AHEAD = [u for u in UNITS if u[0] in "kq"]
        LAST = [u for u in UNITS if u[0] not in "kq"]
        RING = 3
        assert len(UNITS) % RING == 0
        NT = 9

        def by_act(units):
            return [u for u in units if u[:2] not in ("kv", "xr")]

        def by_dve(units):
            return [u for u in units if u[:2] in ("kv", "xr")]

        class Step:
            def __init__(self, i, h0, ahead=False):
                self.i, self.h0, self.par, self.h = i, h0, h0 % 2, i * 2 + h0
                self.first, self.last = isinstance(self.h, int) and self.h == 0, isinstance(self.h, int) and self.h == H - 1
                self.units = AHEAD if ahead else LAST if self.last else UNITS
                h = self.h
                self.u0 = 0 if ahead else h * len(UNITS) + len(AHEAD)
                self.a0 = 0 if ahead else h * len(by_act(UNITS)) + len(by_act(AHEAD))
                self.d0 = 0 if ahead else h * len(by_dve(UNITS)) + len(by_dve(AHEAD))
                self.before = [] if ahead else AHEAD if self.first else UNITS
                self.shift = 0 if ahead else len(AHEAD)

            def bank(self, name):
                return bank[(self.shift + self.units.index(name)) % RING]

            def done(self, eng, name):
                eng.wait_ge(pr_done, self.u0 + (self.units.index(name) + 1))

            def out(self, eng, name):
                for on_, s, n0 in ((by_act, pr_act, self.a0), (by_dve, pr_dve, self.d0)):
                    if name in on_(self.units):
                        eng.wait_ge(s, n0 + (on_(self.units).index(name) + 1))

            def free(self, eng, name):
                n = self.units.index(name) - RING
                if n >= 0:
                    self.out(eng, self.units[n])
                elif self.before:
                    old = self.before[n]
                    for on_, s, n0 in ((by_act, pr_act, self.a0), (by_dve, pr_dve, self.d0)):
                        if old in on_(self.before):
                            eng.wait_ge(s, n0 - (len(on_(self.before)) - on_(self.before).index(old) - 1))

        AHEAD_STEP, FIRST, FINAL = Step(0, 0, ahead=True), Step(0, 0), Step(0, H - 1)

        STEP_ORDER = ((XR, 1, "xr1"), (GR, 1, "gr1"), (K, 2, "kv4"), (V, 2, "kv4"), (Q, 2, "q1"))

        def tail_a(dve, chain, h):
            dve.wait_ge(decay, h + 1)
            chain(nc.vector.tensor_scalar(thr[:, :], ra[:, :], 1.0, None, ALU.add))
            chain(nc.vector.reciprocal(thr[:, :], thr[:, :]))
            dve.wait_ge(roots2, h * 2 + 1)
            nc.vector.tensor_scalar(ra[:, :], thr[:, :], 2.0, -1.0, ALU.mult, ALU.add)
            chain(nc.vector.tensor_tensor(rw[:, :], rw[:, :], thr[:, :], ALU.mult))
            chain(nc.vector.tensor_tensor(rw[:, :], rw[:, :], thi[:, :], ALU.mult))

        def tail_b(chain, h, par):
            a0 = ra[:, SEQ:TOK].rearrange("p (b q) -> p b q", q=DS)[:, :, 0]
            b0 = rw[:, SEQ:TOK].rearrange("p (b q) -> p b q", q=DS)[:, :, 0]
            chain(nc.vector.tensor_tensor(h0t[:, :], a0, hcol[par][:, NCOL + 24:NCOL + 32], ALU.mult))
            nc.vector.tensor_tensor(b0, b0, h0t[:, :], ALU.add)
            chain(nc.vector.memset(a0, 0.0))
            chain(nc.vector.tensor_tensor_scan(rh[:, :], ra[:, :], rw[:, :], 0.0, ALU.mult, ALU.add))
            nc.vector.tensor_scalar(stc[:, bass.ds(h, 1), 27:28], rh[:, SEQ - 1:SEQ]
                                    .rearrange("p (o c) -> p o c", o=1), 1.0, None, ALU.mult)
            nc.vector.tensor_scalar(
                stc[:, bass.ds(h, 1), 28:36],
                rh[:, SEQ:TOK].rearrange("p (o b q) -> p o b q", o=1, q=DS)[:, :, :, DS - 1],
                1.0, None, ALU.mult)

        def tail_c(dve, chain, h, par):
            dve.wait_ge(gtanh, h + 1)
            chain(nc.vector.scalar_tensor_tensor(gw[:, :], gw[:, :], 1.0, gr[par][:, :], ALU.add, ALU.mult))
            chain(nc.vector.scalar_tensor_tensor(
                yT[:, bass.ds(h, 1), :], rh[:, :].rearrange("p (o c) -> p o c", o=1), 0.5,
                gw[:, :].rearrange("p (o c) -> p o c", o=1), ALU.mult, ALU.mult))

        def norm_attention(dve, chain, h):
            dve.wait_ge(roots2, h * 2 + 2)
            chain(nc.vector.reciprocal(oms[:, 2 * NQ:3 * NQ], oms[:, NQ:2 * NQ]))
            nc.vector.tensor_tensor(
                on[:, bass.ds(h, 1), :, :].rearrange("p o t c -> p (o t) c"), oraw[:, :, :],
                oms[:, 2 * NQ:3 * NQ].rearrange("p (t o) -> p t o", o=1).to_broadcast([P, NQ, DV]),
                ALU.mult).then_inc(rnn_done, 1)

        with nc.Block() as block:
            @block.sync
            def _(sp_):
                def load_columns(h, par):
                    sp_.dma_start(hcol[par][:, 0:NCOL], pcol[:, bass.ds(h, 1), :].rearrange("p o c -> p (o c)")) \
                        .then_inc(col_in[par], 16)
                    sp_.dma_start(hcol[par][:, NCOL:], scol[:, bass.ds(h, 1), :].rearrange("p o c -> p (o c)")) \
                        .then_inc(col_in[par], 16)
                    for j, n in enumerate(("w_rg_a", "w_rg_i")):
                        sp_.dma_start(wrg[par][:, j, :], A[n][0, bass.ds(h, 1)].rearrange("o i j -> i (o j)")) \
                            .then_inc(col_in[par], 16)

                def load_cache(h, dst, src, s):
                    sp_.dma_start(dst[:, :, :], src.rearrange("b (k p) c -> p (b k) c", p=P)[:, :, bass.ds(h * P, P)]) \
                        .then_inc(s, 16)

                def store_kv(h, par):
                    for j, n in ((0, "k"), (1 + par, "v")):
                        outp, outs = O[f"new_{n}_prompt"][0, 0], O[f"new_{n}_sample"][0]
                        if n == "k":
                            outp, outs = outp.rearrange("s h m d -> s h (m d)"), outs.rearrange("b s h m d -> b s h (m d)")
                        outp = outp.rearrange("(t p) h c -> p t (h c)", p=P)
                        outs = outs.rearrange("b s h c -> (b s) (h c)")
                        sp_.dma_start(outp[:, :, bass.ds(h * P, P)], kvt[:, j, 0:NQ, :]).then_inc(kv_stored, 16)
                        sp_.dma_start(outs[:, bass.ds(h * P, P)], kvt[:, j, NQ, :]).then_inc(kv_stored, 16)

                k_src = A["cache_k"][0].rearrange("b s h m d -> b s (h m d)")
                v_src = A["cache_v"][0].rearrange("b s h d -> b s (h d)")

                def body(S):
                    h, par = S.h, S.par
                    if not S.last:
                        n = 5 * h + 8
                        ns = 5 * S.h0
                        load_tile(sp_, ns + 0, n, XR, h + 1)
                        refill(sp_, kc_in, ss_done, h + 1)
                        load_cache(h + 1, kc, k_src, kc_in)
                        need(sp_, rnn_done, h)
                        load_columns(h + 1, 1 - par)
                        refill(sp_, vc_in, os_done, h + 1)
                        load_cache(h + 1, vc, v_src, vc_in)
                        load_tile(sp_, ns + 1, n + 1, GR, h + 1)
                        S.out(sp_, "kv4")

                        store_kv(h + 1, 1 - par)

                        def ahead():
                            for x, j in enumerate((K, V, Q)):
                                load_tile(sp_, ns + 2 + x, n + (2 + x), j, h + 2)
                        if S.h0 == 2:
                            with sp_.If(S.i < H // 2 - 2):
                                ahead()
                        else:
                            ahead()

                load_columns(0, 0)
                load_cache(0, kc, k_src, kc_in)
                for n, (j, h) in enumerate(ORDER):
                    if n > EARLY:
                        load_tile(sp_, n, n, j, h)
                load_cache(0, vc, v_src, vc_in)
                AHEAD_STEP.out(sp_, "kv4")
                store_kv(0, 0)
                body(FIRST)
                with sp_.Fori(0, H // 2 - 1) as i:
                    body(Step(i, 1))
                    body(Step(i, 2))
                sp_.wait_ge(kv_stored, 64 * H)

            @block.gpsimd
            def _(pool):
                def body(S):
                    if S.last:
                        return

                    def tiles(x0, x1):
                        for x in range(x0, x1):
                            j, _, unit = STEP_ORDER[x]
                            S.done(pool, unit)
                            split_tile(pool, 5 * S.h0 + x, S.h * 5 + (8 + x), 5 * S.i + ((8 + 5 * S.h0 + x) // 2 + 1), j)
                    tiles(0, 2)
                    if S.h0 == 2:
                        with pool.If(S.i < H // 2 - 2):
                            tiles(2, 5)
                    else:
                        tiles(2, 5)

                nc.gpsimd.memset(qbd[:, :, :, :], 0.0).then_inc(init2, 1)
                nc.gpsimd.memset(xpad[:, 0:3], 0.0).then_inc(init2, 1)
                pool.wait_ge(init2, 2)
                for n, (j, h) in enumerate(ORDER):
                    if n >= 5:
                        AHEAD_STEP.done(pool, "kv4" if j != Q else "q1")
                    if n >= EARLY:
                        split_tile(pool, n, n, n // 2 + 1, j)
                body(FIRST)
                with pool.Fori(0, H // 2 - 1) as i:
                    body(Step(i, 1))
                    body(Step(i, 2))

            @block.tensor
            def _(pe):
                def product(out, pairs):
                    for k, (ah, al, bh, bl) in enumerate(pairs):
                        nc.tensor.matmul(out, ah, bh, start=(k == 0), stop=False)
                        nc.tensor.matmul(out, ah, bl, start=False, stop=False)
                        mm = nc.tensor.matmul(out, al, bh, start=False, stop=(k == len(pairs) - 1))
                    mm.then_inc(pr_done, 1)

                def features(S, name, j):
                    half = int(name[-1])
                    s = slice(half * HALF, (half + 1) * HALF)
                    S.free(pe, name)
                    product(S.bank(name)[:, 0:HALF],
                            [(wh[:, k, j, :], wl[:, k, j, :], xh[:, k, s], xl[:, k, s]) for k in range(KT)])

                def keys_values(S, name):
                    s = slice(int(name[2]) * P, int(name[2]) * P + P)
                    S.free(pe, name)
                    product(S.bank(name)[:, 0:2 * P],
                            [(xh[:, k, s], xl[:, k, s], wh[:, k, K:V + 1, :], wl[:, k, K:V + 1, :])
                             for k in range(KT)])

                def turn_keys(S):
                    for n, ts in enumerate(((0, 1), (2, 3), (4,))):
                        S.free(pe, f"kT{n}")
                        S.out(pe, f"kv{ts[-1]}")
                        for t in ts:
                            mm = nc.tensor.transpose(S.bank(f"kT{n}")[:, (t % 2) * P:(t % 2 + 1) * P],
                                                     kvt[:, 0, t, :], ident)
                        mm.then_inc(pr_done, 1)

                def tbank(S, u):
                    return bank[5 + (S.par * NT + u) % 2]

                def turn_bank(S, u):
                    need(pe, pt_out, S.h * NT + (u - 1))
                    return tbank(S, u)

                def turn_weights(S, qt):
                    pe.wait_ge(comb_ready, S.h * NQ + (qt + 1))
                    b = turn_bank(S, 5 + qt)
                    for k in range(qt + 1):
                        mm = nc.tensor.transpose(b[:, k * P:(k + 1) * P],
                                                 ebuf[(qt + 1) % 2][:, 0, k * P:(k + 1) * P], ident)
                    mm.then_inc(pt_done, 1)

                def values(S, qt):
                    pe.wait_ge(pt_out, S.h * NT + (6 + qt))
                    if qt == 0:
                        pe.wait_ge(os_out, S.h + 1)
                    for k in range(qt + 1):
                        mm = nc.tensor.matmul(bank[7][:, qt * P:(qt + 1) * P], wT[qt % 2][:, k * P:(k + 1) * P],
                                              kvt[:, 1 + S.par, k, :], start=(k == 0), stop=(k == qt))
                    if qt == NQ - 1:
                        mm.then_inc(op_done, 1)

                def scores(S, qt):
                    n = (qt + 1) * P
                    pe.wait_ge(exp_done, S.h * 5 + (qt + 1))
                    for m in range(2):
                        rows = slice(m * DH, (m + 1) * DH)
                        nc.tensor.matmul(bank[3 + m][:, 0:n], qT[rows, qt * P:(qt + 1) * P], kT[rows, 0:n],
                                         start=True, stop=False)
                        mm = nc.tensor.matmul(bank[3 + m][:, n - 64:n], cst[0:1, K_MASKQ:K_MASKQ + P],
                                              cst[0:1, K_MASKV:K_MASKV + 64], start=False, stop=True)
                    mm.then_inc(sc_done, 1)

                def body(S):
                    h, par, n = S.h, S.par, S.h * 5
                    ahead = not S.last
                    pe.wait_ge(kc_in, h * 16 + 16)
                    for u in range(4):
                        b = turn_bank(S, u)
                        for x in range(4):
                            mm = nc.tensor.transpose(b[:, x * P:(x + 1) * P], kc[:, 4 * u + x, :], ident)
                        mm.then_inc(pt_done, 1)
                    if S.first:
                        AHEAD_STEP.out(pe, "kT2")
                    else:
                        pe.wait_ge(pr_act, S.a0)
                    need(pe, exp_done, h * 5)
                    for g in range(2):
                        nc.tensor.matmul(bank[3 + g][:, KNEW:SKEYS],
                                         qbd[:, 4 * g:4 * g + 4, :, :].rearrange("p b m q -> p (b m q)"),
                                         kT[:, SEQ:TOK], start=True, stop=False)
                        nc.tensor.matmul(bank[3 + g][:, KNEW:SKEYS], cst[0:NS, K_IND + g * P:K_IND + (g + 1) * P],
                                         cst[0:NS, K_MST:K_MST + P], start=False, stop=True)
                    pe.wait_ge(pt_out, h * NT + 4)
                    for b in range(NS):
                        r = 32 * (b % 4)
                        mm = nc.tensor.matmul(bank[3 + b // 4][r:r + 32, 0:PAST],
                                              qbd[:, b, :, :].rearrange("p m q -> p (m q)"),
                                              kc[:, 2 * b:2 * b + 2, :].rearrange("p k c -> p (k c)"),
                                              start=True, stop=True)
                    mm.then_inc(ss_done, 1)
                    pe.wait_ge(split, n + 4)
                    features(S, "xr0", XR)
                    features(S, "xr1", XR)
                    pe.wait_ge(selc_ready, h + 1)
                    tb = turn_bank(S, 4)
                    for k in range(3):
                        for g in range(2):
                            mm = nc.tensor.matmul(tb[:, k * P + g * 64:k * P + g * 64 + 64],
                                                  ebuf[0][:, g, k * P:(k + 1) * P], selc[:, g, :],
                                                  start=True, stop=True)
                    mm.then_inc(pt_done, 1)
                    scores(S, 0)
                    if ahead:
                        pe.wait_ge(split, n + 7)
                        keys_values(S, "kv0")
                    pe.wait_ge(pt_out, h * NT + 5)
                    pe.wait_ge(vc_in, h * 16 + 16)
                    need(pe, op_out, h)
                    nc.tensor.matmul(bank[7][:, 0:P], kvt[:, 1 + par, NQ, :], wTs[:, 2, :], start=True, stop=True)
                    for b in range(NS):
                        for k in range(2):
                            mm = nc.tensor.matmul(bank[7][:, b * DS:(b + 1) * DS], vc[:, 2 * b + k, :],
                                                  wTs[:, k, b * DS:(b + 1) * DS], start=False,
                                                  stop=True, skip_group_check=True)
                    mm.then_inc(os_done, 1)
                    if ahead:
                        keys_values(S, "kv1")
                        keys_values(S, "kv2")
                    turn_weights(S, 0)
                    scores(S, 1)
                    pe.wait_ge(split, n + 5)
                    features(S, "gr0", GR)
                    values(S, 0)
                    turn_weights(S, 1)
                    scores(S, 2)
                    features(S, "gr1", GR)
                    values(S, 1)
                    if ahead:
                        keys_values(S, "kv3")
                    turn_weights(S, 2)
                    scores(S, 3)
                    if ahead:
                        keys_values(S, "kv4")
                    pe.wait_ge(conv_done, h + 1)
                    for j, name in enumerate(("ra0", "ra1", "ri0", "ri1")):
                        S.free(pe, name)
                        nc.tensor.matmul(S.bank(name)[:, 0:HALF], wrg[par][:, j // 2, :],
                                         xc[:, (j % 2) * HALF:(j % 2 + 1) * HALF],
                                         start=True, stop=True).then_inc(pr_done, 1)
                    values(S, 2)
                    if ahead:
                        pe.wait_ge(split, n + 8)
                        features(S, "q0", Q)
                        features(S, "q1", Q)
                    turn_weights(S, 3)
                    if ahead:
                        turn_keys(S)
                    values(S, 3)

                pe.wait_ge(init2, 2)
                pe.wait_ge(split, 2)
                for t in range(TT):
                    keys_values(AHEAD_STEP, f"kv{t}")
                pe.wait_ge(split, 3)
                features(AHEAD_STEP, "q0", Q)
                features(AHEAD_STEP, "q1", Q)
                turn_keys(AHEAD_STEP)
                body(FIRST)
                with pe.Fori(0, H // 2 - 1) as i:
                    body(Step(i, 1))
                    body(Step(i, 2))
                body(FINAL)

            @block.scalar
            def _(act):
                def softmax_exp(S, u, n):
                    act.wait_ge(max_ready, S.h * 5 + (u + 1))
                    for m in range(2):
                        ins = nc.scalar.activation(ebuf[u % 2][:, m, 0:n], bank[3 + m][:, 0:n], ACT.Exp,
                                                   bias=stat[:, u, 2 + m:3 + m], scale=SCALE,
                                                   accum_out=stat[:, u, 4 + m:5 + m])
                    ins.then_inc(exp_done, 1)

                def turned(S, u, out, n):
                    act.wait_ge(pt_done, S.h * NT + (u + 1))
                    nc.scalar.activation(out, bank[5 + (S.par * NT + u) % 2][:, 0:n], ACT.Copy).then_inc(pt_out, 1)

                def queries(S):
                    S.done(act, "q0")
                    nc.scalar.activation(qT[:, 0:HALF], S.bank("q0")[:, 0:HALF], ACT.Copy).then_inc(pr_act, 1)
                    S.done(act, "q1")
                    qs = S.bank("q1")[:, SEQ - HALF:HALF].rearrange("p (b q) -> p b q", q=DS)
                    for m in range(2):
                        rows = slice(m * DH, (m + 1) * DH)
                        nc.scalar.activation(qbd[rows, :, m, :], qs[rows], ACT.Copy)
                    nc.scalar.activation(qT[:, HALF:TOK], S.bank("q1")[:, 0:HALF], ACT.Copy).then_inc(pr_act, 1)

                def keys(S):
                    for n, (c0, c1) in enumerate(((0, 256), (256, 512), (512, 640))):
                        S.done(act, f"kT{n}")
                        nc.scalar.activation(kT[:, c0:c1], S.bank(f"kT{n}")[:, 0:c1 - c0], ACT.Copy) \
                            .then_inc(pr_act, 1)

                def tail(h, par):
                    nc.scalar.activation(ra[:, :], thr[:, :], ACT.Tanh, bias=hcol[par][:, C_SP2:C_SP2 + 1],
                                         scale=hcol[par][:, C_SP2:C_SP2 + 1]).then_inc(decay, 1)
                    act.wait_ge(gcube, h + 1)
                    nc.scalar.activation(gw[:, :], gw[:, :], ACT.Tanh, scale=GELU_C).then_inc(gtanh, 1)
                    act.wait_ge(decay, h + 1)
                    nc.scalar.activation(rw[:, :], ra[:, :], ACT.Sqrt).then_inc(roots2, 1)
                    act.wait_ge(ms_ready, h + 1)
                    nc.scalar.activation(oms[:, NQ:2 * NQ], oms[:, 0:NQ], ACT.Sqrt, scale=1.0 / DV,
                                         bias=eps_t[:, 0:1]).then_inc(roots2, 1)

                def body(S):
                    h, par = S.h, S.par
                    for u in range(4):
                        turned(S, u, kc[:, 4 * u:4 * u + 4, :].rearrange("p b k -> p (b k)"), 512)
                    act.wait_ge(ss_done, h + 1)
                    softmax_exp(S, 0, SKEYS)
                    if not S.first:
                        tail(h - 1, 1 - par)
                    turned(S, 4, wTs[:, :, :].rearrange("p k q -> p (k q)"), 3 * P)
                    softmax_exp(S, 1, P)
                    turned(S, 5, wT[0][:, 0:P], P)
                    softmax_exp(S, 2, 2 * P)
                    for half in range(2):
                        S.done(act, f"gr{half}")
                        nc.scalar.activation(gr[par][:, half * HALF:(half + 1) * HALF],
                                             S.bank(f"gr{half}")[:, 0:HALF], ACT.Copy).then_inc(pr_act, 1)
                        if half == 0:
                            turned(S, 6, wT[1][:, 0:2 * P], 2 * P)
                            softmax_exp(S, 3, 3 * P)
                    turned(S, 7, wT[0][:, 0:3 * P], 3 * P)
                    softmax_exp(S, 4, 4 * P)
                    act.wait_ge(col_in[par], S.i * 64 + (S.h0 // 2 * 64 + 64))
                    need(act, rnn_done, h)
                    for name, out, c in (("ra0", thr, R_BA), ("ra1", thr, R_BA), ("ri0", thi, R_BI), ("ri1", thi, R_BI)):
                        S.done(act, name)
                        s = slice(HALF * int(name[2]), HALF * int(name[2]) + HALF)
                        nc.scalar.activation(out[:, s], S.bank(name)[:, 0:HALF], ACT.Tanh,
                                             bias=hcol[par][:, c:c + 1], scale=0.5).then_inc(pr_act, 1)
                    if not S.last:
                        queries(S)
                    turned(S, 8, wT[1][:, 0:4 * P], 4 * P)
                    if not S.last:
                        keys(S)
                    else:
                        S.out(act, "ri1")

                act.wait_ge(init2, 2)
                queries(AHEAD_STEP)
                keys(AHEAD_STEP)
                body(FIRST)
                with act.Fori(0, H // 2 - 1) as i:
                    body(Step(i, 1))
                    body(Step(i, 2))
                body(FINAL)
                tail(H - 1, 1)

            @block.vector
            def _(dve):
                chain = Chain(dve, dve2)

                def row_max(S, u, n):
                    for m in range(2):
                        ins = nc.vector.tensor_reduce(stat[:, u, m:m + 1], bank[3 + m][:, 0:n], AX.X, ALU.max)
                    chain(ins)
                    nc.vector.tensor_scalar(stat[:, u, 2:4], stat[:, u, 0:2], -SCALE, None, ALU.mult) \
                        .then_inc(max_ready, 1)

                def prompt_max(S, qt):
                    dve.wait_ge(sc_done, S.h * NQ + (qt + 1))
                    row_max(S, qt + 1, (qt + 1) * P)

                def combine(S, qt):
                    u = qt + 1
                    n = (qt + 1) * P
                    dve.wait_ge(exp_done, S.h * 5 + (u + 1))
                    chain(nc.vector.reciprocal(stat[:, u, 6:8], stat[:, u, 4:6]))
                    chain(nc.vector.scalar_tensor_tensor(stat[:, u, 8:9], stat[:, u, 4:5], stat[:, u, 7:8], neglam,
                                                         ALU.mult, ALU.mult))
                    nc.vector.scalar_tensor_tensor(ebuf[u % 2][:, 0, 0:n], ebuf[u % 2][:, 1, 0:n], stat[:, u, 8:9],
                                                   ebuf[u % 2][:, 0, 0:n], ALU.mult, ALU.add).then_inc(comb_ready, 1)

                def copy_kv(S, t, par, h):
                    S.done(dve, f"kv{t}")
                    if t == 0:
                        need(dve, kv_stored, h * 64)
                    nc.vector.tensor_copy(kvt[:, 0:2 + par:1 + par, t, :],
                                          S.bank(f"kv{t}")[:, 0:2 * P].rearrange("p (j c) -> p j c", c=P)) \
                        .then_inc(pr_dve, 1)

                def conv(S):
                    cw = hcol[S.par]
                    xcs = xc[:, SEQ:TOK].rearrange("p (b q) -> p b q", q=DS)
                    for j in range(CW):
                        if j == 0:
                            nc.vector.tensor_scalar(xc[:, 0:SEQ], xpad[:, 0:SEQ], cw[:, R_CW:R_CW + 1],
                                                    cw[:, R_CB:R_CB + 1], ALU.mult, ALU.add)
                            chain(nc.vector.tensor_scalar(xcs, spad[:, :, 0:DS], cw[:, R_CW:R_CW + 1],
                                                          cw[:, R_CB:R_CB + 1], ALU.mult, ALU.add))
                            continue
                        nc.vector.scalar_tensor_tensor(xc[:, 0:SEQ], xpad[:, j:j + SEQ], cw[:, j:j + 1],
                                                       xc[:, 0:SEQ], ALU.mult, ALU.add)
                        ins = nc.vector.scalar_tensor_tensor(xcs, spad[:, :, j:j + DS], cw[:, j:j + 1],
                                                             xcs, ALU.mult, ALU.add)
                        if j < CW - 1:
                            chain(ins)
                        else:
                            ins.then_inc(conv_done, 1)

                def body(S):
                    h, par = S.h, S.par
                    base = 0 if S.first else h * (BODY_STEPS + TAIL_STEPS) - TAIL_STEPS
                    chain.at(base)
                    dve.wait_ge(ss_done, h + 1)
                    row_max(S, 0, SKEYS)
                    S.done(dve, "xr0")
                    nc.vector.tensor_copy(xpad[:, 3:3 + HALF], S.bank("xr0")[:, 0:HALF]).then_inc(pr_dve, 1)
                    dve.wait_ge(exp_done, h * 5 + 1)
                    chain(nc.vector.reciprocal(stat[:, 0, 6:8], stat[:, 0, 4:6]))
                    chain(nc.vector.tensor_scalar(stat[:, 0, 8:10], stat[:, 0, 6:8], msign, None, ALU.mult))
                    for g in range(2):
                        ins = nc.vector.tensor_scalar(selc[:, g, :], cst[:, K_SEL:K_SEL + 64],
                                                      stat[:, 0, 8 + g:9 + g], None, ALU.mult)
                    ins.then_inc(selc_ready, 1)
                    S.done(dve, "xr1")
                    nc.vector.tensor_copy(xpad[:, 3 + HALF:3 + SEQ], S.bank("xr1")[:, 0:SEQ - HALF])
                    nc.vector.tensor_copy(spad[:, :, 3:], S.bank("xr1")[:, SEQ - HALF:HALF]
                                          .rearrange("p (b q) -> p b q", q=DS)).then_inc(pr_dve, 1)
                    dve.wait_ge(col_in[par], S.i * 64 + (S.h0 // 2 * 64 + 64))
                    chain(nc.vector.tensor_copy(spad[:, :, 0:3],
                                                hcol[par][:, NCOL:NCOL + 24].rearrange("p (b w) -> p b w", w=3)))
                    prompt_max(S, 0)
                    if not S.first:
                        tail_a(dve, chain, h - 1)
                    if not S.last:
                        copy_kv(S, 0, 1 - par, h + 1)
                    dve.wait_ge(os_done, h + 1)
                    nc.vector.tensor_scalar(oTs[:, bass.ds(h, 1), :], bank[7][:, 0:P]
                                            .rearrange("p (o c) -> p o c", o=1), 1.0, None, ALU.mult) \
                        .then_inc(os_out, 1)
                    combine(S, 0)
                    if not S.last:
                        copy_kv(S, 1, 1 - par, h + 1)
                        copy_kv(S, 2, 1 - par, h + 1)
                    prompt_max(S, 1)
                    if not S.first:
                        tail_b(chain, h - 1, 1 - par)
                    combine(S, 1)
                    if not S.first:
                        tail_c(dve, chain, h - 1, 1 - par)
                        norm_attention(dve, chain, h - 1)
                    prompt_max(S, 2)
                    conv(S)
                    combine(S, 2)
                    if not S.last:
                        copy_kv(S, 3, 1 - par, h + 1)
                    prompt_max(S, 3)
                    nc.vector.tensor_scalar(stc[:, bass.ds(h, 1), 0:3], xpad[:, SEQ:SEQ + 3]
                                            .rearrange("p (o c) -> p o c", o=1), 1.0, None, ALU.mult)
                    nc.vector.tensor_scalar(stc[:, bass.ds(h, 1), 3:27].rearrange("p o (b w) -> p (o b) w", w=3),
                                            spad[:, :, DS:DS + 3], 1.0, None, ALU.mult)
                    if not S.last:
                        copy_kv(S, 4, 1 - par, h + 1)
                    combine(S, 3)
                    S.out(dve, "gr1")
                    chain(nc.vector.tensor_tensor(gw[:, :], gr[par][:, :], gr[par][:, :], ALU.mult))
                    chain(nc.vector.tensor_scalar(gw[:, :], gw[:, :], 0.044715, 1.0, ALU.mult, ALU.add))
                    nc.vector.tensor_tensor(gw[:, :], gw[:, :], gr[par][:, :], ALU.mult).then_inc(gcube, 1)
                    S.out(dve, "ri1")
                    nc.vector.scalar_tensor_tensor(thi[:, :], thi[:, :], 1.0, xc[:, :], ALU.add, ALU.mult)
                    dve.wait_ge(op_done, h + 1)
                    nc.vector.tensor_tensor(oraw[:, :, :], bank[7][:, :].rearrange("p (t c) -> p t c", c=DV),
                                            stat[:, 1:5, 6:7].to_broadcast([P, NQ, DV]), ALU.mult).then_inc(op_out, 1)
                    dve.wait_ge(op_out, h + 1)
                    chain(nc.vector.tensor_tensor(osq, oraw[:, :, :], oraw[:, :, :], ALU.mult))
                    nc.vector.tensor_reduce(oms[:, 0:NQ], osq, AX.X, ALU.add).then_inc(ms_ready, 1)
                    want = BODY_STEPS + (0 if S.first else TAIL_STEPS)
                    assert chain.n == want, (chain.n, want)

                dve.wait_ge(init2, 2)
                for t in range(TT):
                    copy_kv(AHEAD_STEP, t, 0, 0)
                body(FIRST)
                with dve.Fori(0, H // 2 - 1) as i:
                    body(Step(i, 1))
                    body(Step(i, 2))
                body(FINAL)
        st2.close()
        early.close()
        build_rest(nc, A, O, locals())
        mid.close()


def build_rest(nc, A, O, v):
    top, mid, bank, cst, ident, ones = (v[n] for n in ("top", "mid", "bank", "cst", "ident", "ones"))
    sb, sem, eps_t, pcol, subln = (v[n] for n in ("sb", "sem", "eps_t", "pcol", "subln"))
    tail, tail_a, tail_b, tail_c, norm_attention, rnn_done, dve2, steps2 = (
        v[n] for n in ("tail", "tail_a", "tail_b", "tail_c", "norm_attention", "rnn_done", "dve2", "STEPS2"))
    xh, xl, yT, on, oTs, stc = (v[n] for n in ("xh", "xl", "yT", "on", "oTs", "stc"))
    xn2_d, y_d, xp, xs = (v[n] for n in ("xn2_d", "y_d", "xp", "xs"))

    def sbr(name, shape, ctx, dt=F32):
        return ctx.enter_context(nc.sbuf_tensor(name, shape, dt, side="right"))

    late = ExitStack()
    mT = sbr("mT", [P, KT, TOK], late)
    st3 = ExitStack()
    bh = sb("bh", [P, KT, TOK], F32R, ctx=st3)
    bl = sb("bl", [P, KT, TOK], F32R, ctx=st3)
    wraw = [sb(f"wraw{i}", [P, KT, P], ctx=st3) for i in range(2)]
    w3h = [sb(f"w3h{i}", [P, KT, P], F32R, ctx=st3) for i in range(2)]
    w3l = [sb(f"w3l{i}", [P, KT, P], F32R, ctx=st3) for i in range(2)]
    gcol = sb("gcol", [P, 1], ctx=st3)
    tg = sb("tg", [P, TOK], ctx=st3)
    m2 = sb("m2", [P, TOK], ctx=st3)
    srow2 = sb("srow2", [36, D], ctx=st3)
    zcol3 = sb("zcol3", [P, 1], ctx=st3)
    zero = sb("zero", [P, D], ctx=st3)
    zero_set, y_zeroed = sem("zero_set"), sem("y_zeroed")
    wraw_in = [sem(f"wraw_in{i}") for i in range(2)]
    gcol_in, w3_highs, w3_split, zcol3_set = sem("gcol_in"), sem("w3_highs"), sem("w3_split"), sem("zcol3_set")
    x2_in, wo_in = [sem(f"x2_in{t}") for t in range(TT)], sem("wo_in")
    at_done, at_high, at_low, osq_ready = sem("at_done"), sem("at_high"), sem("at_low"), sem("osq_ready")
    oms_done, stc_turned, oroot, os_norm = sem("oms_done"), sem("stc_turned"), sem("oroot"), sem("os_norm")
    os_high, y_high, y_low = sem("os_high"), sem("y_high"), sem("y_low")
    st_out, st_stored = sem("st_out"), sem("st_stored")
    mg_done, mg_act, mg_dve, merged = sem("mg_done"), sem("mg_act"), sem("mg_dve"), sem("merged")
    dve3 = sem("dve3")
    w_out = A["w_out"][0].rearrange("(k p) n -> p k n", p=P)
    w_cols = A["w_in"][0].rearrange("(k p) n -> p k n", p=P)
    gate0 = 5 * D
    GATE, BRANCH = range(2)
    roots3 = (tg, m2)

    with nc.Block() as block:
        @block.sync
        def _(sp_):
            def load_w(br, n, j):
                s = n + br * KT
                if not (isinstance(s, int) and s == 0):
                    sp_.wait_ge(wraw_in[j], 16)
                    sp_.wait_ge(w3_split, s * 2 + (j - 1))
                src = w_cols[:, :, gate0 + br * D:gate0 + (br + 1) * D] if j == GATE else \
                    A[("w_attn_proj", "w_rnn_proj")[br]][0].rearrange("(k p) n -> p k n", p=P)
                sp_.dma_start(wraw[j][:, :, :], src[:, :, bass.ds(n * P, P)]).then_inc(wraw_in[j], 16)

            def load_step(br, n):
                load_w(br, n, GATE)
                load_w(br, n, BRANCH)
                s = n + br * KT
                if not (isinstance(s, int) and s == 0):
                    sp_.wait_ge(mg_act, s * 2 + CREDIT)
                sp_.dma_start(gcol[:, :], pcol[:, bass.ds(n, 1), R_GA + br:R_GA + br + 1]
                              .rearrange("p o c -> p (o c)")).then_inc(gcol_in, 16)

            load_step(0, 0)
            load_step(0, 1)
            sp_.wait_ge(at_done, H)
            sp_.dma_start(on[:, :, :, :].rearrange("p k t c -> p k (t c)"), w_out[:, :, 0:D // 2]).then_inc(wo_in, 16)
            with sp_.Fori(2, KT) as n:
                load_step(0, n)
            with sp_.Fori(0, KT) as n:
                load_step(1, n)
            sp_.wait_ge(st_out, 2)
            for dst, r0, r1 in ((O["new_conv_prompt"][0, 0], 0, 3),
                                (O["new_conv_sample"][0].rearrange("b w d -> (b w) d"), 3, 27),
                                (O["new_rnn_prompt"][0], 27, 28), (O["new_rnn_sample"][0], 28, 36)):
                sp_.dma_start(dst, srow2[r0:r1, :]).then_inc(st_stored, 16)
            sp_.wait_ge(st_stored, 64)

        @block.gpsimd
        def _(pool):
            for s in (mg_act, mg_dve, merged):
                pool.sem_inc(s, CREDIT)
            nc.gpsimd.memset(zcol3[:, :], 0.0).then_inc(zcol3_set, 1)
            pool.wait_ge(zcol3_set, 1)

            def split_w(s, j):
                if not (isinstance(s, int) and s == 0):
                    pool.wait_ge(mg_done, s * 4 + (2 * j - 2))
                pool.wait_ge(wraw_in[j], s * 16 + 16)
                nc.gpsimd.tensor_tensor(w3h[j][:, :, :], wraw[j][:, :, :],
                                        zcol3[:, 0:1].rearrange("p (a b) -> p a b", a=1).to_broadcast([P, KT, P]),
                                        ALU.add).then_inc(w3_highs, 1)
                pool.wait_ge(w3_highs, s * 2 + (j + 1))
                nc.gpsimd.tensor_tensor(w3l[j][:, :, :], wraw[j][:, :, :], w3h[j][:, :, :].bitcast(F32),
                                        ALU.subtract).then_inc(w3_split, 1)

            split_w(0, GATE)
            split_w(0, BRANCH)
            nc.gpsimd.memset(zero[:, :], 0.0).then_inc(zero_set, 1)
            with pool.Fori(1, 2 * KT) as s:
                split_w(s, GATE)
                split_w(s, BRANCH)

        @block.tensor
        def _(pe):
            for g in range(2):
                pe.wait_ge(osq_ready, g + 1)
                nc.tensor.matmul(bank[g][:, :], ones, roots3[g][:, 0:512], start=True, stop=True) \
                    .then_inc(oms_done, 1)
            for h in range(H):
                if h >= 4:
                    pe.wait_ge(at_low, h - 3)
                if h == H - 1:
                    pe.wait_ge(rnn_done, H)
                for t in range(NQ):
                    mm = nc.tensor.transpose(bank[4 + h % 4][:, t * P:(t + 1) * P], on[:, h, t, :], ident)
                mm.then_inc(at_done, 1)
            pe.wait_ge(oroot, 2)

            def step(br, n):
                s = n + br * KT
                for j in (GATE, BRANCH):
                    pe.wait_ge(w3_split, s * 2 + (j + 1))
                    pe.wait_ge((mg_act, mg_dve)[j], s * 2 + CREDIT)
                    if j == BRANCH and br == 0:
                        pe.wait_ge(at_low, H)
                        pe.wait_ge(os_norm, 4)
                    elif j == BRANCH:
                        pe.wait_ge(y_low, KT)
                    mh, ml = (xh, xl) if j == GATE else (bh, bl)
                    for half in range(2):
                        out, c = bank[2 * j + half][:, 0:HALF], slice(half * HALF, (half + 1) * HALF)
                        for k in range(KT):
                            nc.tensor.matmul(out, w3h[j][:, k, :], mh[:, k, c], start=(k == 0), stop=False)
                            nc.tensor.matmul(out, w3h[j][:, k, :], ml[:, k, c], start=False, stop=False)
                            mm = nc.tensor.matmul(out, w3l[j][:, k, :], mh[:, k, c], start=False, stop=(k == KT - 1))
                        mm.then_inc(mg_done, 1)

            with pe.Fori(0, KT) as n:
                step(0, n)
            pe.wait_ge(dve2, steps2)
            for g in range(2):
                for k in range(4):
                    mm = nc.tensor.transpose(bank[4 + g][0:36, k * P:(k + 1) * P], stc[:, 4 * g + k, :], ident)
                mm.then_inc(stc_turned, 1)
            with pe.Fori(0, KT) as n:
                step(1, n)

        @block.scalar
        def _(act):
            for g in range(2):
                act.wait_ge(oms_done, g + 1)
                nc.scalar.activation(roots3[g][:, 0:512], bank[g][:, :], ACT.Sqrt, scale=1.0 / DV,
                                     bias=eps_t[:, 0:1]).then_inc(oroot, 1)
            for h in range(H):
                act.wait_ge(at_done, h + 1)
                nc.scalar.activation(bh[:, h, 0:SEQ], bank[4 + h % 4][:, :], ACT.Copy,
                                     scale=subln[:, 0:1]).then_inc(at_high, 1)
            for g in range(2):
                act.wait_ge(os_norm, g + 1)
                nc.scalar.activation(bh[:, 4 * g:4 * g + 4, SEQ:TOK], oTs[:, 4 * g:4 * g + 4, :], ACT.Copy) \
                    .then_inc(os_high, 1)

            def step(br, n):
                s = n + br * KT
                act.wait_ge(gcol_in, s * 16 + 16)
                act.wait_ge(mg_dve, s * 2 + CREDIT)
                for half in range(2):
                    act.wait_ge(mg_done, s * 4 + (half + 1))
                    nc.scalar.activation(tg[:, half * HALF:(half + 1) * HALF], bank[half][:, 0:HALF], ACT.Tanh,
                                         bias=gcol[:, 0:1], scale=0.5).then_inc(mg_act, 1)

            with act.Fori(0, KT) as n:
                step(0, n)
            act.wait_ge(dve2, steps2)
            act.wait_ge(mg_done, 4 * KT)
            for k in range(KT):
                nc.scalar.activation(bh[:, k, :], yT[:, k, :], ACT.Copy).then_inc(y_high, 1)
            act.wait_ge(zero_set, 1)
            for b in range(NE + 1, NBLK + 1):
                act.dma_start(y_d[b * P:(b + 1) * P, :], zero[:, :]).then_inc(y_zeroed, 16)
            with act.Fori(0, KT) as n:
                step(1, n)
            act.wait_ge(y_zeroed, 16 * OVMAX)

        @block.vector
        def _(dve):
            chain = Chain(dve, dve3)
            for g in range(2):
                nc.vector.tensor_tensor(roots3[g][:, 0:512].rearrange("p (k q) -> p k q", q=P),
                                        oTs[:, 4 * g:4 * g + 4, :], oTs[:, 4 * g:4 * g + 4, :], ALU.mult) \
                    .then_inc(osq_ready, 1)
            tail_chain = Chain(dve, dve2, steps2 - 10)
            norm_attention(dve, tail_chain, H - 1)

            def attn_low(h):
                dve.wait_ge(at_high, h + 1)
                nc.vector.scalar_tensor_tensor(bl[:, h, 0:SEQ], bank[4 + h % 4][:, :], subln[:, 0:1],
                                               bh[:, h, 0:SEQ].bitcast(F32), ALU.mult, ALU.subtract).then_inc(at_low, 1)

            for h in range(4):
                attn_low(h)
            for g in range(2):
                dve.wait_ge(oroot, g + 1)
                chain(nc.vector.reciprocal(roots3[g][:, 0:512], roots3[g][:, 0:512]))
                nc.vector.scalar_tensor_tensor(oTs[:, 4 * g:4 * g + 4, :], oTs[:, 4 * g:4 * g + 4, :], subln[:, 0:1],
                                               roots3[g][:, 0:512].rearrange("p (k q) -> p k q", q=P),
                                               ALU.mult, ALU.mult).then_inc(os_norm, 1)
                attn_low(4 + 2 * g)
                attn_low(5 + 2 * g)
            for g in range(2):
                dve.wait_ge(os_high, g + 1)
                nc.vector.tensor_tensor(bl[:, 4 * g:4 * g + 4, SEQ:TOK], oTs[:, 4 * g:4 * g + 4, :],
                                        bh[:, 4 * g:4 * g + 4, SEQ:TOK].bitcast(F32), ALU.subtract).then_inc(os_norm, 1)

            def step(br, n):
                s = n + br * KT
                if br:
                    dve.wait_ge(merged, n + CREDIT)
                for half in range(2):
                    c = slice(half * HALF, (half + 1) * HALF)
                    dve.wait_ge(mg_done, s * 4 + (half + 3))
                    dve.wait_ge(mg_act, s * 2 + (half + 1 + CREDIT))
                    dst = m2[:, c].rearrange("p (o c) -> p o c", o=1) if br else mT[:, bass.ds(n, 1), c]
                    nc.vector.scalar_tensor_tensor(dst, tg[:, c].rearrange("p (o c) -> p o c", o=1), 1.0,
                                                   bank[2 + half][:, 0:HALF].rearrange("p (o c) -> p o c", o=1),
                                                   ALU.add, ALU.mult).then_inc(mg_dve, 1)
                if br:
                    dve.wait_ge(mg_dve, s * 2 + (2 + CREDIT))
                    nc.vector.tensor_tensor(mT[:, bass.ds(n, 1), :], m2[:, :].rearrange("p (o c) -> p o c", o=1),
                                            mT[:, bass.ds(n, 1), :], ALU.add).then_inc(merged, 1)

            tail_a(dve, tail_chain, H - 1)
            tail_b(tail_chain, H - 1, 1)
            tail_c(dve, tail_chain, H - 1, 1)
            assert tail_chain.base + tail_chain.n == steps2
            with dve.Fori(0, KT) as n:
                step(0, n)
            for k in range(KT):
                dve.wait_ge(y_high, k + 1)
                nc.vector.tensor_tensor(bl[:, k, :], yT[:, k, :], bh[:, k, :].bitcast(F32), ALU.subtract) \
                    .then_inc(y_low, 1)
            for g in range(2):
                dve.wait_ge(stc_turned, g + 1)
                nc.vector.tensor_copy(srow2[:, g * 512:(g + 1) * 512], bank[4 + g][0:36, :]).then_inc(st_out, 1)
            dve.wait_ge(mg_dve, 2 * KT + CREDIT)
            with dve.Fori(0, KT) as n:
                step(1, n)
    st3.close()
    tail.close()
    mid.close()

    x2 = sb("x2", [P, TT, D])
    w13 = [sb(f"w13_{i}", [P, 2, KT, FE]) for i in range(2)]
    w2b = [sb(f"w2_{i}", [P, FE // P, D]) for i in range(2)]
    wgt = sb("wgt", [P, 2, TT])
    slot = sb("slot", [P, 2, TT], I32)
    ovc = sb("ovc", [1, NE], I32)
    ovp = sb("ovp", [1, NE + 1], I32)
    idxt = sb("idxt", [P, NROWS])
    w13_in = [[sem(f"w13_in{half}{i}") for i in range(2)] for half in range(2)]
    w2_in = [sem(f"w2_in{i}") for i in range(2)]

    OUT_UNITS = [(0, 0), (1, 0), (0, 1), (1, 1)] + [(t, half) for t in range(2, TT) for half in range(2)]
    w1s = A["w1"][0].rearrange("e (k p) f -> e p k f", p=P)
    w3s = A["w3"][0].rearrange("e (k p) f -> e p k f", p=P)
    w2s = A["w2"][0].rearrange("e (k p) n -> e p k n", p=P)

    def load13(eng, e, par, half):
        k = slice(half * KT // 2, (half + 1) * KT // 2)
        for j, src in enumerate((w1s, w3s)):
            eng.dma_start(w13[par][:, j, k, :], src[bass.ds(e, 1), :, k, :].rearrange("o p k f -> p (o k) f")) \
                .then_inc(w13_in[half][par], 16)

    def load2(eng, e, par, s):
        eng.dma_start(w2b[par][:, :, :], w2s[bass.ds(e, 1)].rearrange("o p k n -> p (o k) n")).then_inc(s, 16)

    wo = (on[:, :, :, :].rearrange("p k t c -> p k (t c)"),
          sbr("wo1", [P, KT, D // 2], late)[:, :, :])
    st4 = ExitStack()
    g2 = sb("g2", [P, D], ctx=st4)
    xn2 = [sb(f"xn2_{i}", [P, D], ctx=st4) for i in range(2)]
    xn2T = sb("xn2T", [P, KT, P], ctx=st4)
    sq4 = sb("sq4", [P, 512], ctx=st4)
    wr = sb("wr", [P, KT, NG + NE], ctx=st4)
    rb = sb("rb", [P, NG + NE], ctx=st4)
    lg = sb("lg", [P, TT, NG + NE], ctx=st4)
    ss4 = sb("ss4", [P, 4, TT], ctx=st4)
    sm = sb("sm", [P, TT, 64], ctx=st4)
    oh = sb("oh", [P, 3, TT, NE], ctx=st4)
    rk = sb("rk", [P, 2, TT, NE], ctx=st4)
    ex = sb("ex", [P, 8, NE], ctx=st4)
    ex2 = sb("ex2", [P, TT, NE], ctx=st4)
    ohp = sb("ohp", [P, TT + 1, NE], ctx=st4)
    pr = sb("pr", [P, 6, 2, TT], ctx=st4)
    at_place = sb("at_place", [P, 2 * TT, P], ctx=st4)
    at_block = sb("at_block", [P, 2 * TT, NROWS], ctx=st4)
    r_in, mo_done, x2_ready = sem("r_in"), sem("mo_done"), sem("x2_ready")
    ss_ready, root4, xn2_ready = sem("ss_ready"), sem("root4"), sem("xn2_ready")
    xn2_stored = [sem(f"xn2_stored{i}") for i in range(2)]
    x2t_done, x2t_out, rt_done = sem("x2t_done"), sem("x2t_out"), sem("rt_done")
    gl_ready, ge_ready, ranks_done, oh_ready = sem("gl_ready"), sem("ge_ready"), sem("ranks_done"), sem("oh_ready")
    hot_ready, inv_done, dve4, act4 = sem("hot_ready"), sem("inv_done"), sem("dve4"), sem("act4")

    with nc.Block() as block:
        @block.sync
        def _(sp_):
            for t in range(TT):
                if t == 2:
                    sp_.dma_start(wo[1], w_out[:, :, D // 2:]).then_inc(wo_in, 16)
                sp_.dma_start(x2[:, t, :], xp[:, t, :] if t < NQ else xs).then_inc(x2_in[t], 16)
            sp_.dma_start(g2[:, :], A["norm2_g"].to_broadcast([P, D])).then_inc(r_in, 16)
            sp_.dma_start(wr[:, :, 0:NG], A["w_group"][0].rearrange("(k p) n -> p k n", p=P)).then_inc(r_in, 16)
            sp_.dma_start(wr[:, :, NG:], A["w_router"][0].rearrange("(k p) n -> p k n", p=P)).then_inc(r_in, 16)
            sp_.dma_start(rb[:, 0:NG], A["b_group"].to_broadcast([P, NG])).then_inc(r_in, 16)
            sp_.dma_start(rb[:, NG:], A["b_router"].to_broadcast([P, NE])).then_inc(r_in, 16)
            for e in range(2):
                load13(sp_, e, e, 0)
                load13(sp_, e, e, 1)
                load2(sp_, e, e, w2_in[e])
            for t in range(TT):
                sp_.wait_ge(xn2_ready, t + 1)
                sp_.dma_start(xn2_d[t * P:(t + 1) * P, :], xn2[t % 2][:, :]).then_inc(xn2_stored[t % 2], 16)
            sp_.wait_ge(xn2_stored[0], 48)
            sp_.wait_ge(xn2_stored[1], 32)

        @block.tensor
        def _(pe):

            def route(t):
                pe.wait_ge(r_in, 80)
                pe.wait_ge(xn2_ready, t + 1)
                if t >= 1:
                    pe.wait_ge(x2t_out, 2 * t)
                for half in range(2):
                    for k in range(4):
                        c = (4 * half + k) * P
                        mm = nc.tensor.transpose(bank[4 + half][:, k * P:(k + 1) * P], xn2[t % 2][:, c:c + P], ident)
                    mm.then_inc(x2t_done, 1)
                pe.wait_ge(x2t_out, 2 * t + 2)
                for k in range(KT):
                    mm = nc.tensor.matmul(bank[6][:, t * 32:t * 32 + NG + NE], xn2T[:, k, :], wr[:, k, :],
                                          start=(k == 0), stop=(k == KT - 1))
                mm.then_inc(rt_done, 1)

            for u, (t, half) in enumerate(OUT_UNITS):
                if u < 4 and half != OUT_UNITS[u - 1][1]:
                    pe.wait_ge(wo_in, 16 * (half + 1))
                if u >= 4:
                    pe.wait_ge(x2_ready, u - 3)
                for k in range(KT):
                    mm = nc.tensor.matmul(bank[u % 4][:, :], mT[:, k, t * P:(t + 1) * P], wo[half][:, k, :],
                                          start=(k == 0), stop=(k == KT - 1))
                mm.then_inc(mo_done, 1)
                if half == 0:
                    continue
                if t >= 1:
                    route(t - 1)
            route(TT - 1)
            pe.wait_ge(oh_ready, TT)
            nc.tensor.matmul(bank[7][:, 0:TT * NE], cst[:, K_TRI:K_TRI + P],
                             oh[:, 2, :, :].rearrange("p t e -> p (t e)"), start=True, stop=False)
            nc.tensor.matmul(bank[7][:, 0:TT * NE], ones, ohp[:, 0:TT, :].rearrange("p t e -> p (t e)"),
                             start=False, stop=True)
            nc.tensor.matmul(bank[7][:, TT * NE:(TT + 1) * NE], ones, ohp[:, TT, :], start=True, stop=True) \
                .then_inc(ranks_done, 1)
            for n in range(2 * TT):
                pe.wait_ge(hot_ready, n + 1)
                mm = nc.tensor.matmul(bank[5][:, 0:NROWS], at_place[:, n, :], at_block[:, n, :],
                                      start=(n == 0), stop=(n == 2 * TT - 1))
            mm.then_inc(inv_done, 1)

        @block.scalar
        def _(act):
            for t in range(TT):
                act.wait_ge(x2_ready, OUT_UNITS.index((t, 1)) + 1)
                if t >= 1:
                    act.wait_ge(act4, t)
                for half in range(2):
                    ins = nc.scalar.activation(sq4[:, :], x2[:, t, half * 512:(half + 1) * 512], ACT.Square,
                                               accum_out=ss4[:, half, t:t + 1])
                    ins.then_inc(act4, 1) if half else ins.then_inc(ss_ready, 1)
                    if half == 0:
                        act.wait_ge(ss_ready, 2 * t + 1)
                act.wait_ge(act4, t + 1)
                nc.scalar.activation(ss4[:, 2, t:t + 1], ss4[:, 0, t:t + 1], ACT.Identity,
                                     bias=ss4[:, 1, t:t + 1]).then_inc(ss_ready, 1)
                act.wait_ge(ss_ready, 2 * t + 2)
                nc.scalar.activation(ss4[:, 3, t:t + 1], ss4[:, 2, t:t + 1], ACT.Sqrt, scale=1.0 / D,
                                     bias=eps_t[:, 0:1]).then_inc(root4, 1)
                act.wait_ge(x2t_done, 2 * t + 1)
                if t >= 1:
                    act.wait_ge(rt_done, t)
                nc.scalar.activation(xn2T[:, 0:4, :].rearrange("p k q -> p (k q)"), bank[4][:, :], ACT.Copy) \
                    .then_inc(x2t_out, 1)
                act.wait_ge(x2t_done, 2 * t + 2)
                nc.scalar.activation(xn2T[:, 4:8, :].rearrange("p k q -> p (k q)"), bank[5][:, :], ACT.Copy) \
                    .then_inc(x2t_out, 1)
            act.wait_ge(gl_ready, 1)
            nc.scalar.activation(sm[:, :, 8:13], sm[:, :, 0:5], ACT.Exp).then_inc(ge_ready, 1)

        @block.vector
        def _(dve):
            chain = Chain(dve, dve4)
            for u, (t, half) in enumerate(OUT_UNITS):
                s = slice(half * 512, (half + 1) * 512)
                dve.wait_ge(x2_in[t], 16)
                dve.wait_ge(mo_done, u + 1)
                nc.vector.scalar_tensor_tensor(x2[:, t, s], bank[u % 4][:, :], 0.5, x2[:, t, s],
                                               ALU.mult, ALU.add).then_inc(x2_ready, 1)
                if half == 0:
                    continue
                dve.wait_ge(r_in, 80)
                dve.wait_ge(root4, t + 1)
                chain(nc.vector.reciprocal(ss4[:, 2, t:t + 1], ss4[:, 3, t:t + 1]))
                if t >= 2:
                    dve.wait_ge(xn2_stored[t % 2], 16 * (t // 2))
                nc.vector.scalar_tensor_tensor(xn2[t % 2][:, :], x2[:, t, :], ss4[:, 2, t:t + 1], g2[:, :],
                                               ALU.mult, ALU.mult).then_inc(xn2_ready, 1)
            dve.wait_ge(rt_done, TT)
            chain(nc.vector.tensor_tensor(
                lg[:, :, :], bank[6][:, 0:TT * 32].rearrange("p (t c) -> p t c", c=32)[:, :, 0:NG + NE],
                rb[:, :].rearrange("p (o c) -> p o c", o=1).to_broadcast([P, TT, NG + NE]), ALU.add))

            def col(i, n=1):
                return sm[:, :, i:i + n]

            def tt(out, a, b, op):
                chain(nc.vector.tensor_tensor(out, a, b, op))

            def ts(out, a, s1, s2, op0, op1=None):
                if op1 is None:
                    chain(nc.vector.tensor_scalar(out, a, s1, None, op0))
                else:
                    chain(nc.vector.tensor_scalar(out, a, s1, s2, op0, op1))

            def first_max(src, top_, hot, best):
                chain(nc.vector.tensor_reduce(top_, src, AX.X, ALU.max))
                tt(hot, src, top_.to_broadcast([P, TT, 4]), ALU.is_equal)
                tt(hot, hot, cst[:, K_DOWN:K_DOWN + 4].rearrange("p (o c) -> p o c", o=1).to_broadcast([P, TT, 4]),
                   ALU.mult)
                chain(nc.vector.tensor_reduce(best, hot, AX.X, ALU.max))
                tt(hot, hot, best.to_broadcast([P, TT, 4]), ALU.is_equal)

            gmax, ghot, ein, e1, f1, em, e2, f2 = col(16), col(20, 4), col(24, 4), col(28), col(32, 4), col(36, 4), \
                col(40), col(44, 4)
            first_max(lg[:, :, 0:NG], gmax, ghot, col(17))
            tt(col(0, 4), lg[:, :, 0:NG], gmax.to_broadcast([P, TT, 4]), ALU.subtract)
            tt(ein, lg[:, :, NG:NG + EG], ghot[:, :, 0:1].to_broadcast([P, TT, EG]), ALU.mult)
            for g in range(1, NG):
                tt(col(48, 4), lg[:, :, NG + g * EG:NG + (g + 1) * EG],
                   ghot[:, :, g:g + 1].to_broadcast([P, TT, EG]), ALU.mult)
                tt(ein, ein, col(48, 4), ALU.add)
            first_max(ein, e1, f1, col(18))
            ts(col(48, 4), f1, -1.0, 1.0, ALU.mult, ALU.add)
            tt(em, ein, col(48, 4), ALU.mult)
            ts(col(52, 4), f1, -BIG, None, ALU.mult)
            tt(em, em, col(52, 4), ALU.add)
            first_max(em, e2, f2, col(19))
            nc.vector.tensor_tensor(col(4), e2, e1, ALU.subtract).then_inc(gl_ready, 1)
            for k, f in enumerate((f1, f2)):
                for g in range(NG):
                    ins = nc.vector.tensor_tensor(oh[:, k, :, g * EG:(g + 1) * EG], f,
                                                  ghot[:, :, g:g + 1].to_broadcast([P, TT, EG]), ALU.mult)
            chain(ins)
            chain(nc.vector.tensor_tensor(oh[:, 2, :, :], oh[:, 0, :, :], oh[:, 1, :, :], ALU.add))
            chain(nc.vector.memset(ohp[:, 0, :], 0.0))
            for t in range(TT):
                ins = nc.vector.tensor_tensor(ohp[:, t + 1, :], ohp[:, t, :], oh[:, 2, t, :], ALU.add)
                ins.then_inc(oh_ready, 1)
                dve.wait_ge(oh_ready, t + 1)
            dve.wait_ge(ge_ready, 1)
            chain(nc.vector.tensor_reduce(col(56), col(8, 4), AX.X, ALU.add))
            ts(col(57), col(12), 1.0, None, ALU.add)
            tt(col(56), col(56), col(57), ALU.mult)
            chain(nc.vector.reciprocal(col(58), col(56)))
            ts(wgt[:, 0, :], sm[:, :, 58], 1.0, None, ALU.mult)
            tt(wgt[:, 1, :], sm[:, :, 58], sm[:, :, 12], ALU.mult)
            dve.wait_ge(ranks_done, 1)
            cnt, ov, pre, tmp = (ex[:, i, :] for i in range(4))
            chain(nc.vector.tensor_copy(cnt, bank[7][:, TT * NE:(TT + 1) * NE]))
            ts(ov, cnt, float(P), None, ALU.is_gt)
            for j in range(2, TT):
                chain(nc.vector.scalar_tensor_tensor(ov, cnt, float(j * P), ov, ALU.is_gt, ALU.add))
            a, b = ex[:, 4, :], ex[:, 5, :]
            chain(nc.vector.tensor_copy(a, ov))
            for d in (1, 2, 4, 8):
                chain(nc.vector.tensor_copy(b[:, 0:d], a[:, 0:d]))
                tt(b[:, d:], a[:, d:], a[:, 0:NE - d], ALU.add)
                a, b = b, a
            tt(pre, a, ov, ALU.subtract)
            incl = a
            zz = rk[:, :, :, :]

            def of_pairs(out, x):
                tt(zz, oh[:, 0:2, :, :], x, ALU.mult)
                chain(nc.vector.tensor_reduce(out, zz, AX.X, ALU.add))

            rank, row, q, place, slotf = (pr[:, n, :, :] for n in range(5))
            chain(nc.vector.scalar_tensor_tensor(tmp, pre, 1.0, cst[:, K_RAMP:K_RAMP + NE], ALU.add, ALU.add))
            r = ex2[:, :, :]
            chain(nc.vector.tensor_copy(r, bank[7][:, 0:TT * NE].rearrange("p (t e) -> p t e", e=NE)))
            of_pairs(rank, r.rearrange("p (o t) e -> p o t e", o=1).to_broadcast([P, 2, TT, NE]))
            of_pairs(row, tmp.rearrange("p (o i e) -> p o i e", o=1, i=1).to_broadcast([P, 2, TT, NE]))
            ts(q, rank, float(P), None, ALU.is_ge)
            for j in range(2, TT):
                chain(nc.vector.scalar_tensor_tensor(q, rank, float(j * P), q, ALU.is_ge, ALU.add))
            chain(nc.vector.scalar_tensor_tensor(place, q, -float(P), rank, ALU.mult, ALU.add))
            tt(row, row, q, ALU.add)
            for n in range(2 * TT):
                k, t = n // TT, n % TT
                nc.vector.tensor_scalar(at_place[:, n, :], cst[:, K_RAMP:K_RAMP + P], pr[:, 3, k, t:t + 1], None,
                                        ALU.is_equal)
                nc.vector.tensor_scalar(at_block[:, n, :], cst[:, K_RAMP:K_RAMP + NROWS], pr[:, 1, k, t:t + 1],
                                        cst[:, K_TOK + t:K_TOK + t + 1], ALU.is_equal, ALU.mult).then_inc(hot_ready, 1)
            chain(nc.vector.scalar_tensor_tensor(slotf, row, float(P), place, ALU.mult, ALU.add))
            nc.vector.tensor_copy(slot[:, :, :], slotf)
            nc.vector.tensor_copy(ovc[:, :], ov[0:1])
            nc.vector.tensor_copy(ovp[:, 0:NE], pre[0:1])
            nc.vector.tensor_copy(ovp[:, NE:], incl[0:1, NE - 1:NE])
            dve.wait_ge(inv_done, 1)
            nc.vector.tensor_copy(idxt[:, :], bank[5][:, 0:NROWS])
    st4.close()
    late.close()

    gf = sb("gf", [P, D])
    st5 = ExitStack()
    UPC, DNC = KT, FE // P
    NCH = UPC + DNC
    RING5 = 4
    assert UPC % RING5 == 0 and NCH % RING5 == 0
    PER_DVE, PER_POOL = NCH // RING5 * (RING5 - 1), NCH // RING5
    UP_DVE, UP_POOL = UPC // RING5 * (RING5 - 1), UPC // RING5

    idx = sb("idx", [P, 1], I32, ctx=st5)
    xg = sb("xg", [P, D], ctx=st5)
    xeh = sb("xeh", [P, KT, P], F32R, ctx=st5)
    xel = sb("xel", [P, KT, P], F32R, ctx=st5)
    th = sb("th", [P, FE], ctx=st5)
    gg = sb("gg", [P, FE], ctx=st5)
    hTh = sb("hTh", [P, FE], F32R, ctx=st5)
    hTl = sb("hTl", [P, FE], F32R, ctx=st5)
    yb = sb("yb", [P, D], ctx=st5)
    ch = sb("ch", [P, RING5, 2, 512], F32R, ctx=st5)
    cl = sb("cl", [P, RING5, 2, 512], F32R, ctx=st5)
    gate = sb("gate", [P, 3], ctx=st5)

    gf_in, idx_in, xg_in, y_stored = sem("gf_in"), sem("idx_in"), sem("xg_in"), sem("y_stored")
    xt_done, xt_high, xt_low = sem("xt_done"), sem("xt_high"), sem("xt_low")
    used, ch_high, ch_low_dve, ch_low_pool = sem("used"), sem("ch_high"), sem("ch_low_dve"), sem("ch_low_pool")
    th_ready, s_ready, gg_ready = sem("th_ready"), sem("s_ready"), sem("gg_ready")
    ht_done, ht_high, ht_low = sem("ht_done"), sem("ht_high"), sem("ht_low")
    y_act, y_dve, held, gate_set = sem("y_act"), sem("y_dve"), sem("held"), sem("gate_set")

    class Turn:
        def __init__(self, b, up, down):
            self.b, self.up, self.down = b, up, down
            if down is None:
                self.n, self.nd, self.np = 0, 0, 0
            elif up is None:
                self.n, self.nd, self.np = b * NCH - NCH, b * PER_DVE - PER_DVE, b * PER_POOL - PER_POOL
            else:
                self.n = b * NCH - DNC
                self.nd, self.np = b * PER_DVE - (PER_DVE - UP_DVE), b * PER_POOL - (PER_POOL - UP_POOL)

        def raw(self, c):
            if c < UPC:
                return w13[self.up[0]][:, :, c, :]
            return w2b[self.down[0]][:, c - UPC, :].rearrange("p (j n) -> p j n", j=2)

        def high(self, eng, c):
            eng.wait_ge(ch_high, self.n + (c + 1))

        def low(self, eng, c):
            if c % RING5 == RING5 - 1:
                eng.wait_ge(ch_low_pool, self.np + (c // RING5 + 1))
            else:
                eng.wait_ge(ch_low_dve, self.nd + (c // RING5 * (RING5 - 1) + c % RING5 + 1))

    def each_block(eng, step, last):
        def count(row, e, top_):
            return eng.value_load(row[0:1, bass.ds(e, 1)], min_val=0, max_val=top_)

        def expert(e, up, down):
            if down is None:
                step(Turn(0, up, None))
            else:
                step(Turn(count(ovp, e, OVMAX) + e, up, down))
            n = count(ovc, e, TT - 1)
            with eng.If(n > 0):
                with eng.Fori(count(ovp, e, OVMAX - 1), count(ovp, e + 1, OVMAX)) as j:
                    step(Turn(j + (e + 1), up, up))

        expert(0, (0, 1), None)
        with eng.Fori(0, NE // 2 - 1) as i:
            expert(i * 2 + 1, (1, i + 1), (0, i + 1))
            expert(i * 2 + 2, (0, i + 2), (1, i + 1))
        expert(NE - 1, (1, NE // 2), (0, NE // 2))
        last(Turn(count(ovp, NE, OVMAX) + NE, None, (1, NE // 2)))

    with nc.Block() as block:
        @block.sync
        def _(sp_):
            with sp_.Fori(0, NE // 2 - 1) as i:
                for par in range(2):
                    e = i * 2 + (2 + par)
                    b = sp_.value_load(ovp[0:1, bass.ds(e - 1, 1)], min_val=0, max_val=OVMAX) + (i * 2 + par)
                    sp_.wait_ge(used, b * NCH + UPC // 2)
                    load13(sp_, e, par, 0)
                    sp_.wait_ge(used, b * NCH + UPC)
                    load13(sp_, e, par, 1)
                    sp_.wait_ge(used, b * NCH + (UPC + NCH))
                    load2(sp_, e, par, w2_in[par])
            sp_.dma_start(gf[:, :], A["final_norm_g"].rearrange("(o d) -> o d", o=1).to_broadcast([P, D])) \
                .then_inc(gf_in, 16)

        @block.gpsimd
        def _(pool):
            for s in (y_stored, held):
                pool.sem_inc(s, CREDIT)
            nc.gpsimd.memset(gate[:, 0:1], 0.0).then_inc(gate_set, 1)
            pool.wait_ge(gate_set, 1)

            def gather(b):
                if not isinstance(b, int) or b > 0:
                    pool.wait_ge(xt_done, b)
                pool.wait_ge(idx_in, b + 1)
                if not isinstance(b, int):
                    hold(b - 3)
                pool.indirect_dma_start(xg[:, :], None, xn2_d, bass.IndirectOffsetOnAxis(ap=idx[:, 0:1], axis=0)) \
                    .then_inc(xg_in, 16)

            def hold(n):
                pool.wait_ge(held, n + CREDIT)
                nc.gpsimd.tensor_tensor(gate[:, 1:2], gate[:, 0:1], gate[:, 0:1], ALU.add).then_inc(held, 1)

            def low(S, c):
                S.high(pool, c)
                nc.gpsimd.tensor_tensor(cl[:, c % RING5, :, :], S.raw(c), ch[:, c % RING5, :, :].bitcast(F32),
                                        ALU.subtract).then_inc(ch_low_pool, 1)

            def step(S):
                for c in range(RING5 - 1, UPC if S.down is None else NCH, RING5):
                    low(S, c)
                gather(S.b + 2)

            def last(S):
                low(S, NCH - 1)
                pool.wait_ge(xg_in, S.b * 16 + 32)
                hold(S.b - 1)

            gather(0)
            gather(1)
            each_block(pool, step, last)

        @block.tensor
        def _(pe):
            def chunk(S, c):
                S.low(pe, c)
                first, end = c in (0, UPC), c in (UPC - 1, NCH - 1)
                k = c if c < UPC else c - UPC
                ah, al = (xeh[:, k, :], xel[:, k, :]) if c < UPC else \
                    (hTh[:, k * P:(k + 1) * P], hTl[:, k * P:(k + 1) * P])
                for j in range(2):
                    out = bank[(2 if c < UPC else 5) + j][:, :]
                    high, low = ch[:, c % RING5, j, :], cl[:, c % RING5, j, :]
                    nc.tensor.matmul(out, ah, high, start=first, stop=False)
                    nc.tensor.matmul(out, ah, low, start=False, stop=False)
                    mm = nc.tensor.matmul(out, al, high, start=False, stop=end)
                mm.then_inc(used, 1)

            def turn_tokens(b):
                pe.wait_ge(xg_in, b * 16 + 16)
                if not isinstance(b, int) or b > 0:
                    pe.wait_ge(xt_high, b)
                    pe.wait_ge(xt_low, b)
                for k in range(KT):
                    mm = nc.tensor.transpose(bank[k // 4][:, k % 4 * P:(k % 4 + 1) * P], xg[:, k * P:(k + 1) * P],
                                             ident)
                mm.then_inc(xt_done, 1)

            def turn_hidden():
                for k in range(DNC):
                    mm = nc.tensor.transpose(bank[4][:, k * P:(k + 1) * P], gg[:, k * P:(k + 1) * P], ident)
                mm.then_inc(ht_done, 1)

            def down(S):
                pe.wait_ge(y_act, S.b)
                pe.wait_ge(y_dve, S.b)
                pe.wait_ge(ht_high, S.b)
                pe.wait_ge(ht_low, S.b)
                for c in range(UPC, NCH):
                    chunk(S, c)

            def step(S):
                if S.down is not None:
                    pe.wait_ge(gg_ready, S.b)
                pe.wait_ge(xt_high, S.b + 1)
                pe.wait_ge(xt_low, S.b + 1)
                for c in range(UPC):
                    if c == UPC // 2 and S.down is not None:
                        turn_hidden()
                    chunk(S, c)
                turn_tokens(S.b + 1)
                if S.down is not None:
                    down(S)

            def last(S):
                pe.wait_ge(gg_ready, S.b)
                turn_hidden()
                down(S)

            for half in range(2):
                nc.tensor.matmul(bank[5 + half][:, :], ident, cst[:, 0:512], start=True, stop=True)
            turn_tokens(0)
            each_block(pe, step, last)

        @block.scalar
        def _(act):
            def high(S, c):
                if c in (0, UPC // 2):
                    act.wait_ge(w13_in[c // (UPC // 2)][S.up[0]], S.up[1] * 32)
                if c == UPC:
                    act.wait_ge(w2_in[S.down[0]], S.down[1] * 16)
                if S.down is not None or c >= RING5:
                    act.wait_ge(used, S.n + (c - RING5 + 1))
                nc.scalar.activation(ch[:, c % RING5, :, :], S.raw(c), ACT.Copy).then_inc(ch_high, 1)

            def turned(b):
                act.wait_ge(xt_done, b + 1)
                for half in range(2):
                    ins = nc.scalar.activation(xeh[:, 4 * half:4 * half + 4, :].rearrange("p k q -> p (k q)"),
                                               bank[half][:, :], ACT.Copy)
                ins.then_inc(xt_high, 1)

            def outputs(S, final=False):
                n = S.b + 1 if final else S.b
                act.wait_ge(y_stored, n * 16 + (CREDIT - 16))
                act.wait_ge(used, S.b * NCH if final else n * NCH - DNC)
                nc.scalar.activation(yb[:, 0:512], bank[5][:, :], ACT.Copy).then_inc(y_act, 1)

            def store(S, final=False):
                n = S.b + 1 if final else S.b
                act.wait_ge(y_act, n)
                act.wait_ge(y_dve, n)
                act.dma_start(y_d[bass.ds((n - 1) * P, P), :], yb[:, :]).then_inc(y_stored, 16)

            def hidden(S):
                act.wait_ge(ht_done, S.b)
                nc.scalar.activation(hTh[:, :], bank[4][:, :], ACT.Copy).then_inc(ht_high, 1)

            def step(S):
                for c in range(UPC):
                    if c == RING5 and S.down is None:
                        turned(0)
                    if c == RING5 - 1 and S.down is not None:
                        outputs(S)
                    high(S, c)
                    if c == RING5 + 1 and S.down is not None:
                        store(S)
                if S.down is not None:
                    hidden(S)
                    for c in range(UPC, NCH):
                        high(S, c)
                turned(S.b + 1)
                if S.down is not None:
                    act.wait_ge(s_ready, S.b)
                nc.scalar.activation(th[:, :], bank[2][:, :], ACT.Tanh, scale=0.5).then_inc(th_ready, 1)

            def last(S):
                outputs(S)
                store(S)
                hidden(S)
                for c in range(UPC, NCH):
                    high(S, c)
                outputs(S, True)
                store(S, True)
                act.wait_ge(y_stored, S.b * 16 + (CREDIT + 16))
                nc.scalar.activation(gate[:, 2:3], eps_t[:, 0:1], ACT.Copy)

            each_block(act, step, last)

        @block.vector
        def _(dve):
            def low(S, c):
                S.high(dve, c)
                nc.vector.tensor_tensor(cl[:, c % RING5, :, :], S.raw(c), ch[:, c % RING5, :, :].bitcast(F32),
                                        ALU.subtract).then_inc(ch_low_dve, 1)

            def indices(b):
                nc.vector.tensor_scalar(idx[:, :], idxt[:, bass.ds(b + 1, 1)], 1.0, None, ALU.mult) \
                    .then_inc(idx_in, 1)

            def turned(b):
                dve.wait_ge(xt_high, b + 1)
                for half in range(2):
                    s = slice(4 * half, 4 * half + 4)
                    ins = nc.vector.tensor_tensor(xel[:, s, :].rearrange("p k q -> p (k q)"), bank[half][:, :],
                                                  xeh[:, s, :].bitcast(F32).rearrange("p k q -> p (k q)"),
                                                  ALU.subtract)
                ins.then_inc(xt_low, 1)
                indices(b + 1)

            def outputs(S, final=False):
                n = S.b + 1 if final else S.b
                dve.wait_ge(y_stored, n * 16 + (CREDIT - 16))
                dve.wait_ge(used, S.b * NCH if final else n * NCH - DNC)
                nc.vector.tensor_copy(yb[:, 512:D], bank[6][:, :]).then_inc(y_dve, 1)

            def hidden(S):
                dve.wait_ge(ht_high, S.b)
                nc.vector.tensor_tensor(hTl[:, :], bank[4][:, :], hTh[:, :].bitcast(F32), ALU.subtract) \
                    .then_inc(ht_low, 1)

            def step(S):
                for c in range(UPC):
                    if c % RING5 < RING5 - 1:
                        low(S, c)
                    elif c < RING5 and S.down is not None:
                        outputs(S)
                    elif c < RING5:
                        turned(0)
                if S.down is not None:
                    hidden(S)
                    for c in range(UPC, NCH):
                        if c % RING5 < RING5 - 1:
                            low(S, c)
                turned(S.b + 1)
                dve.wait_ge(th_ready, S.b + 1)
                nc.vector.scalar_tensor_tensor(gg[:, :], th[:, :], 1.0, bank[2][:, :], ALU.add, ALU.mult) \
                    .then_inc(s_ready, 1)
                dve.wait_ge(s_ready, S.b + 1)
                nc.vector.scalar_tensor_tensor(gg[:, :], gg[:, :], 0.5, bank[3][:, :], ALU.mult, ALU.mult) \
                    .then_inc(gg_ready, 1)

            def last(S):
                outputs(S)
                hidden(S)
                for c in range(UPC, NCH - 1):
                    low(S, c)
                outputs(S, True)

            indices(0)
            each_block(dve, step, last)
    st5.close()

    st6 = ExitStack()
    yg = [sb(f"yg{t}", [P, 2, D], ctx=st6) for t in range(TT)]
    sq6 = sb("sq6", [P, D], ctx=st6)
    yo = [sb(f"yo{i}", [P, D], ctx=st6) for i in range(2)]
    ss6 = sb("ss6", [P, 3, TT], ctx=st6)
    yg_in = [sem(f"yg_in{t}") for t in range(TT)]
    yo_stored = [sem(f"yo_stored{i}") for i in range(2)]
    x3_ready, sq6_ready, root6, yo_ready, dve6 = sem("x3_ready"), sem("sq6_ready"), sem("root6"), sem("yo_ready"), sem("dve6")
    yp = O["y_prompt"].rearrange("b (t p) d -> p (b t) d", p=P)
    ysm = O["y_sample"].rearrange("b s d -> (b s) d")

    with nc.Block() as block:
        @block.gpsimd
        def _(pool):
            for t in range(TT):
                for k in range(2):
                    pool.indirect_dma_start(yg[t][:, k, :], None, y_d,
                                            bass.IndirectOffsetOnAxis(ap=slot[:, k, t:t + 1], axis=0)) \
                        .then_inc(yg_in[t], 16)

        @block.vector
        def _(dve):
            chain = Chain(dve, dve6)
            dve.wait_ge(gf_in, 16)

            def scale_out(t):
                dve.wait_ge(root6, t + 1)
                chain(nc.vector.reciprocal(ss6[:, 2, t:t + 1], ss6[:, 1, t:t + 1]))
                if t >= 2:
                    dve.wait_ge(yo_stored[t % 2], 16 * (t // 2))
                nc.vector.scalar_tensor_tensor(yo[t % 2][:, :], x2[:, t, :], ss6[:, 2, t:t + 1], gf[:, :],
                                               ALU.mult, ALU.mult).then_inc(yo_ready, 1)

            for t in range(TT):
                dve.wait_ge(yg_in[t], 32)
                chain(nc.vector.scalar_tensor_tensor(x2[:, t, :], yg[t][:, 0, :], wgt[:, 0, t:t + 1],
                                                     x2[:, t, :], ALU.mult, ALU.add))
                nc.vector.scalar_tensor_tensor(x2[:, t, :], yg[t][:, 1, :], wgt[:, 1, t:t + 1],
                                               x2[:, t, :], ALU.mult, ALU.add).then_inc(x3_ready, 1)
                if t >= 1:
                    scale_out(t - 1)
            scale_out(TT - 1)

        @block.scalar
        def _(act):
            for t in range(TT):
                act.wait_ge(x3_ready, t + 1)
                nc.scalar.activation(sq6[:, :], x2[:, t, :], ACT.Square, accum_out=ss6[:, 0, t:t + 1]) \
                    .then_inc(sq6_ready, 1)
                act.wait_ge(sq6_ready, t + 1)
                nc.scalar.activation(ss6[:, 1, t:t + 1], ss6[:, 0, t:t + 1], ACT.Sqrt, scale=1.0 / D,
                                     bias=eps_t[:, 0:1]).then_inc(root6, 1)

        @block.sync
        def _(sp_):
            for t in range(TT):
                sp_.wait_ge(yo_ready, t + 1)
                sp_.dma_start(yp[:, t, :] if t < NQ else ysm, yo[t % 2][:, :]).then_inc(yo_stored[t % 2], 16)
            sp_.wait_ge(yo_stored[0], 48)
            sp_.wait_ge(yo_stored[1], 32)
    st6.close()


_INS = ["x_prompt", "x_sample", "cache_k", "cache_v", "state_conv", "state_rnn", "norm1_g", "w_in",
        "lambda_q1", "lambda_k1", "lambda_q2", "lambda_k2", "subln_g", "w_attn_proj", "conv_w", "conv_b",
        "w_rg_a", "b_rg_a", "w_rg_i", "b_rg_i", "rg_lambda", "w_rnn_proj", "b_gate", "w_out", "norm2_g",
        "w_group", "b_group", "w_router", "b_router", "w1", "w3", "w2", "final_norm_g"]
_OUTS = [("y_prompt", (1, SEQ, D)), ("y_sample", (NS, DS, D)),
         ("new_k_prompt", (1, 1, SEQ, H, 2, DH)), ("new_v_prompt", (1, 1, SEQ, H, DV)),
         ("new_conv_prompt", (1, 1, CW - 1, D)), ("new_rnn_prompt", (1, 1, D)),
         ("new_k_sample", (1, NS, DS, H, 2, DH)), ("new_v_sample", (1, NS, DS, H, DV)),
         ("new_conv_sample", (1, NS, CW - 1, D)), ("new_rnn_sample", (1, NS, D))]


def kernel(**inputs):
    import concourse.bacc as bacc
    from concourse.bass_utils import run_bass_kernel_spmd

    nc = bacc.Bacc("TRN2", target_bir_lowering=False, num_devices=1)
    arrays = {name: np.ascontiguousarray(inputs[name]) for name in _INS}
    arrays["shape_constants"] = shape_constants()
    A = {n: nc.dram_tensor(f"in_{n}", a.shape, mybir.dt.from_np(a.dtype), kind="ExternalInput").ap()
         for n, a in arrays.items()}
    O = {n: nc.dram_tensor(f"out_{n}", s, F32, kind="ExternalOutput").ap() for n, s in _OUTS}
    build(nc, A, O)
    r = run_bass_kernel_spmd(nc, [{f"in_{n}": a for n, a in arrays.items()}], core_ids=[0])
    return tuple(r.results[0][f"out_{n}"] for n, _ in _OUTS)
```
